# Optimizing a Trainium2 kernel written in Bass

```python
import jax, jax.numpy as jnp
from jax import lax
import numpy as np

D_MODEL = 1024
BATCH = 1
SEQ = 512
DEPTH = 2
DEC_BATCH = 1
DEC_SEQ = 32
PAST_LEN = 256

CHUNK = 64
Q_BLOCK = 128
N_MEM = 256
MEM_HEADS = 4
MEM_HEAD = D_MODEL // MEM_HEADS
MEM_SCALE = MEM_HEAD ** -0.5
RG_WIDTH = D_MODEL // 4
RG_BLOCKS = 4
RG_BLOCK = RG_WIDTH // RG_BLOCKS
CONV_W = 4
LRU_C = 8.0
RW_HEADS = 4
RW_HEAD = 64
RW_WIDTH = RW_HEADS * RW_HEAD
RW_DECAY_LORA = 32
RW_A_LORA = 32
RW_G_LORA = 64
RW_IN = 3 * RW_WIDTH + RW_DECAY_LORA + RW_A_LORA + RW_G_LORA
RW_SPLITS = [RW_WIDTH, 2 * RW_WIDTH, 3 * RW_WIDTH, 3 * RW_WIDTH + RW_DECAY_LORA,
             3 * RW_WIDTH + RW_DECAY_LORA + RW_A_LORA]
GN_EPS = 64e-5
L2_EPS = 1e-12
MLA_HEADS = 8
QK_NOPE = 64
QK_ROPE = 32
V_HEAD = 64
Q_LORA = 256
KV_LORA = 128
MLA_IN = Q_LORA + KV_LORA + QK_ROPE
MLA_WIDTH = MLA_HEADS * V_HEAD
MLA_SCALE = (QK_NOPE + QK_ROPE) ** -0.5
ROPE_BASE = 10000.0
MIX_IN = 2 * RG_WIDTH + RW_IN + MLA_IN
MIX_SPLITS = [RG_WIDTH, 2 * RG_WIDTH, 2 * RG_WIDTH + RW_IN]
MIX_WIDTH = RG_WIDTH + RW_WIDTH + MLA_WIDTH
D_FF = 4 * D_MODEL
EPS = 1e-6

kernel_name = 'hybrid_streaming_encoder_step'

def rmsnorm(x, g):
    xf = x.astype(jnp.float32)
    y = xf * lax.rsqrt(jnp.mean(xf * xf, axis=-1, keepdims=True) + EPS)
    return (y * g).astype(x.dtype)

def apply_rope(x, pos):
    half = x.shape[-1] // 2
    inv = ROPE_BASE ** (-jnp.arange(half, dtype=jnp.float32) / half)
    ang = pos.astype(jnp.float32)[:, None] * inv
    shp = (pos.shape[0],) + (1,) * (x.ndim - 3) + (half,)
    cos, sin = jnp.cos(ang).reshape(shp), jnp.sin(ang).reshape(shp)
    xf = x.astype(jnp.float32)
    x1, x2 = xf[..., :half], xf[..., half:]
    return jnp.concatenate([x1 * cos - x2 * sin, x2 * cos + x1 * sin], axis=-1).astype(x.dtype)

def _lin_combine(left, right):
    a_l, b_l = left
    a_r, b_r = right
    return a_l * a_r, a_r * b_l + b_r

def rglru_mixer(xr, gate, conv_buf, h0, P):
    B, S, W = xr.shape
    xp = jnp.concatenate([conv_buf.astype(xr.dtype), xr], axis=1)
    conv = P['rg_conv_b'] + sum(xp[:, j:j + S] * P['rg_conv_w'][j] for j in range(CONV_W))
    xc = conv.astype(jnp.float32)
    xb = xc.reshape(B, S, RG_BLOCKS, RG_BLOCK)
    r = jax.nn.sigmoid(jnp.einsum('bsgi,gij->bsgj', xb, P['rg_wa']).reshape(B, S, W) + P['rg_ba'])
    i = jax.nn.sigmoid(jnp.einsum('bsgi,gij->bsgj', xb, P['rg_wx']).reshape(B, S, W) + P['rg_bx'])
    log_a = -LRU_C * r * jax.nn.softplus(-P['rg_lambda'].astype(jnp.float32))
    a = jnp.exp(log_a)
    b = jnp.sqrt(-jnp.expm1(2.0 * log_a)) * (i * xc)
    a_cum, b_cum = lax.associative_scan(_lin_combine, (a, b), axis=1)
    h = a_cum * h0.astype(jnp.float32)[:, None, :] + b_cum
    y = jax.nn.gelu(gate.astype(jnp.float32)) * h
    return y.astype(xr.dtype), xp[:, -(CONV_W - 1):], h[:, -1].astype(xr.dtype)

def rwkv7_mixer(p, shift_prev, state0, P):
    B, S, _ = p.shape
    prev = jnp.concatenate([shift_prev[:, None, :].astype(p.dtype), p[:, :-1]], axis=1)
    xs = (p + P['rw_mu'] * (prev - p)).astype(jnp.float32)
    r, k, v, wd, ad, gd = jnp.split(xs, RW_SPLITS, axis=-1)
    log_w = -jax.nn.softplus(-(P['rw_w0'] + jnp.tanh(wd) @ P['rw_w2'])) - 0.5
    w = jnp.exp(-jnp.exp(log_w))
    a = jax.nn.sigmoid(P['rw_a0'] + ad @ P['rw_a2'])
    g = jax.nn.sigmoid(gd) @ P['rw_g2']
    heads = lambda t: t.reshape(B, S, RW_HEADS, RW_HEAD)
    kk = heads(k * P['rw_k_k'])
    kk = kk * lax.rsqrt(jnp.sum(kk * kk, axis=-1, keepdims=True) + L2_EPS)
    k = k * (1.0 + (a - 1.0) * P['rw_k_a'])
    r_h, w_h, k_h, v_h, a_h = heads(r), heads(w), heads(k), heads(v), heads(a)

    def step(Sm, inp):
        r_t, w_t, k_t, v_t, kk_t, a_t = inp
        sa = jnp.einsum('bhij,bhj->bhi', Sm, kk_t)
        Sm = (Sm * w_t[:, :, None, :] - sa[..., None] * (kk_t * a_t)[:, :, None, :]
              + v_t[..., None] * k_t[:, :, None, :])
        return Sm, jnp.einsum('bhij,bhj->bhi', Sm, r_t)

    seq_first = lambda t: jnp.moveaxis(t, 1, 0)
    s_fin, y = lax.scan(step, state0.astype(jnp.float32),
                        (seq_first(r_h), seq_first(w_h), seq_first(k_h), seq_first(v_h),
                         seq_first(kk), seq_first(a_h)))
    y = jnp.moveaxis(y, 0, 1)
    mu = jnp.mean(y, axis=-1, keepdims=True)
    var = jnp.mean(jnp.square(y - mu), axis=-1, keepdims=True)
    y = ((y - mu) * lax.rsqrt(var + GN_EPS)).reshape(B, S, RW_WIDTH) * P['rw_gn_w'] + P['rw_gn_b']
    bonus = jnp.sum(r_h * k_h * P['rw_r_k'], axis=-1, keepdims=True) * v_h
    y = (y + bonus.reshape(B, S, RW_WIDTH)) * g
    return y.astype(p.dtype), p[:, -1], s_fin.astype(p.dtype)

def mla_project(p, pos, P):
    cq, ckv, kr = jnp.split(p, [Q_LORA, Q_LORA + KV_LORA], axis=-1)
    q = jnp.einsum('bsc,chd->bshd', rmsnorm(cq, P['mla_q_norm']), P['mla_w_uq'])
    q_rope = apply_rope(q[..., QK_NOPE:], pos)
    q_lat = jnp.einsum('bshd,chd->bshc', q[..., :QK_NOPE], P['mla_w_uk'])
    return q_lat, q_rope, rmsnorm(ckv, P['mla_kv_norm']), apply_rope(kr, pos)

def mla_attend_blockcausal(q_lat, q_rope, ckv, kr):
    B, S, H, C = q_lat.shape
    nb = S // Q_BLOCK
    qb = q_lat.reshape(B, nb, Q_BLOCK, H, C).transpose(1, 0, 2, 3, 4)
    rb = q_rope.reshape(B, nb, Q_BLOCK, H, QK_ROPE).transpose(1, 0, 2, 3, 4)
    key_chunk = jnp.arange(S) // CHUNK

    def one(args):
        blk, qlb, qrb = args
        q_chunk = (blk * Q_BLOCK + jnp.arange(Q_BLOCK)) // CHUNK
        s = (jnp.einsum('bqhc,bkc->bhqk', qlb, ckv)
             + jnp.einsum('bqhr,bkr->bhqk', qrb, kr)).astype(jnp.float32) * MLA_SCALE
        s = jnp.where(key_chunk[None, :] <= q_chunk[:, None], s, -jnp.inf)
        pr = jax.nn.softmax(s, axis=-1).astype(ckv.dtype)
        return jnp.einsum('bhqk,bkc->bqhc', pr, ckv)

    o = lax.map(one, (jnp.arange(nb), qb, rb))
    return o.transpose(1, 0, 2, 3, 4).reshape(B, S, H, C)

def mla_attend_full(q_lat, q_rope, ckv, kr):
    s = (jnp.einsum('bqhc,bkc->bhqk', q_lat, ckv)
         + jnp.einsum('bqhr,bkr->bhqk', q_rope, kr)).astype(jnp.float32) * MLA_SCALE
    pr = jax.nn.softmax(s, axis=-1).astype(ckv.dtype)
    return jnp.einsum('bhqk,bkc->bqhc', pr, ckv)

def token_mix(x, pos, P, rg_buf, rg_h, rw_shift, rw_state, past_ckv, past_kr):
    B, S, _ = x.shape
    p = rmsnorm(x, P['norm_mix']) @ P['w_in']
    p_rg, p_gate, p_rw, p_mla = jnp.split(p, MIX_SPLITS, axis=-1)
    y_rg, rg_buf_new, rg_h_new = rglru_mixer(p_rg, p_gate, rg_buf, rg_h, P)
    y_rw, rw_shift_new, rw_state_new = rwkv7_mixer(p_rw, rw_shift, rw_state, P)
    q_lat, q_rope, ckv, kr = mla_project(p_mla, pos, P)
    if past_ckv is None:
        o_lat = mla_attend_blockcausal(q_lat, q_rope, ckv, kr)
    else:
        o_lat = mla_attend_full(q_lat, q_rope,
                                jnp.concatenate([past_ckv.astype(ckv.dtype), ckv], axis=1),
                                jnp.concatenate([past_kr.astype(kr.dtype), kr], axis=1))
    y_mla = jnp.einsum('bshc,chv->bshv', o_lat, P['mla_w_uv']).reshape(B, S, MLA_WIDTH)
    y = jnp.concatenate([y_rg, y_rw, y_mla], axis=-1) @ P['w_out']
    return x + y, (rg_buf_new, rg_h_new, rw_shift_new, rw_state_new, ckv, kr)

def mem_project(mem, g, wk, wv):
    m = rmsnorm(mem, g)
    return jnp.einsum('bmd,dhe->bmhe', m, wk), jnp.einsum('bmd,dhe->bmhe', m, wv)

def mem_attend(h, mk, mv, wq, wo):
    q = jnp.einsum('bsd,dhe->bshe', h, wq)
    s = jnp.einsum('bshe,bmhe->bhsm', q, mk.astype(q.dtype)).astype(jnp.float32) * MEM_SCALE
    pr = jax.nn.softmax(s, axis=-1).astype(q.dtype)
    o = jnp.einsum('bhsm,bmhe->bshe', pr, mv.astype(q.dtype))
    return jnp.einsum('bshe,hed->bsd', o, wo)

def layer(x, pos, P, rg_buf, rg_h, rw_shift, rw_state, past_ckv, past_kr, mem_k, mem_v):
    x, new_state = token_mix(x, pos, P, rg_buf, rg_h, rw_shift, rw_state, past_ckv, past_kr)
    x = x + mem_attend(rmsnorm(x, P['norm_mem']), mem_k, mem_v, P['mem_w_q'], P['mem_w_o'])
    h = rmsnorm(x, P['norm_ffn'])
    x = x + jnp.square(jax.nn.relu(h @ P['ffn_w1'])) @ P['ffn_w2']
    return x, new_state

def setup_inputs(seed: int = 0) -> dict:
    key = jax.random.key(seed)
    keys = iter(jax.random.split(key, 64))
    f32 = jnp.float32
    L = DEPTH

    def nrm(shape, scale):
        return scale * jax.random.normal(next(keys), shape, f32)

    def gain(shape):
        return 1.0 + 0.05 * jax.random.normal(next(keys), shape, f32)

    def unif(shape, lo, hi):
        return jax.random.uniform(next(keys), shape, f32, lo, hi)

    return {
        'x_prompt': nrm((BATCH, SEQ, D_MODEL), 1.0),
        'x_sample': nrm((DEC_BATCH, DEC_SEQ, D_MODEL), 1.0),
        'state_rg_conv': nrm((L, DEC_BATCH, CONV_W - 1, RG_WIDTH), 1.0),
        'state_rg_h': nrm((L, DEC_BATCH, RG_WIDTH), 0.5),
        'state_rw_shift': nrm((L, DEC_BATCH, RW_IN), 1.0),
        'state_rw_wkv': nrm((L, DEC_BATCH, RW_HEADS, RW_HEAD, RW_HEAD), 0.1),
        'cache_mla_ckv': nrm((L, DEC_BATCH, PAST_LEN, KV_LORA), 1.0),
        'cache_mla_krope': nrm((L, DEC_BATCH, PAST_LEN, QK_ROPE), 1.0),
        'cache_mem_k': nrm((L, DEC_BATCH, N_MEM, MEM_HEADS, MEM_HEAD), 1.0),
        'cache_mem_v': nrm((L, DEC_BATCH, N_MEM, MEM_HEADS, MEM_HEAD), 1.0),
        'mem_prompt': nrm((BATCH, N_MEM, D_MODEL), 1.0),
        'norm_mix': gain((L, D_MODEL)),
        'w_in': nrm((L, D_MODEL, MIX_IN), D_MODEL ** -0.5),
        'rg_conv_w': nrm((L, CONV_W, RG_WIDTH), CONV_W ** -0.5),
        'rg_conv_b': nrm((L, RG_WIDTH), 0.01),
        'rg_wa': nrm((L, RG_BLOCKS, RG_BLOCK, RG_BLOCK), RG_BLOCK ** -0.5),
        'rg_ba': nrm((L, RG_WIDTH), 0.01),
        'rg_wx': nrm((L, RG_BLOCKS, RG_BLOCK, RG_BLOCK), RG_BLOCK ** -0.5),
        'rg_bx': nrm((L, RG_WIDTH), 0.01),
        'rg_lambda': unif((L, RG_WIDTH), 2.0, 6.0),
        'rw_mu': unif((L, RW_IN), 0.0, 1.0),
        'rw_w0': nrm((L, RW_WIDTH), 0.5),
        'rw_w2': nrm((L, RW_DECAY_LORA, RW_WIDTH), 0.1),
        'rw_a0': nrm((L, RW_WIDTH), 0.5),
        'rw_a2': nrm((L, RW_A_LORA, RW_WIDTH), 0.1),
        'rw_g2': nrm((L, RW_G_LORA, RW_WIDTH), RW_G_LORA ** -0.5),
        'rw_k_k': 0.85 + nrm((L, RW_WIDTH), 0.05),
        'rw_k_a': gain((L, RW_WIDTH)),
        'rw_r_k': nrm((L, RW_HEADS, RW_HEAD), 0.1),
        'rw_gn_w': gain((L, RW_WIDTH)),
        'rw_gn_b': nrm((L, RW_WIDTH), 0.01),
        'mla_q_norm': gain((L, Q_LORA)),
        'mla_kv_norm': gain((L, KV_LORA)),
        'mla_w_uq': nrm((L, Q_LORA, MLA_HEADS, QK_NOPE + QK_ROPE), Q_LORA ** -0.5),
        'mla_w_uk': nrm((L, KV_LORA, MLA_HEADS, QK_NOPE), KV_LORA ** -0.5),
        'mla_w_uv': nrm((L, KV_LORA, MLA_HEADS, V_HEAD), KV_LORA ** -0.5),
        'w_out': nrm((L, MIX_WIDTH, D_MODEL), MIX_WIDTH ** -0.5),
        'norm_mem': gain((L, D_MODEL)),
        'norm_mem_kv': gain((L, D_MODEL)),
        'mem_w_q': nrm((L, D_MODEL, MEM_HEADS, MEM_HEAD), D_MODEL ** -0.5),
        'mem_w_k': nrm((L, D_MODEL, MEM_HEADS, MEM_HEAD), D_MODEL ** -0.5),
        'mem_w_v': nrm((L, D_MODEL, MEM_HEADS, MEM_HEAD), D_MODEL ** -0.5),
        'mem_w_o': nrm((L, MEM_HEADS, MEM_HEAD, D_MODEL), D_MODEL ** -0.5),
        'norm_ffn': gain((L, D_MODEL)),
        'ffn_w1': nrm((L, D_MODEL, D_FF), D_MODEL ** -0.5),
        'ffn_w2': nrm((L, D_FF, D_MODEL), D_FF ** -0.5),
        'norm_final': gain((D_MODEL,)),
    }

def reference(x_prompt, x_sample, state_rg_conv, state_rg_h, state_rw_shift, state_rw_wkv,
              cache_mla_ckv, cache_mla_krope, cache_mem_k, cache_mem_v, mem_prompt,
              norm_mix, w_in, rg_conv_w, rg_conv_b, rg_wa, rg_ba, rg_wx, rg_bx, rg_lambda,
              rw_mu, rw_w0, rw_w2, rw_a0, rw_a2, rw_g2, rw_k_k, rw_k_a, rw_r_k, rw_gn_w, rw_gn_b,
              mla_q_norm, mla_kv_norm, mla_w_uq, mla_w_uk, mla_w_uv, w_out,
              norm_mem, norm_mem_kv, mem_w_q, mem_w_k, mem_w_v, mem_w_o,
              norm_ffn, ffn_w1, ffn_w2, norm_final):
    Bp, S_p, _ = x_prompt.shape
    S_s = x_sample.shape[1]
    past = cache_mla_ckv.shape[2]
    dt = x_prompt.dtype
    pos_p = jnp.arange(S_p, dtype=jnp.int32)
    pos_s = past + jnp.arange(S_s, dtype=jnp.int32)
    z_conv = jnp.zeros((Bp, CONV_W - 1, RG_WIDTH), dt)
    z_h = jnp.zeros((Bp, RG_WIDTH), dt)
    z_shift = jnp.zeros((Bp, RW_IN), dt)
    z_wkv = jnp.zeros((Bp, RW_HEADS, RW_HEAD, RW_HEAD), dt)

    xp, xs = x_prompt, x_sample
    p_states, s_states = [], []
    for l in range(DEPTH):
        P = {
            'norm_mix': norm_mix[l], 'w_in': w_in[l], 'w_out': w_out[l],
            'rg_conv_w': rg_conv_w[l], 'rg_conv_b': rg_conv_b[l], 'rg_wa': rg_wa[l],
            'rg_ba': rg_ba[l], 'rg_wx': rg_wx[l], 'rg_bx': rg_bx[l], 'rg_lambda': rg_lambda[l],
            'rw_mu': rw_mu[l], 'rw_w0': rw_w0[l], 'rw_w2': rw_w2[l], 'rw_a0': rw_a0[l],
            'rw_a2': rw_a2[l], 'rw_g2': rw_g2[l], 'rw_k_k': rw_k_k[l], 'rw_k_a': rw_k_a[l],
            'rw_r_k': rw_r_k[l], 'rw_gn_w': rw_gn_w[l], 'rw_gn_b': rw_gn_b[l],
            'mla_q_norm': mla_q_norm[l], 'mla_kv_norm': mla_kv_norm[l],
            'mla_w_uq': mla_w_uq[l], 'mla_w_uk': mla_w_uk[l], 'mla_w_uv': mla_w_uv[l],
            'norm_mem': norm_mem[l], 'mem_w_q': mem_w_q[l], 'mem_w_o': mem_w_o[l],
            'norm_ffn': norm_ffn[l], 'ffn_w1': ffn_w1[l], 'ffn_w2': ffn_w2[l],
        }
        mem_k_l, mem_v_l = mem_project(mem_prompt, norm_mem_kv[l], mem_w_k[l], mem_w_v[l])
        xp, st_p = layer(xp, pos_p, P, z_conv, z_h, z_shift, z_wkv, None, None, mem_k_l, mem_v_l)
        xs, st_s = layer(xs, pos_s, P, state_rg_conv[l], state_rg_h[l], state_rw_shift[l],
                         state_rw_wkv[l], cache_mla_ckv[l], cache_mla_krope[l],
                         cache_mem_k[l], cache_mem_v[l])
        p_states.append(st_p + (mem_k_l, mem_v_l))
        s_states.append(st_s)

    y_prompt = rmsnorm(xp, norm_final)
    y_sample = rmsnorm(xs, norm_final)
    sp = [jnp.stack(t) for t in zip(*p_states)]
    ss = [jnp.stack(t) for t in zip(*s_states)]
    return (y_prompt, y_sample,
            sp[0], sp[1], sp[2], sp[3], sp[4], sp[5], sp[6], sp[7],
            ss[0], ss[1], ss[2], ss[3], ss[4], ss[5])


_drawn_inputs = setup_inputs


def setup_inputs(seed=0):
    import zlib

    import numpy as np

    out = dict(_drawn_inputs(seed))
    spreads = {}
    factors = {'rg_ba': 26.372,
     'rg_bx': 8.0,
     'rw_k_k': 3.606,
     'rw_gn_w': 3.183,
     'rw_gn_b': 8.0,
     'mla_q_norm': 8.0,
     'norm_mem': 8.0}
    for name, (base, spread) in spreads.items():
        noise = np.random.default_rng([zlib.crc32(name.encode()), seed]).standard_normal(out[name].shape)
        drawn = base * np.exp(spread * noise) if base else spread * noise
        out[name] = __import__('jax').numpy.asarray(drawn.astype(out[name].dtype))
    for name, factor in factors.items():
        out[name] = (out[name] * factor).astype(out[name].dtype)
    return out
```

```python
import numpy as np
import concourse.bass as bass
from concourse import mybir
from contextlib import ExitStack

DEPTH, SEQ, DEC, PAST, D = 2, 512, 32, 256, 1024
T = SEQ + DEC
HALF = T // 2
KT = D // 128
MEM, MHEADS = 256, 4
RG_COLS, CONV = 2, 4
RGW = (CONV - 1) + SEQ + (CONV - 1) + DEC
XCW = RGW - (CONV - 1)
XH = XCW // 2 + 1
RWT = 7
RWW = 1 + SEQ + 1 + DEC
CH = 64
GRP = 128
NG = SEQ // GRP + 1
FR = NG * GRP
HEADS, NOPE, ROPE = 8, 64, 32
QKD = NOPE + ROPE
KEYS = T + PAST
MLA_SCALE = float(QKD) ** -0.5
MEM_SCALE = 256.0 ** -0.5
FF = 32
EPS, GN_EPS, L2_EPS = 1e-6, 64e-5, 1e-12
EXP_HALF = float(np.exp(-0.5))
GELU_C = float(np.sqrt(2.0 / np.pi))
NEG = -1e30

VEC = {}
_n = 0
for _name, _w in (("g_mix", 8), ("g_mem", 8), ("g_memkv", 8), ("g_ffn", 8), ("conv_w", 8), ("conv_b", 2),
                  ("rg_ba", 2), ("rg_bx", 2), ("w0", 2), ("a0", 2), ("lam", 2), ("mu", 7), ("k_k", 2), ("k_a", 2),
                  ("r_k", 2), ("gn_w", 2), ("gn_b", 2), ("q_norm", 2), ("kv_norm", 1), ("h0", 2),
                  ("shift", 7), ("conv_s", 6)):
    VEC[_name] = _n
    _n += _w
NV = _n

LW = {}
_n = 0
for _name, _w in (("wa", 256), ("wx", 256), ("low", 256), ("uq", 2 * HEADS * QKD), ("uqs", 2 * HEADS * ROPE),
                  ("uk", HEADS * NOPE), ("uv", HEADS * 64), ("ckv", PAST), ("kr", PAST), ("S0", 256)):
    LW[_name] = _n
    _n += _w
NLW = _n

CST = {}
_n = 0
for _name, _w in (("ident", 128), ("ones", 128), ("bones", 128), ("mask2", 256), ("maskL", 128), ("lev", 6 * 128),
                  ("lev1t", 128), ("cos", T), ("sin", T), ("reset", GRP), ("maskq", 128), ("maskk", 128), ("g_final", 8)):
    CST[_name] = _n
    _n += _w
NCST = _n

STAGES = [("in", 8), ("out", 4), ("mk", 4), ("mv", 4), ("mq", 4), ("mo", 4), ("f1", 16), ("f2", 16)]
CHUNKS = [(st, c) for st, n in STAGES for c in range(n)]
NCH = len(CHUNKS)
RING = 3
TILES = []
for _st, _k in STAGES:
    for _i in range(8 if _st == "f2" else 2 * _k):
        TILES.append((_st, _i, "act" if _st in ("mk", "mv", "f1") else "dve"))
NT = len(TILES)
TILE0 = {}
for _i, (_st, _j, _e) in enumerate(TILES):
    TILE0.setdefault(_st, _i)
EVAC_PER_LAYER = {e: sum(t[2] == e for t in TILES) for e in ("act", "dve")}


def evac_value(layer, tile):
    eng = TILES[tile][2]
    return eng, layer * EVAC_PER_LAYER[eng] + sum(t[2] == eng for t in TILES[:tile + 1])


OUTS = [("y_out", (128, 8, T)), ("last_out", (DEPTH, 128, 30)), ("wkv_out", (DEPTH, 128, 2, 2, 128)),
        ("ckv_out", (DEPTH, 128, T)), ("kr_out", (DEPTH, ROPE, T)),
        ("memk_out", (DEPTH, 128, 8, MEM)), ("memv_out", (DEPTH, 128, 2, D))]

NSTATE = 2 * NG - 1
PER_LAYER = {
    "sq_ready": 24, "rms_sum": 3, "rms_rstd": 3, "h_ready": 24,
    "frames_zeroed": 1, "rows_kept": 2,
    "rg_conv": 1, "rg_z": 4, "rg_gates": 1, "rg_gelu_in": 1, "rg_gelu": 1, "rg_ix": 1, "rg_ln": 1, "rg_q": 1,
    "rg_sq": 1, "rg_done": 1,
    "low_ready": 1, "low_tanh": 1, "low_z": 4, "low_gate": 4, "kk_raw": 1, "kk_sq": 1, "kk_sum": 2,
    "kk_rstd": 1, "rk_ready": 1, "rk_sum": 2,
    "decay_cum": NG, "decay_exp": NG, "factors": NG, "masked": NG, "tok_T": NG, "tok_out": NG, "scores": NG,
    "scores_out": NG, "mv": NG, "mv_out": NG, "lev_T": 5 * NG, "lev_P": 5 * NG, "lev_P_out": 5 * NG,
    "lev_X": 5 * NG, "lev_X_out": 5 * NG, "xr": NG, "xr_out": NG, "ab": NG, "ab_out": NG,
    "state_mm": NSTATE, "state_out": NSTATE, "y_out": NG,
    "gn_sum": 4, "gn_mean": 1, "gn_sq": 1, "gn_rstd": 1, "g_out": 1, "rw_y": 1,
    "lat_sq": 1, "lat_sum": 2, "lat_rstd": 2, "cq_n": 1, "ckv_n": 1, "kr_ready": 1,
    "v_mm": 7, "v_out": 7, "q_mm": HEADS, "q_out": 2 * HEADS, "k_mm": HEADS, "k_out": HEADS,
    "a_score": 40, "a_max": 40, "a_exp": 40, "a_norm": 40, "a_T": 40, "a_T_out": 40, "a_pv": 40, "a_o": 40,
    "m_score": 20, "m_max": 20, "m_exp": 20, "m_norm": 20, "m_T": 20, "m_T_out": 20, "m_pv": 16, "m_o": 16,
    "memn": 1, "hid_sq": 32,
}


def build(nc, wall, lw_d, vec_d, cst_d, x_d, mem_d, mks_d, mvs_d, outs):
    F32 = mybir.dt.float32
    ALU = mybir.AluOpType
    ACT = mybir.ActivationFunctionType
    AX = mybir.AxisListType.X
    ctx = ExitStack()
    with ctx:
        def sb(name, shape):
            return ctx.enter_context(nc.sbuf_tensor(name, shape, F32))

        def sem(name):
            return ctx.enter_context(nc.semaphore(name))

        xT = sb("xT", [128, 8, T])
        hT = sb("hT", [128, 8, T])
        ring = sb("ring", [128, RING, 8, 256])
        big = sb("big", [128, 32 * T])
        tmp = sb("tmp", [128, 10000])
        memT = sb("memT", [128, 8, MEM])
        lw = sb("lw", [128, NLW])
        vec = sb("vec", [128, DEPTH, NV])
        cst = sb("cst", [128, NCST])
        rs = sb("rs", [128, T])
        stat = sb("stat", [128, 64])
        last_rows = sb("last_rows", [128, 30])
        derv = sb("derv", [128, DEPTH, 12])
        PS = ctx.enter_context(nc.psum_tensor("PS", [128, 8 * 512], F32))

        def carve(region, at, limit, *specs):
            got = []
            for shape in specs:
                n = int(np.prod(shape))
                v = region[:, at:at + n]
                if len(shape) == 2:
                    v = v.rearrange("p (a b) -> p a b", a=shape[0])
                if len(shape) == 3:
                    v = v.rearrange("p (a b c) -> p a b c", a=shape[0], b=shape[1])
                got.append(v)
                at += n
            assert at <= limit, (at, limit)
            return got

        flat = hT[:, :, :].rearrange("p a b -> p (a b)")
        raw, xs, ell, bneg, kk, cq, ckv, kr, rg, gate, Vm, Wm = carve(
            big, 0, 32 * T, (RWT, RWW), (RWT, FR), (2, FR), (2, FR), (2, FR), (2, T), (T,), (T,), (2, RGW),
            (2, T), (2, 192), (2, 192))
        bonus, X, XT, L, P, TT = carve(big, 0, RWT * RWW, (2, T), (4, 128), (4, 128), (4, 128), (4, 128), (4, 128))
        xc, ra, ru, rln, rix, gx, rh = carve(
            tmp, 0, 10000, (2, XCW), (2, XCW), (2, XCW), (2, XCW), (2, XCW), (2, T), (2, T))
        (Lc, dm, le, ep, en1, en, ee, af, rf, bf, kf, be, ke, AR, LG, MG, BE, KE, S, Abd, Bbd, Rt, rp, yl) = carve(
            tmp, 0, 10000, *[(2, 128)] * 13, (4, 256), (4, 256), (4, 256), (2, 2, 128), (2, 2, 128), (2, 2, 128),
            (2, 2, 128), (2, 2, 128), (4, 128), (2, 128), (2, 128))
        yrw, Ym = carve(flat, 4 * T, 8 * T, (2, FR), (2, 192))
        e1, e2 = carve(flat, 4 * T, 8 * T, (2, T), (2, T))
        aq, ak, aP, aPT, av = carve(tmp, 0, 10000, (2, T), (2, KEYS), (2, 512), (2, 512), (7, 512))
        mq, mks, mvs, memn = carve(big, 0, 24 * T, (8, T), (8, MEM), (2, D), (8, MEM))
        mkp, mvp, mP, mPT = carve(tmp, 0, 10000, (8, MEM), (2, D), (2, 256), (2, 2, T))
        hid = big[:, :].rearrange("p (a b) -> p a b", a=32)
        sqbig = hid[:, 24:32, :]

        def C(name, a, b, rows=slice(0, 128)):
            return cst[rows, CST[name] + a:CST[name] + b]

        def V(l, name, i=0):
            return vec[:, l, VEC[name] + i:VEC[name] + i + 1]

        def W(name, a, b, rows=slice(0, 128)):
            return lw[rows, LW[name] + a:LW[name] + b]

        def bc(ap, n):
            return ap.unsqueeze(1).to_broadcast([128, n, ap.shape[-1]])

        def pair(ap, n=2):
            return ap.rearrange("p (a b) -> p a b", a=n)

        ident, ones, bones = (C(n, 0, 128) for n in ("ident", "ones", "bones"))
        rows_of = [slice(0, 64), slice(64, 128)]
        rope = slice(64, 96)
        C_TINY, C_EPS, C_L2, C_GN, C_ONE = 59, 60, 61, 62, 63

        def K(i):
            return stat[:, i:i + 1]

        def Q(q, n=T):
            return PS[:, q * 1024 + 512 - (n + 1) // 2:q * 1024 + 512 - (n + 1) // 2 + n]

        def bank(i, a=0, b=512):
            return PS[:, i * 512 + a:i * 512 + b]

        w_load = [sem(f"w_load{i}") for i in range(RING)]
        pe_done = sem("pe_done")
        evac = {"act": sem("evac_act"), "dve": sem("evac_dve")}
        setup_ld, lw_ld, mem_ld = sem("setup_ld"), sem("lw_ld"), sem("mem_ld")
        stored = {n: sem("stored_" + n) for n in ("last", "wkv", "latent", "mem", "y")}
        vstep, astep, setup_abs, setup_exp, setup_vec = (
            sem(n) for n in ("vstep", "astep", "setup_abs", "setup_exp", "setup_vec"))
        s = {n: sem(n) for n in PER_LAYER}
        before = dict(sq_ready=8, rms_sum=1, rms_rstd=1, h_ready=8)

        def at(l, name, i=1):
            return before.get(name, 0) + l * PER_LAYER[name] + i

        tile_v, chunk_v, n_ = {}, [], 0
        for st_, c_ in CHUNKS:
            if st_ == "f2" and c_ % 4 != 3:
                n_ += 1
            else:
                for k_ in range(2):
                    n_ += 1
                    tile_v[TILE0[st_] + (2 * (c_ // 4) + k_ if st_ == "f2" else 2 * c_ + k_)] = n_
            chunk_v.append(n_)
        PE_LAYER = n_

        def tile_done(l, st, i):
            return l * PE_LAYER + tile_v[TILE0[st] + i]

        def wait_evac(e, l, st, i):
            eng, v = evac_value(l, TILE0[st] + i)
            e.wait_ge(evac[eng], v)

        block = ctx.enter_context(nc.Block())

        @block.sync
        def _(e):
            e.dma_start(xT[:, :, :], x_d).then_inc(setup_ld, 16)
            e.dma_start(cst[:, :], cst_d).then_inc(setup_ld, 16)
            e.dma_start(vec[:, :, :], vec_d).then_inc(setup_ld, 16)
            e.dma_start(memT[:, :, :], mem_d).then_inc(setup_ld, 16)
            for l in range(DEPTH):
                for c in range(NCH):
                    n = l * NCH + c
                    if n >= RING:
                        m = n - RING
                        e.wait_ge(pe_done, (m // NCH) * PE_LAYER + chunk_v[m % NCH])
                    e.dma_start(ring[:, n % RING, :, :].rearrange("p a b -> p (a b)"),
                                wall[l, c]).then_inc(w_load[n % RING], 16)

        @block.gpsimd
        def _(e):
            e.dma_start(lw[:, :], lw_d[0]).then_inc(lw_ld, 16)

            def put(kind, out, src):
                e.dma_start(out, src).then_inc(stored[kind], 16)

            for l in range(DEPTH):
                if l:
                    e.wait_ge(stored["last"], 16 * l)
                wait_evac(e, l, "in", 0)
                e.memset(xs[:, :, T:FR], 0.0)
                e.memset(ell[:, :, T:FR], 0.0)
                e.memset(bneg[:, :, T:FR], 0.0)
                e.memset(kk[:, :, T:FR], 0.0)
                for m in (Vm, Wm):
                    e.memset(m[:, :, 64:128], 0.0)
                wait_evac(e, l, "in", 15)
                e.tensor_copy(pair(last_rows[:, 0:14], 7), raw[:, :, SEQ:RWW:RWW - 1 - SEQ])\
                    .then_inc(s["rows_kept"], 1)
                for c, a in ((0, SEQ), (3, RGW - 3)):
                    e.tensor_copy(pair(last_rows[:, 14:26])[:, :, c:c + 3], rg[:, :, a:a + 3])
                e.wait_ge(s["rg_done"], at(l, "rg_done"))
                e.tensor_copy(pair(last_rows[:, 26:30]), rh[:, :, SEQ - 1:T:DEC]).then_inc(s["rows_kept"], 1)
                e.wait_ge(s["rows_kept"], at(l, "rows_kept", 2))
                put("last", outs["last_out"][l], last_rows[:, :])
                for m in (AR, BE, KE):
                    e.memset(m, 0.0)
                e.memset(Ym[:, :, 64:128], 0.0)
                e.memset(S[:, 0, :, :], 0.0).then_inc(s["frames_zeroed"], 1)
                e.wait_ge(s["state_out"], at(l, "state_out", NSTATE - 1))
                put("wkv", outs["wkv_out"][l, :, 0], S[:, 0, :, :])
                e.wait_ge(s["state_out"], at(l, "state_out", NSTATE))
                put("wkv", outs["wkv_out"][l, :, 1], S[:, 1, :, :])
                e.wait_ge(s["kr_ready"], at(l, "kr_ready"))
                put("latent", outs["kr_out"][l], kr[rope, :])
                e.wait_ge(s["ckv_n"], at(l, "ckv_n"))
                put("latent", outs["ckv_out"][l], ckv)
                wait_evac(e, l, "out", 0)
                if l + 1 < DEPTH:
                    e.dma_start(lw[:, :], lw_d[l + 1]).then_inc(lw_ld, 16)
                e.dma_start(mks[:, :, :], mks_d[l]).then_inc(mem_ld, 16)
                e.dma_start(mvs[:, :, :], mvs_d[l]).then_inc(mem_ld, 16)
                wait_evac(e, l, "mk", 7)
                put("mem", outs["memk_out"][l], mkp)
                wait_evac(e, l, "mv", 7)
                put("mem", outs["memv_out"][l], mvp)
            e.wait_ge(s["h_ready"], at(DEPTH, "h_ready", 8))
            put("y", outs["y_out"], hT[:, :, :])
            for kind, n in (("last", 1), ("wkv", 2), ("latent", 2), ("mem", 2)):
                e.wait_ge(stored[kind], 16 * n * DEPTH)
            e.wait_ge(stored["y"], 16)

        @block.tensor
        def _(e):
            def mm(out, a, b, start=True, stop=True):
                return e.matmul(out, lhsT=a, rhs=b, start=start, stop=stop)

            def halves(out, a, b, start=True, stop=True, n=T):
                h = (n + 1) // 2
                mm(out[:, 0:h], a, b[:, 0:h], start, stop)
                return mm(out[:, h:n], a, b[:, h:n], start, stop)

            def rms(r, sq, n=T):
                for k in range(8):
                    e.wait_ge(s["sq_ready"], 8 * r + k + 1)
                    if n == T:
                        last = halves(Q(2), ones, sq[:, k, :], k == 0, k == 7)
                    else:
                        last = mm(bank(4, 0, n), ones, sq[:, k, 0:n], k == 0, k == 7)
                last.then_inc(s["rms_sum"], 1)

            def dense(l, st, rhs):
                for ci, (st_, c) in enumerate(CHUNKS):
                    if st_ != st:
                        continue
                    n = l * NCH + ci
                    slot = n % RING
                    e.wait_ge(w_load[slot], 16 * (n // RING + 1))
                    for k2 in range(2):
                        i = 2 * (c // 4) + k2 if st == "f2" else 2 * c + k2
                        t = TILE0[st] + i
                        first, final = st != "f2" or c % 4 == 0, st != "f2" or c % 4 == 3
                        if first and l * NT + t >= 2:
                            eng, v = evac_value(l if t >= 2 else l - 1, (t - 2) % NT)
                            e.wait_ge(evac[eng], v)
                        out = Q(t % 2)
                        for k in range(8):
                            w = ring[:, slot, k, 128 * k2:128 * k2 + 128]
                            a, z = first and k == 0, final and k == 7
                            if st == "mv":
                                last = mm(bank(2 * (t % 2), 0, 256), memn[:, k, 128 * k2:128 * k2 + 128],
                                          ring[:, slot, k, :], a, z)
                            elif st == "mk":
                                last = mm(bank(2 * (t % 2), 0, 256), w, memn[:, k, :], a, z)
                            elif st == "in" and i in (10, 11):
                                last = halves(out[rope, :], w[:, 0:ROPE], rhs(k), a, z)
                            elif st == "f2":
                                last = halves(out, w, rhs(8 * (c % 4) + k), a, z)
                            else:
                                last = halves(out, w, rhs(k), a, z)
                        if final or k2 == 1:
                            last.then_inc(pe_done, 1)

            e.wait_ge(setup_ld, 64)
            rms(0, hT, MEM)
            for l in range(DEPTH):
                rms(1 + 3 * l, hT)
                e.wait_ge(s["h_ready"], at(l, "h_ready", 8))
                dense(l, "in", lambda k: hT[:, k, :])

                e.wait_ge(lw_ld, 16 * (l + 1))
                e.wait_ge(s["rg_conv"], at(l, "rg_conv"))
                wait_evac(e, l, "in", 15)
                for g, name in enumerate(("wa", "wx")):
                    for t in range(2):
                        halves(Q(2 * g + t, XCW), W(name, 128 * t, 128 * t + 128), xc[:, t, :],
                               n=XCW).then_inc(s["rg_z"], 1)

                e.wait_ge(s["rg_gates"], at(l, "rg_gates"))
                e.wait_ge(s["low_tanh"], at(l, "low_tanh"))
                for m in range(2):
                    rows = slice(32 * m, 32 * m + 32)
                    for t in range(2):
                        halves(Q(2 * m + t), W("low", 128 * t, 128 * t + 128, rows),
                               xs[rows, 6, 0:T]).then_inc(s["low_z"], 1)
                e.wait_ge(s["low_gate"], at(l, "low_gate", 4))
                e.wait_ge(s["kk_sq"], at(l, "kk_sq"))
                for t in range(2):
                    halves(Q(t), bones, e1[:, t, :]).then_inc(s["kk_sum"], 1)
                e.wait_ge(s["rk_ready"], at(l, "rk_ready"))
                for t in range(2):
                    halves(Q(2 + t), bones, e2[:, t, :]).then_inc(s["rk_sum"], 1)

                e.wait_ge(s["rg_done"], at(l, "rg_done"))
                for g in range(NG):
                    e.wait_ge(s["factors"], at(l, "factors", g + 1))
                    if g:
                        e.wait_ge(s["y_out"], at(l, "y_out", g))
                    for t in range(2):
                        e.transpose(bank(0, 128 * t, 128 * t + 128), xs[:, 4 + t, GRP * g:GRP * g + GRP], ident)
                        e.transpose(bank(0, 256 + 128 * t, 384 + 128 * t), af[:, t, :], ident)
                        e.transpose(bank(1, 128 * t, 128 * t + 128), be[:, t, :], ident)
                        last = e.transpose(bank(1, 256 + 128 * t, 384 + 128 * t), ke[:, t, :], ident)
                    last.then_inc(s["tok_T"], 1)
                    e.wait_ge(s["masked"], at(l, "masked", g + 1))
                    for u in range(4):
                        mm(PS[:, 1024 + 256 * u:1280 + 256 * u], bf[:, u // 2, :], AR[:, u, :])
                        mm(PS[:, 2048 + 256 * u:2304 + 256 * u], kf[:, u // 2, :], AR[:, u, :])
                        last = mm(bank(6, 128 * u, 128 * u + 128), AR[:, u, 0:128], bf[:, u // 2, :])
                    last.then_inc(s["scores"], 1)
                    e.wait_ge(s["tok_out"], at(l, "tok_out", g + 1))
                    e.wait_ge(s["scores_out"], at(l, "scores_out", g + 1))
                    for u in range(4):
                        last = mm(bank(7, 64 * u, 64 * u + 64), MG[:, u, 0:128],
                                  Vm[:, u // 2, 128 * (u % 2):128 * (u % 2) + 64])
                    last.then_inc(s["mv"], 1)
                    for b in range(5):
                        n = 5 * g + b
                        e.wait_ge(s["lev_T"], at(l, "lev_T", n + 1))
                        if b:
                            e.wait_ge(s["lev_X_out"], at(l, "lev_X_out", n))
                        for u in range(4):
                            last = mm(bank(0, 128 * u, 128 * u + 128), TT[:, u, :], X[:, u, :])
                        last.then_inc(s["lev_P"], 1)
                        e.wait_ge(s["lev_P_out"], at(l, "lev_P_out", n + 1))
                        for u in range(4):
                            mm(bank(1, 128 * u, 128 * u + 128), XT[:, u, :], P[:, u, :])
                            last = mm(bank(2, 128 * u, 128 * u + 128), P[:, u, :], XT[:, u, :])
                        last.then_inc(s["lev_X"], 1)
                    e.wait_ge(s["lev_X_out"], at(l, "lev_X_out", 5 * g + 5))
                    e.wait_ge(s["mv_out"], at(l, "mv_out", g + 1))
                    for u in range(4):
                        last = mm(bank(3, 128 * u, 128 * u + 128), XT[:, u, :], Rt[:, u, :])
                    last.then_inc(s["xr"], 1)
                    e.wait_ge(s["xr_out"], at(l, "xr_out", g + 1))

                    def both(m, t):
                        return m[:, t, :].rearrange("p (a b) -> p a b", a=3)[:, 0:3:2, :]

                    for t in range(2):
                        for h in range(2):
                            mm(bank(4, 256 * t, 256 * t + 256)[rows_of[h], :], Wm[:, t, 128 * h:128 * h + 64],
                               BE[:, t, :, :].rearrange("p a b -> p (a b)"))
                    for t in range(2):
                        for c in range(2):
                            o = pair(bank(5, 256 * t + 128 * c, 256 * t + 128 * c + 128))
                            mm(o, KE[:, t, c, :], both(Vm, t), True, False)
                            mm(o, BE[:, t, c, :], both(Ym, t), False, True)
                    for t in range(2):
                        o = bank(6, 128 * t, 128 * t + 128)
                        mm(o, Wm[:, t, 0:128], LG[:, 2 * t, 128:256], True, False)
                        mm(o, Wm[:, t, 64:192], LG[:, 2 * t + 1, 128:256], False, True)
                    for t in range(2):
                        o = bank(6, 256 + 128 * t, 384 + 128 * t)
                        mm(o, Vm[:, t, 0:128], MG[:, 2 * t, 128:256], True, False)
                        mm(o, Vm[:, t, 64:192], MG[:, 2 * t + 1, 128:256], False, False)
                        mm(o, Ym[:, t, 0:128], LG[:, 2 * t, 128:256], False, False)
                        last = mm(o, Ym[:, t, 64:192], LG[:, 2 * t + 1, 128:256], False, True)
                    last.then_inc(s["ab"], 1)
                    e.wait_ge(s["ab_out"], at(l, "ab_out", g + 1))
                    for c in range(2 if g < NG - 1 else 1):
                        n = 2 * g + c
                        src = pair(W("S0", 0, 256)) if g == NG - 1 else S[:, c, :, :]
                        if n:
                            e.wait_ge(s["state_out"], at(l, "state_out", n))
                        for t in range(2):
                            mm(bank(0, 128 * t + 64 * c, 128 * t + 64 * c + 64), src[:, t, :],
                               rp[:, t, 64 * c:64 * c + 64])
                        for t in range(2):
                            last = mm(bank(7, 128 * t, 128 * t + 128), Abd[:, t, c, :], src[:, t, :])
                        last.then_inc(s["state_mm"], 1)

                e.wait_ge(s["y_out"], at(l, "y_out", NG))
                for t in range(2):
                    halves(Q(t), bones, yrw[:, t, 0:T]).then_inc(s["gn_sum"], 1)
                for t in range(2):
                    last = halves(Q(2 + t), W("low", 128 * t, 128 * t + 128, rows_of[1]), xs[64:128, 6, 0:T])
                last.then_inc(s["g_out"], 1)
                e.wait_ge(s["gn_sq"], at(l, "gn_sq"))
                for t in range(2):
                    halves(Q(t), bones, ell[:, t, 0:T]).then_inc(s["gn_sum"], 1)

                e.wait_ge(s["rw_y"], at(l, "rw_y"))
                e.wait_ge(s["lat_sq"], at(l, "lat_sq"))
                for t in range(2):
                    last = halves(Q(0), ones, kk[:, t, 0:T], t == 0, t == 1)
                last.then_inc(s["lat_sum"], 1)
                halves(Q(1), ones, bneg[:, 0, 0:T]).then_inc(s["lat_sum"], 1)
                e.wait_ge(s["ckv_n"], at(l, "ckv_n"))
                for j in range(7):
                    src = ckv[:, 128 * j:128 * j + (128 if j < 4 else DEC)] if j < 5 else \
                        W("ckv", 128 * (j - 5), 128 * (j - 4))
                    if j >= 2:
                        e.wait_ge(s["v_out"], at(l, "v_out", j - 1))
                    mm(bank(4 + j % 2)[0:src.shape[-1], :], src, W("uv", 0, 512)).then_inc(s["v_mm"], 1)
                e.wait_ge(s["cq_n"], at(l, "cq_n"))
                e.wait_ge(s["v_out"], at(l, "v_out", 7))

                units = [(h, b) for h in range(HEADS) for b in range(5)]

                def project(h):
                    if h:
                        e.wait_ge(s["k_out"], at(l, "k_out", h))
                    for k in range(2):
                        halves(Q(0)[0:QKD, :], W("uq", (k * HEADS + h) * QKD, (k * HEADS + h + 1) * QKD),
                               cq[:, k, :], k == 0, k == 1)
                    for k in range(2):
                        last = halves(Q(1)[rope, :], W("uqs", (k * HEADS + h) * ROPE, (k * HEADS + h + 1) * ROPE),
                                      cq[:, k, :], k == 0, k == 1)
                    last.then_inc(s["q_mm"], 1)
                    e.wait_ge(s["q_out"], at(l, "q_out", 2 * h + 1))
                    halves(Q(0)[0:64, :], W("uk", 64 * h, 64 * h + 64), ckv)
                    mm(bank(2, 0, PAST)[0:64, :], W("uk", 64 * h, 64 * h + 64),
                       W("ckv", 0, PAST)).then_inc(s["k_mm"], 1)

                def score(u):
                    h, b = units[u]
                    if b == 0:
                        e.wait_ge(s["q_out"], at(l, "q_out", 2 * h + 2))
                        e.wait_ge(s["k_out"], at(l, "k_out", h + 1))
                    if u >= 2:
                        e.wait_ge(s["a_exp"], at(l, "a_exp", u - 1))
                    o = bank(4 + u % 2)
                    if b < 4:
                        nk = 128 * b + 128
                        mm(o[:, 0:nk], aq[0:QKD, h % 2, 128 * b:128 * b + 128], ak[0:QKD, h % 2, 0:nk], True, False)
                        mm(o[:, nk - 128:nk], C("maskq", 0, 128, slice(0, 1)), C("maskk", 0, 128, slice(0, 1)),
                           False, True).then_inc(s["a_score"], 1)
                    else:
                        mm(o[0:DEC, 0:KEYS - SEQ], aq[0:QKD, h % 2, SEQ:T],
                           ak[0:QKD, h % 2, SEQ:KEYS]).then_inc(s["a_score"], 1)

                def tail(u):
                    h, b = units[u]
                    e.wait_ge(s["a_norm"], at(l, "a_norm", u + 1))
                    if u:
                        e.wait_ge(s["a_T_out"], at(l, "a_T_out", u))
                    if b < 4:
                        for j in range(b + 1):
                            last = e.transpose(bank(6, 128 * j, 128 * j + 128),
                                               aP[:, u % 2, 128 * j:128 * j + 128], ident)
                    else:
                        e.transpose(bank(6, 0, DEC)[0:DEC, :], aP[0:DEC, u % 2, 0:DEC], ident[0:DEC, 0:DEC])
                        for j in range(2):
                            last = e.transpose(bank(6, 128 * j + 128, 128 * j + 128 + DEC),
                                               aP[0:DEC, u % 2, DEC + 128 * j:DEC + 128 * j + 128],
                                               ident[0:DEC, 0:DEC])
                    last.then_inc(s["a_T"], 1)

                def pv(u):
                    h, b = units[u]
                    e.wait_ge(s["a_T_out"], at(l, "a_T_out", u + 1))
                    if u >= 1:
                        e.wait_ge(s["a_o"], at(l, "a_o", u))
                    rows = rows_of[h % 2]
                    if b < 4:
                        o = bank(7, 0, 128)[rows, :]
                        for j in range(b + 1):
                            last = mm(o, av[:, j, 64 * h:64 * h + 64], aPT[:, u % 2, 128 * j:128 * j + 128],
                                      j == 0, j == b)
                    else:
                        o = bank(7, 0, DEC)[rows, :]
                        mm(o, av[0:DEC, 4, 64 * h:64 * h + 64], aPT[0:DEC, u % 2, 0:DEC], True, False)
                        for j in range(2):
                            last = mm(o, av[:, 5 + j, 64 * h:64 * h + 64],
                                      aPT[:, u % 2, 128 * j + 128:128 * j + 128 + DEC], False, j == 1)
                    last.then_inc(s["a_pv"], 1)

                project(0)
                for u in range(len(units) + 2):
                    if u < len(units):
                        if units[u][1] == 2 and units[u][0] + 1 < HEADS:
                            project(units[u][0] + 1)
                        score(u)
                    if u >= 2:
                        pv(u - 2)
                    if 1 <= u <= len(units):
                        tail(u - 1)

                e.wait_ge(s["a_o"], at(l, "a_o", 40))
                dense(l, "out", lambda k: hT[:, k, :])
                e.wait_ge(s["memn"], at(l, "memn"))
                dense(l, "mk", None)
                dense(l, "mv", None)
                rms(2 + 3 * l, sqbig)
                e.wait_ge(s["h_ready"], at(l, "h_ready", 16))
                dense(l, "mq", lambda k: hT[:, k, :])
                wait_evac(e, l, "mv", 7)
                wait_evac(e, l, "mq", 7)
                e.wait_ge(mem_ld, 32 * (l + 1))

                munits = [(h, b) for h in range(MHEADS) for b in range(5)]

                def mscore(u):
                    h, b = munits[u]
                    if u >= 2:
                        e.wait_ge(s["m_exp"], at(l, "m_exp", u - 1))
                    n = 128 if b < 4 else DEC
                    keys = mkp if b < 4 else mks
                    for j in range(2):
                        last = mm(bank(4 + u % 2, 0, MEM)[0:n, :], mq[:, 2 * h + j, 128 * b:128 * b + n],
                                  keys[:, 2 * h + j, :], j == 0, j == 1)
                    last.then_inc(s["m_score"], 1)

                def mtail(u):
                    h, b = munits[u]
                    n = 128 if b < 4 else DEC
                    e.wait_ge(s["m_norm"], at(l, "m_norm", u + 1))
                    if u:
                        e.wait_ge(s["m_T_out"], at(l, "m_T_out", u))
                    for j in range(2):
                        last = e.transpose(bank(6, 128 * j, 128 * j + n), mP[0:n, u % 2, 128 * j:128 * j + 128],
                                           ident[0:n, 0:n])
                    last.then_inc(s["m_T"], 1)

                def mpv(h):
                    e.wait_ge(s["m_T_out"], at(l, "m_T_out", 5 * h + 5))
                    for i in range(2):
                        if h:
                            e.wait_ge(s["m_o"], at(l, "m_o", 4 * (h - 1) + 2 * i + 2))
                        for k, (va, a, b) in enumerate(((mvp, 0, SEQ), (mvs, SEQ, T))):
                            for j in range(2):
                                last = mm(bank(2 * k + i, 0, b - a),
                                          va[:, j, 256 * h + 128 * i:256 * h + 128 * i + 128],
                                          mPT[:, h % 2, j, a:b], j == 0, j == 1)
                            last.then_inc(s["m_pv"], 1)

                for u in range(len(munits) + 2):
                    if u < len(munits):
                        mscore(u)
                    if 1 <= u <= len(munits):
                        mtail(u - 1)
                    if u >= 2 and (u - 2) % 5 == 4:
                        mpv((u - 2) // 5)
                e.wait_ge(s["m_o"], at(l, "m_o", 16))
                dense(l, "mo", lambda k: hT[:, k, :])
                rms(3 + 3 * l, sqbig)
                e.wait_ge(s["h_ready"], at(l, "h_ready", 24))
                dense(l, "f1", lambda k: hT[:, k, :])
                e.wait_ge(s["hid_sq"], at(l, "hid_sq", 32))
                dense(l, "f2", lambda k: hid[:, k, :])
            rms(1 + 3 * DEPTH, hT)

        @block.scalar
        def _(e):
            steps = 0

            def act(out, in_, f, **kw):
                return e.activation(out, in_, f, **kw)

            def link(ins):
                nonlocal steps
                steps += 1
                ins.then_inc(astep, 1)
                e.wait_ge(astep, steps)

            def squares(dst, src, n=T, l=None, st=None):
                for k in range(8):
                    if st:
                        wait_evac(e, l, st, k)
                    act(dst[:, k, 0:n], src[:, k, 0:n], ACT.Square).then_inc(s["sq_ready"], 1)

            def rstd(r, n=T):
                e.wait_ge(s["rms_sum"], r + 1)
                link(act(rs[:, 0:n], Q(2) if n == T else bank(4, 0, n), ACT.Ln, scale=1.0 / D, bias=K(C_EPS)))
                act(rs[:, 0:n], rs[:, 0:n], ACT.Exp, scale=-0.5).then_inc(s["rms_rstd"], 1)

            e.wait_ge(setup_ld, 64)
            e.wait_ge(setup_abs, 1)
            act(stat[:, 0:4], stat[:, 4:8], ACT.Exp, scale=-1.0).then_inc(setup_exp, 1)
            squares(hT, memT, MEM)
            rstd(0, MEM)
            e.wait_ge(setup_vec, 1)
            for l in range(DEPTH):
                if l == 0:
                    e.wait_ge(s["h_ready"], 8)
                    squares(hT, xT)
                else:
                    squares(hT, xT, l=l - 1, st="f2")
                rstd(1 + 3 * l)

                for t in range(2):
                    e.wait_ge(s["rg_z"], at(l, "rg_z", t + 1))
                    act(ra[:, t, :], Q(t, XCW), ACT.Tanh, scale=0.5, bias=derv[:, l, t:t + 1])
                for t in range(2):
                    e.wait_ge(s["rg_z"], at(l, "rg_z", t + 3))
                    last = act(rix[:, t, :], Q(2 + t, XCW), ACT.Tanh, scale=0.5, bias=derv[:, l, 2 + t:3 + t])
                last.then_inc(s["rg_gates"], 1)
                e.wait_ge(s["rg_gates"], at(l, "rg_gates"))
                for t in range(2):
                    last = act(ru[:, t, :], ra[:, t, :], ACT.Tanh, scale=derv[:, l, 8 + t:9 + t],
                               bias=derv[:, l, 8 + t:9 + t])
                link(last)
                for t in range(2):
                    act(ra[:, t, :], ra[:, t, :], ACT.Exp, scale=derv[:, l, 10 + t:11 + t],
                        bias=derv[:, l, 10 + t:11 + t])
                e.wait_ge(s["low_ready"], at(l, "low_ready"))
                act(xs[0:32, 6, 0:T], xs[0:32, 6, 0:T], ACT.Tanh)
                act(xs[64:128, 6, 0:T], xs[64:128, 6, 0:T], ACT.Tanh, scale=0.5).then_inc(s["low_tanh"], 1)
                e.wait_ge(s["rg_gelu_in"], at(l, "rg_gelu_in"))
                act(gx, gx, ACT.Tanh, scale=GELU_C).then_inc(s["rg_gelu"], 1)
                for t in range(4):
                    e.wait_ge(s["low_z"], at(l, "low_z", t + 1))
                    act((ell if t < 2 else bneg)[:, t % 2, 0:T], Q(t), ACT.Tanh, scale=0.5,
                        bias=derv[:, l, 4 + t:5 + t]).then_inc(s["low_gate"], 1)
                e.wait_ge(s["kk_raw"], at(l, "kk_raw"))
                act(e1, kk[:, :, 0:T], ACT.Square).then_inc(s["kk_sq"], 1)
                e.wait_ge(s["rg_ix"], at(l, "rg_ix"))
                act(xc, ru, ACT.Ln, bias=K(C_ONE))
                act(rln, ru, ACT.Ln, scale=2.0, bias=K(C_TINY)).then_inc(s["rg_ln"], 1)
                for t in range(2):
                    e.wait_ge(s["kk_sum"], at(l, "kk_sum", t + 1))
                    last = act(e1[:, t, :], Q(t), ACT.Ln, bias=K(C_L2))
                link(last)
                act(e1, e1, ACT.Exp, scale=-0.5).then_inc(s["kk_rstd"], 1)
                e.wait_ge(s["rg_q"], at(l, "rg_q"))
                act(ru, ru, ACT.Exp, scale=0.5).then_inc(s["rg_sq"], 1)

                e.wait_ge(s["frames_zeroed"], at(l, "frames_zeroed"))
                for g in range(NG):
                    e.wait_ge(s["decay_cum"], at(l, "decay_cum", g + 1))
                    act(en1, dm, ACT.Exp, scale=-1.0)
                    act(ep, Lc, ACT.Exp)
                    act(en, Lc, ACT.Exp, scale=-1.0)
                    act(ee, le, ACT.Exp)
                    act(stat[:, 8:12], Lc.rearrange("p a (c n) -> p (a c) n", c=2)[:, :, CH - 1], ACT.Exp,
                        scale=-1.0).then_inc(s["decay_exp"], 1)
                    e.wait_ge(s["tok_T"], at(l, "tok_T", g + 1))
                    for t in range(2):
                        act(Vm[:, t, :].rearrange("p (a b) -> p a b", a=3)[:, 0:3:2, :],
                            pair(bank(0, 128 * t, 128 * t + 128)), ACT.Copy)
                        act(Rt[:, 2 * t:2 * t + 2, 0:64], pair(bank(0, 256 + 128 * t, 384 + 128 * t)), ACT.Copy)
                    for c in range(2):
                        act(BE[rows_of[c], :, c, :], pair(bank(1, 0, 256))[rows_of[c]], ACT.Copy)
                        last = act(KE[rows_of[c], :, c, :], pair(bank(1, 256, 512))[rows_of[c]], ACT.Copy)
                    last.then_inc(s["tok_out"], 1)
                    e.wait_ge(s["mv"], at(l, "mv", g + 1))
                    act(Rt[:, :, 64:128], pair(bank(7, 0, 256), 4), ACT.Copy).then_inc(s["mv_out"], 1)
                    e.wait_ge(s["xr"], at(l, "xr", g + 1))
                    for t in range(2):
                        o = pair(bank(3, 256 * t, 256 * t + 256))
                        act(Wm[:, t, :].rearrange("p (a b) -> p a b", a=3)[:, 0:3:2, :], o[:, :, 0:64], ACT.Copy)
                        last = act(Ym[:, t, :].rearrange("p (a b) -> p a b", a=3)[:, 0:3:2, :], o[:, :, 64:128],
                                   ACT.Copy)
                    last.then_inc(s["xr_out"], 1)

                e.wait_ge(s["gn_mean"], at(l, "gn_mean"))
                act(ell[:, :, 0:T], yrw[:, :, 0:T], ACT.Square).then_inc(s["gn_sq"], 1)
                for t in range(2):
                    e.wait_ge(s["gn_sum"], at(l, "gn_sum", 3 + t))
                    last = act(ell[:, t, 0:T], Q(t), ACT.Ln, scale=1.0 / 64, bias=K(C_GN))
                link(last)
                act(ell[:, :, 0:T], ell[:, :, 0:T], ACT.Exp, scale=-0.5).then_inc(s["gn_rstd"], 1)
                act(kk[:, :, 0:T], cq, ACT.Square)
                act(bneg[:, 0, 0:T], ckv, ACT.Square).then_inc(s["lat_sq"], 1)
                e.wait_ge(s["rw_y"], at(l, "rw_y"))
                for t, n in enumerate((256, 128)):
                    e.wait_ge(s["lat_sum"], at(l, "lat_sum", t + 1))
                    link(act(ell[:, t, 0:T], Q(t), ACT.Ln, scale=1.0 / n, bias=K(C_EPS)))
                    act(ell[:, t, 0:T], ell[:, t, 0:T], ACT.Exp, scale=-0.5).then_inc(s["lat_rstd"], 1)
                e.wait_ge(stored["wkv"], 32 * (l + 1))
                for j in range(7):
                    n = DEC if j == 4 else 128
                    e.wait_ge(s["v_mm"], at(l, "v_mm", j + 1))
                    act(av[0:n, j, :], bank(4 + j % 2)[0:n, :], ACT.Copy).then_inc(s["v_out"], 1)

                units = [(h, b) for h in range(HEADS) for b in range(5)]

                def keys_out(h):
                    if h >= 2:
                        e.wait_ge(s["a_score"], at(l, "a_score", 5 * (h - 1)))
                    e.wait_ge(s["k_mm"], at(l, "k_mm", h + 1))
                    act(ak[0:64, h % 2, 0:T], Q(0)[0:64, :], ACT.Copy)
                    act(ak[0:64, h % 2, T:KEYS], bank(2, 0, PAST)[0:64, :], ACT.Copy).then_inc(s["k_out"], 1)

                keys_out(0)
                for u in range(len(units) + 2):
                    if u < len(units):
                        h, b = units[u]
                        if b == 2 and h + 1 < HEADS:
                            keys_out(h + 1)
                        n, nk = (128, 128 * b + 128) if b < 4 else (DEC, KEYS - SEQ)
                        e.wait_ge(s["a_max"], at(l, "a_max", u + 1))
                        act(aP[0:n, u % 2, 0:nk], bank(4 + u % 2, 0, nk)[0:n, :], ACT.Exp, scale=MLA_SCALE,
                            bias=stat[0:n, 18 + u % 2:19 + u % 2],
                            accum_out=stat[0:n, 20 + u % 2:21 + u % 2]).then_inc(s["a_exp"], 1)
                    if 1 <= u <= len(units):
                        h, b = units[u - 1]
                        e.wait_ge(s["a_T"], at(l, "a_T", u))
                        if b < 4:
                            last = act(aPT[:, (u - 1) % 2, 0:128 * b + 128], bank(6, 0, 128 * b + 128), ACT.Copy)
                        else:
                            act(aPT[0:DEC, (u - 1) % 2, 0:DEC], bank(6, 0, DEC)[0:DEC, :], ACT.Copy)
                            last = act(pair(aPT[:, (u - 1) % 2, 128:384])[:, :, 0:DEC],
                                       pair(bank(6, 128, 384))[:, :, 0:DEC], ACT.Copy)
                        last.then_inc(s["a_T_out"], 1)
                    if u >= 2:
                        h, b = units[u - 2]
                        n = 128 if b < 4 else DEC
                        e.wait_ge(s["a_pv"], at(l, "a_pv", u - 1))
                        rows = rows_of[h % 2]
                        act(hT[rows, 4 + h // 2, 128 * b:128 * b + n], bank(7, 0, n)[rows, :],
                            ACT.Copy).then_inc(s["a_o"], 1)

                squares(sqbig, xT, l=l, st="out")
                for st, dst in (("mk", mkp), ("mv", mvp)):
                    for i in range(8):
                        t = TILE0[st] + i
                        e.wait_ge(pe_done, tile_done(l, st, i))
                        to = dst[:, i, :] if st == "mk" else dst[:, i % 2, 256 * (i // 2):256 * (i // 2) + 256]
                        act(to, bank(2 * (t % 2), 0, 256), ACT.Copy).then_inc(evac["act"], 1)
                rstd(2 + 3 * l)
                munits = [(h, b) for h in range(MHEADS) for b in range(5)]

                def out_tiles(h):
                    for i in range(2):
                        for k, (a, b) in enumerate(((0, SEQ), (SEQ, T))):
                            e.wait_ge(s["m_pv"], at(l, "m_pv", 4 * h + 2 * i + k + 1))
                            act(hT[:, 2 * h + i, a:b], bank(2 * k + i, 0, b - a), ACT.Copy).then_inc(s["m_o"], 1)

                for u in range(len(munits) + 2):
                    if u < len(munits):
                        h, b = munits[u]
                        n = 128 if b < 4 else DEC
                        e.wait_ge(s["m_max"], at(l, "m_max", u + 1))
                        act(mP[0:n, u % 2, :], bank(4 + u % 2, 0, MEM)[0:n, :], ACT.Exp, scale=MEM_SCALE,
                            bias=stat[0:n, 18 + u % 2:19 + u % 2],
                            accum_out=stat[0:n, 20 + u % 2:21 + u % 2]).then_inc(s["m_exp"], 1)
                    if 1 <= u <= len(munits):
                        h, b = munits[u - 1]
                        n = 128 if b < 4 else DEC
                        e.wait_ge(s["m_T"], at(l, "m_T", u))
                        act(mPT[:, h % 2, :, 128 * b:128 * b + n], pair(bank(6, 0, 256))[:, :, 0:n],
                            ACT.Copy).then_inc(s["m_T_out"], 1)
                    if u >= 2 and (u - 2) % 5 == 4:
                        out_tiles((u - 2) // 5)
                squares(sqbig, xT, l=l, st="mo")
                rstd(3 + 3 * l)
                for i in range(32):
                    e.wait_ge(pe_done, tile_done(l, "f1", i))
                    act(hid[:, i, :], Q((TILE0["f1"] + i) % 2), ACT.Relu).then_inc(evac["act"], 1)
            squares(hT, xT, l=DEPTH - 1, st="f2")
            rstd(1 + 3 * DEPTH)

        @block.vector
        def _(e):
            steps = 0

            def link(ins):
                nonlocal steps
                steps += 1
                ins.then_inc(vstep, 1)
                e.wait_ge(vstep, steps)

            tt, stt, ts = e.tensor_tensor, e.scalar_tensor_tensor, e.tensor_scalar

            def normed(r, gain, dst, src=xT, n=T, own=False):
                e.wait_ge(s["rms_rstd"], r + 1)
                for k in range(8):
                    if gain is None:
                        ins = tt(dst[:, k, 0:n], src[:, k, 0:n], rs[:, 0:n], ALU.mult)
                    else:
                        ins = stt(dst[:, k, 0:n], src[:, k, 0:n], gain(k), rs[:, 0:n], ALU.mult, ALU.mult)
                    ins.then_inc(s["h_ready"], 1)

            def take_tile(l, st, i):
                t = TILE0[st] + i
                e.wait_ge(pe_done, tile_done(l, st, i))
                return Q(t % 2)

            def residual(l, st):
                for i in range(8):
                    ps = take_tile(l, st, i)
                    tt(xT[:, i, :], ps, xT[:, i, :], ALU.add).then_inc(evac["dve"], 1)

            for c, v in ((C_TINY, 1e-37), (C_EPS, EPS), (C_L2, L2_EPS), (C_GN, GN_EPS), (C_ONE, 1.0)):
                e.memset(K(c), v)
            e.wait_ge(setup_ld, 64)
            lam = vec[:, :, VEC["lam"]:VEC["lam"] + 2]
            four = lambda a: pair(stat[:, a:a + 4])
            stt(four(4), lam, -1.0, lam, ALU.mult, ALU.max).then_inc(setup_abs, 1)
            link(ts(four(24), lam, -1.0, 0.0, ALU.mult, ALU.max))
            e.wait_ge(setup_exp, 1)
            link(ts(four(28), four(0), 2.0, None, ALU.add))
            link(e.reciprocal(four(32), four(28)))
            link(tt(four(28), four(0), four(32), ALU.mult))
            link(tt(four(32), four(28), four(28), ALU.mult))
            link(ts(four(36), four(32), 1.0 / 15, None, ALU.mult))
            for k in (13, 11, 9, 7, 5, 3):
                link(stt(four(36), four(36), 1.0 / k, four(32), ALU.add, ALU.mult))
            link(stt(four(36), four(36), 1.0, four(28), ALU.add, ALU.mult))
            link(stt(four(36), four(36), 2.0, four(24), ALU.mult, ALU.add))
            ts(derv[:, :, 8:10], four(36), 4.0, None, ALU.mult)
            ts(derv[:, :, 10:12], four(36), -4.0, None, ALU.mult)
            ts(derv[:, :, 0:8], vec[:, :, VEC["rg_ba"]:VEC["rg_ba"] + 8], 0.5, None,
               ALU.mult).then_inc(setup_vec, 1)
            e.wait_ge(setup_vec, 1)
            normed(0, None, memT, memT, MEM)

            for l in range(DEPTH):
                normed(1 + 3 * l, lambda k: V(l, "g_mix", k), hT)

                if l:
                    e.wait_ge(stored["mem"], 32 * l)
                e.memset(raw[:, :, 0:1], 0.0)
                e.tensor_copy(raw[:, :, SEQ + 1], vec[:, l, VEC["shift"]:VEC["shift"] + 7])
                e.memset(rg[:, :, 0:3], 0.0)
                link(e.tensor_copy(rg[:, :, 3 + SEQ:6 + SEQ], pair(vec[:, l, VEC["conv_s"]:VEC["conv_s"] + 6])))
                for i in range(16):
                    ps = take_tile(l, "in", i)
                    if i < RWT:
                        e.tensor_copy(raw[:, i, 1:1 + SEQ], ps[:, 0:SEQ])
                        e.tensor_copy(raw[:, i, 2 + SEQ:RWW], ps[:, SEQ:T]).then_inc(evac["dve"], 1)
                        wait_evac(e, l, "in", i)
                        tt(xs[:, i, 0:SEQ], raw[:, i, 0:SEQ], raw[:, i, 1:1 + SEQ], ALU.subtract)
                        link(tt(xs[:, i, SEQ:T], raw[:, i, 1 + SEQ:RWW - 1], raw[:, i, 2 + SEQ:RWW], ALU.subtract))
                        stt(xs[:, i, 0:SEQ], xs[:, i, 0:SEQ], V(l, "mu", i), raw[:, i, 1:1 + SEQ], ALU.mult, ALU.add)
                        ins = stt(xs[:, i, SEQ:T], xs[:, i, SEQ:T], V(l, "mu", i), raw[:, i, 2 + SEQ:RWW],
                                  ALU.mult, ALU.add)
                        if i == 6:
                            ins.then_inc(s["low_ready"], 1)
                        else:
                            link(ins)
                        if i in (2, 3):
                            ins = ts(kk[:, i - 2, 0:T], xs[:, i, 0:T], V(l, "k_k", i - 2), None, ALU.mult)
                            if i == 3:
                                ins.then_inc(s["kk_raw"], 1)
                    elif i < 9:
                        e.tensor_copy(cq[:, i - 7, :], ps).then_inc(evac["dve"], 1)
                    elif i == 9:
                        e.tensor_copy(ckv, ps).then_inc(evac["dve"], 1)
                    elif i == 10:
                        tt(kr[rope, :], ps[rope, :], C("cos", 0, T, rope), ALU.mult).then_inc(evac["dve"], 1)
                    elif i == 11:
                        tt(rs[rope, :], ps[rope, :], C("sin", 0, T, rope), ALU.mult).then_inc(evac["dve"], 1)
                        wait_evac(e, l, "in", 11)
                        tt(kr[rope, :], kr[rope, :], rs[rope, :], ALU.add).then_inc(s["kr_ready"], 1)
                    elif i < 14:
                        t = i - 12
                        e.tensor_copy(rg[:, t, 3:3 + SEQ], ps[:, 0:SEQ])
                        e.tensor_copy(rg[:, t, 6 + SEQ:RGW], ps[:, SEQ:T]).then_inc(evac["dve"], 1)
                        wait_evac(e, l, "in", i)
                        link(ts(xc[:, t, :], rg[:, t, 0:XCW], V(l, "conv_w", t), V(l, "conv_b", t),
                                ALU.mult, ALU.add))
                        for j in range(1, CONV):
                            ins = stt(xc[:, t, :], rg[:, t, j:j + XCW], V(l, "conv_w", 2 * j + t), xc[:, t, :],
                                      ALU.mult, ALU.add)
                            if j < CONV - 1 or t == 0:
                                link(ins)
                        if t:
                            ins.then_inc(s["rg_conv"], 1)
                    else:
                        e.tensor_copy(gate[:, i - 14, :], ps).then_inc(evac["dve"], 1)
                wait_evac(e, l, "in", 15)

                link(tt(gx, gate, gate, ALU.mult))
                link(ts(gx, gx, 0.044715, 1.0, ALU.mult, ALU.add))
                tt(gx, gx, gate, ALU.mult).then_inc(s["rg_gelu_in"], 1)
                e.wait_ge(s["rg_gates"], at(l, "rg_gates"))
                stt(rix, rix, 1.0, xc, ALU.add, ALU.mult).then_inc(s["rg_ix"], 1)
                e.wait_ge(s["rg_gelu"], at(l, "rg_gelu"))
                link(stt(gate, gx, 1.0, gate, ALU.add, ALU.mult))

                e.wait_ge(s["low_gate"], at(l, "low_gate", 4))
                ts(ell[:, :, 0:T], ell[:, :, 0:T], 0.5 * EXP_HALF, 0.5 * EXP_HALF, ALU.mult, ALU.add)
                ts(xs[64:128, 6, 0:T], xs[64:128, 6, 0:T], 0.5, 0.5, ALU.mult, ALU.add)
                link(ts(bneg[:, :, 0:T], bneg[:, :, 0:T], 0.5, 0.5, ALU.mult, ALU.add))
                for t in range(2):
                    link(ts(e2[:, t, :], bneg[:, t, 0:T], -1.0, V(l, "k_a", t), ALU.add, ALU.mult))
                    link(stt(xs[:, 2 + t, 0:T], e2[:, t, :], 1.0, xs[:, 2 + t, 0:T], ALU.add, ALU.mult))
                    ins = stt(e2[:, t, :], xs[:, t, 0:T], V(l, "r_k", t), xs[:, 2 + t, 0:T], ALU.mult, ALU.mult)
                ins.then_inc(s["rk_ready"], 1)
                e.wait_ge(s["rg_ln"], at(l, "rg_ln"))
                tt(ru, rln, xc, ALU.subtract).then_inc(s["rg_q"], 1)
                e.wait_ge(s["kk_rstd"], at(l, "kk_rstd"))
                link(tt(kk[:, :, 0:T], kk[:, :, 0:T], e1, ALU.mult))
                link(stt(bneg[:, :, 0:T], kk[:, :, 0:T], -1.0, bneg[:, :, 0:T], ALU.mult, ALU.mult))
                e.wait_ge(s["rows_kept"], at(l, "rows_kept", 1))
                for t in range(2):
                    e.wait_ge(s["rk_sum"], at(l, "rk_sum", t + 1))
                    link(tt(bonus[:, t, :], Q(2 + t), xs[:, 4 + t, 0:T], ALU.mult))

                e.wait_ge(s["rg_sq"], at(l, "rg_sq"))
                link(stt(rix, ru, 0.5, rix, ALU.mult, ALU.mult))
                for t in range(2):
                    e.tensor_tensor_scan(rh[:, t, 0:SEQ], ra[:, t, 0:SEQ], rix[:, t, 0:SEQ], 0.0, ALU.mult, ALU.add)
                    ins = e.tensor_tensor_scan(rh[:, t, SEQ:T], ra[:, t, SEQ + 3:XCW], rix[:, t, SEQ + 3:XCW],
                                               V(l, "h0", t), ALU.mult, ALU.add)
                link(ins)
                stt(hT[:, 0:2, :], gate, 0.5, rh, ALU.mult, ALU.mult).then_inc(s["rg_done"], 1)

                e.wait_ge(s["frames_zeroed"], at(l, "frames_zeroed"))
                chunks = lambda m: m.rearrange("p a (c n) -> p (a c) n", c=2)
                for g in range(NG):
                    cols = slice(GRP * g, GRP * g + GRP)
                    for t in range(2):
                        ins = e.tensor_tensor_scan(Lc[:, t, :], C("reset", 0, GRP), ell[:, t, cols], 0.0,
                                                   ALU.mult, ALU.add)
                    link(ins)
                    tt(dm, Lc, ell[:, :, cols], ALU.subtract)
                    end = chunks(Lc)[:, :, CH - 1:CH].to_broadcast([128, 4, CH])
                    tt(chunks(le), chunks(Lc), end, ALU.subtract).then_inc(s["decay_cum"], 1)
                    e.wait_ge(s["decay_exp"], at(l, "decay_exp", g + 1))
                    tt(af, kk[:, :, cols], en1, ALU.mult)
                    tt(rf, xs[:, 0:2, cols], en, ALU.mult)
                    tt(bf, bneg[:, :, cols], ep, ALU.mult)
                    tt(kf, xs[:, 2:4, cols], ep, ALU.mult)
                    tt(be, bneg[:, :, cols], ee, ALU.mult)
                    tt(ke, xs[:, 2:4, cols], ee, ALU.mult).then_inc(s["factors"], 1)
                    e.wait_ge(s["factors"], at(l, "factors", g + 1))
                    for h in range(2):
                        e.tensor_copy(AR[rows_of[h], h:4:2, 0:128], af[rows_of[h]])
                        ins = e.tensor_copy(AR[rows_of[h], h:4:2, 128:256], rf[rows_of[h]])
                    ins.then_inc(s["masked"], 1)
                    e.wait_ge(s["scores"], at(l, "scores", g + 1))
                    mask2 = bc(C("mask2", 0, 256), 4)
                    tt(L, pair(bank(6), 4), bc(C("maskL", 0, 128), 4), ALU.mult)
                    tt(LG, pair(PS[:, 1024:2048], 4), mask2, ALU.mult)
                    tt(MG, pair(PS[:, 2048:3072], 4), mask2, ALU.mult).then_inc(s["scores_out"], 1)
                    e.wait_ge(s["scores_out"], at(l, "scores_out", g + 1))

                    def level(b):
                        return bc(C("lev", 128 * b, 128 * b + 128), 4)

                    LT = LG[:, :, 0:128]
                    tt(X, L, bc(C("lev1t", 0, 128), 4), ALU.mult)
                    link(tt(XT, LT, level(0), ALU.mult))
                    tt(X, X, bc(ident, 4), ALU.add)
                    tt(XT, XT, bc(ident, 4), ALU.add)
                    tt(TT, LT, level(1), ALU.mult).then_inc(s["lev_T"], 1)
                    for b in range(5):
                        n = 5 * g + b
                        e.wait_ge(s["lev_P"], at(l, "lev_P", n + 1))
                        e.tensor_copy(P, pair(bank(0), 4)).then_inc(s["lev_P_out"], 1)
                        if b < 4:
                            tt(TT, LT, level(b + 2), ALU.mult).then_inc(s["lev_T"], 1)
                        e.wait_ge(s["lev_X"], at(l, "lev_X", n + 1))
                        tt(X, X, pair(bank(1), 4), ALU.add)
                        tt(XT, XT, pair(bank(2), 4), ALU.add).then_inc(s["lev_X_out"], 1)
                        e.wait_ge(s["lev_X_out"], at(l, "lev_X_out", n + 1))
                    e.wait_ge(s["ab"], at(l, "ab", g + 1))
                    flat2 = lambda m: m.rearrange("p a c n -> p (a c) n")
                    link(tt(flat2(Abd), pair(bank(4), 4), bc(bones, 4), ALU.mult))
                    for i in range(4):
                        m = flat2(Abd)[:, i, :]
                        stt(m, ident, K(8 + i), m, ALU.mult, ALU.add)
                    tt(flat2(Bbd), pair(bank(5), 4), bc(bones, 4), ALU.mult)
                    tt(rp, pair(bank(6, 0, 256)), rf, ALU.add)
                    e.tensor_copy(yl, pair(bank(6, 256, 512))).then_inc(s["ab_out"], 1)
                    e.wait_ge(s["ab_out"], at(l, "ab_out", g + 1))
                    nc_ = 2 if g < NG - 1 else 1
                    for c in range(nc_):
                        n = 2 * g + c
                        e.wait_ge(s["state_mm"], at(l, "state_mm", n + 1))
                        tt(S[:, 1 - c, :, :], pair(bank(7, 0, 256)), Bbd[:, :, c, :], ALU.add)\
                            .then_inc(s["state_out"], 1)
                    tt(yrw[:, :, GRP * g:GRP * g + CH * nc_], pair(bank(0, 0, 256))[:, :, 0:CH * nc_],
                       yl[:, :, 0:CH * nc_], ALU.add).then_inc(s["y_out"], 1)

                for t in range(2):
                    e.wait_ge(s["gn_sum"], at(l, "gn_sum", t + 1))
                    ins = stt(yrw[:, t, 0:T], Q(t), -1.0 / 64, yrw[:, t, 0:T], ALU.mult, ALU.add)
                ins.then_inc(s["gn_mean"], 1)
                e.wait_ge(s["gn_rstd"], at(l, "gn_rstd"))
                link(tt(yrw[:, :, 0:T], yrw[:, :, 0:T], ell[:, :, 0:T], ALU.mult))
                for t in range(2):
                    ins = ts(yrw[:, t, 0:T], yrw[:, t, 0:T], V(l, "gn_w", t), V(l, "gn_b", t), ALU.mult, ALU.add)
                link(ins)
                link(tt(yrw[:, :, 0:T], yrw[:, :, 0:T], bonus, ALU.add))
                e.wait_ge(s["g_out"], at(l, "g_out"))
                for t in range(2):
                    ins = tt(hT[:, 2 + t, :], Q(2 + t), yrw[:, t, 0:T], ALU.mult)
                ins.then_inc(s["rw_y"], 1)

                e.wait_ge(stored["wkv"], 32 * (l + 1))
                for j in range(2):
                    e.tensor_copy(ak[rope, j, 0:T], kr[rope, :])
                    e.tensor_copy(ak[rope, j, T:KEYS], W("kr", 0, PAST, rope))
                e.wait_ge(s["lat_rstd"], at(l, "lat_rstd", 2))
                stt(ckv, ckv, V(l, "kv_norm"), ell[:, 1, 0:T], ALU.mult, ALU.mult).then_inc(s["ckv_n"], 1)
                for t in range(2):
                    ins = stt(cq[:, t, :], cq[:, t, :], V(l, "q_norm", t), ell[:, 0, 0:T], ALU.mult, ALU.mult)
                ins.then_inc(s["cq_n"], 1)

                units = [(h, b) for h in range(HEADS) for b in range(5)]

                def queries_out(h):
                    if h >= 2:
                        e.wait_ge(s["a_score"], at(l, "a_score", 5 * (h - 1)))
                    e.wait_ge(s["q_mm"], at(l, "q_mm", h + 1))
                    q = aq[:, h % 2, :]
                    e.tensor_copy(q[0:64, :], Q(0)[0:64, :])
                    tt(q[rope, :], Q(0)[rope, :], C("cos", 0, T, rope), ALU.mult)
                    tt(rs[rope, :], Q(1)[rope, :], C("sin", 0, T, rope), ALU.mult).then_inc(s["q_out"], 1)
                    e.wait_ge(s["q_out"], at(l, "q_out", 2 * h + 1))
                    tt(q[rope, :], q[rope, :], rs[rope, :], ALU.add).then_inc(s["q_out"], 1)
                    e.wait_ge(s["q_out"], at(l, "q_out", 2 * h + 2))

                def maximum(u, name, n, nk, scale):
                    e.wait_ge(s[name + "_score"], at(l, name + "_score", u + 1))
                    link(e.reduce_max(stat[0:n, 16 + u % 2:17 + u % 2], bank(4 + u % 2, 0, nk)[0:n, :], AX))
                    ts(stat[0:n, 18 + u % 2:19 + u % 2], stat[0:n, 16 + u % 2:17 + u % 2], -scale, None,
                       ALU.mult).then_inc(s[name + "_max"], 1)

                def normalise(u, name, p, n, nk):
                    e.wait_ge(s[name + "_exp"], at(l, name + "_exp", u + 1))
                    r = stat[0:n, 22 + u % 2:23 + u % 2]
                    link(e.reciprocal(r, stat[0:n, 20 + u % 2:21 + u % 2]))
                    m = p[0:n, u % 2, 0:nk]
                    ts(m, m, r, None, ALU.mult).then_inc(s[name + "_norm"], 1)

                def size(b):
                    return (128, 128 * b + 128) if b < 4 else (DEC, KEYS - SEQ)

                queries_out(0)
                for u in range(len(units) + 1):
                    if u < len(units):
                        h, b = units[u]
                        if b == 2 and h + 1 < HEADS:
                            queries_out(h + 1)
                        maximum(u, "a", *size(b), MLA_SCALE)
                    if u:
                        normalise(u - 1, "a", aP, *size(units[u - 1][1]))

                e.wait_ge(s["a_o"], at(l, "a_o", 40))
                e.wait_ge(stored["latent"], 32 * (l + 1))
                for k in range(8):
                    ins = ts(memn[:, k, :], memT[:, k, :], V(l, "g_memkv", k), None, ALU.mult)
                ins.then_inc(s["memn"], 1)
                residual(l, "out")
                normed(2 + 3 * l, lambda k: V(l, "g_mem", k), hT)
                for i in range(8):
                    ps = take_tile(l, "mq", i)
                    e.tensor_copy(mq[:, i, :], ps).then_inc(evac["dve"], 1)
                munits = [(h, b) for h in range(MHEADS) for b in range(5)]
                for u in range(len(munits) + 1):
                    if u < len(munits):
                        maximum(u, "m", 128 if munits[u][1] < 4 else DEC, MEM, MEM_SCALE)
                    if u:
                        normalise(u - 1, "m", mP, 128 if munits[u - 1][1] < 4 else DEC, MEM)
                residual(l, "mo")
                normed(3 + 3 * l, lambda k: V(l, "g_ffn", k), hT)
                for i in range(32):
                    wait_evac(e, l, "f1", i)
                    tt(hid[:, i, :], hid[:, i, :], hid[:, i, :], ALU.mult).then_inc(s["hid_sq"], 1)
                residual(l, "f2")
            normed(1 + 3 * DEPTH, lambda k: C("g_final", k, k + 1), hT)


_VECTORS = {"g_mix": "norm_mix", "g_mem": "norm_mem", "g_memkv": "norm_mem_kv", "g_ffn": "norm_ffn",
            "conv_w": "rg_conv_w", "conv_b": "rg_conv_b", "rg_ba": "rg_ba", "rg_bx": "rg_bx", "w0": "rw_w0",
            "a0": "rw_a0", "lam": "rg_lambda", "mu": "rw_mu", "k_k": "rw_k_k", "k_a": "rw_k_a", "r_k": "rw_r_k",
            "gn_w": "rw_gn_w", "gn_b": "rw_gn_b", "q_norm": "mla_q_norm", "kv_norm": "mla_kv_norm",
            "h0": "state_rg_h", "shift": "state_rw_shift"}


def _constants(norm_final):
    f = np.float32
    c = np.zeros((128, NCST), f)

    def put(name, a, rows=slice(0, 128)):
        c[rows, CST[name]:CST[name] + a.shape[1]] = a

    i = np.arange(128)
    row, col = i[:, None], i[None, :]
    same = row // CH == col // CH
    put("ident", np.eye(128, dtype=f))
    put("ones", np.ones((128, 128), f))
    put("bones", same.astype(f))
    put("mask2", np.concatenate([same & (row < col), same & (row <= col)], 1).astype(f))
    put("maskL", (same & (col < row)).astype(f))
    levels = []
    for b in range(6):
        n = 1 << b
        levels.append((row // (2 * n) == col // (2 * n)) & (row // n % 2 == 0) & (col // n % 2 == 1))
    put("lev", np.concatenate(levels, 1).astype(f))
    put("lev1t", levels[0].T.astype(f))
    half = ROPE // 2
    inv = f(10000.0) ** (-np.arange(half, dtype=f) / f(half))
    pos = np.concatenate([np.arange(SEQ), PAST + np.arange(DEC)]).astype(f)
    ang = inv[:, None] * pos[None, :]
    put("cos", np.concatenate([np.cos(ang)] * 2).astype(f), slice(64, 96))
    put("sin", np.concatenate([-np.sin(ang), np.sin(ang)]).astype(f), slice(64, 96))
    put("reset", np.broadcast_to((i % CH != 0).astype(f), (128, 128)))
    put("maskq", (i < CH).astype(f)[None, :], slice(0, 1))
    put("maskk", np.where(i >= CH, f(NEG), f(0))[None, :], slice(0, 1))
    put("g_final", np.asarray(norm_final).reshape(8, 128).T)
    return c


def kernel(**inputs):
    import concourse.bacc as bacc
    from concourse.bass_utils import run_bass_kernel_spmd

    a = {k: np.asarray(v) for k, v in inputs.items()}
    f = np.float32
    L = DEPTH

    def rows(m):
        return np.moveaxis(m.reshape((-1, 128) + m.shape[1:]), 0, 1)

    vec = np.zeros((128, L, NV), f)
    for name, src in _VECTORS.items():
        v = a[src].reshape(L, -1, 128)
        vec[:, :, VEC[name]:VEC[name] + v.shape[1]] = v.transpose(2, 0, 1)
    conv = a["state_rg_conv"].reshape(L, 3, 2, 128).transpose(3, 0, 2, 1).reshape(128, L, 6)
    vec[:, :, VEC["conv_s"]:VEC["conv_s"] + 6] = conv

    lw = np.zeros((L, 128, NLW), f)

    def put(name, at, m, r=slice(0, 128)):
        lw[:, r, LW[name] + at:LW[name] + at + m.shape[-1]] = m

    for name, src in (("wa", "rg_wa"), ("wx", "rg_wx")):
        for b in range(4):
            put(name, 64 * b, a[src][:, b], slice(64 * (b % 2), 64 * (b % 2) + 64))
    put("low", 0, a["rw_w2"], slice(0, 32))
    put("low", 0, a["rw_a2"], slice(32, 64))
    put("low", 0, a["rw_g2"], slice(64, 128))
    uq = a["mla_w_uq"].reshape(L, 2, 128, HEADS, QKD).transpose(0, 2, 1, 3, 4)
    put("uq", 0, uq.reshape(L, 128, -1))
    half = ROPE // 2
    uqs = np.concatenate([uq[..., NOPE + half:], uq[..., NOPE:NOPE + half]], -1)
    put("uqs", 0, uqs.reshape(L, 128, -1))
    put("uk", 0, a["mla_w_uk"].reshape(L, 128, -1))
    put("uv", 0, a["mla_w_uv"].reshape(L, 128, -1))
    put("ckv", 0, a["cache_mla_ckv"][:, 0].transpose(0, 2, 1))
    put("kr", 0, a["cache_mla_krope"][:, 0].transpose(0, 2, 1), slice(64, 96))
    st = a["state_rw_wkv"][:, 0].transpose(0, 1, 3, 2)
    for h in range(4):
        put("S0", 128 * (h // 2) + 64 * (h % 2), st[:, h], slice(64 * (h % 2), 64 * (h % 2) + 64))

    wall = np.zeros((L, NCH, 128, 8, 256), f)
    w_in = a["w_in"]
    rw0, mla0 = 512, 512 + 896
    order = [(rw0 + 128 * i, 128) for i in range(7)] + [(mla0, 128), (mla0 + 128, 128), (mla0 + 256, 128),
             (mla0 + 384, ROPE), (None, ROPE), (0, 128), (128, 128), (256, 128), (384, 128)]
    swapped = np.concatenate([w_in[:, :, mla0 + 384 + half:mla0 + 416], w_in[:, :, mla0 + 384:mla0 + 384 + half]], 2)
    mats = {"out": a["w_out"], "mk": a["mem_w_k"].reshape(L, D, D), "mv": a["mem_w_v"].reshape(L, D, D),
            "mq": a["mem_w_q"].reshape(L, D, D), "mo": a["mem_w_o"].reshape(L, D, D), "f1": a["ffn_w1"],
            "f2": a["ffn_w2"]}
    for ci, (stg, c) in enumerate(CHUNKS):
        if stg == "in":
            for k2 in range(2):
                at, w = order[2 * c + k2]
                m = swapped if at is None else w_in[:, :, at:at + w]
                wall[:, ci, :, :, 128 * k2:128 * k2 + w] = m.reshape(L, 8, 128, w).transpose(0, 2, 1, 3)
        else:
            k, n = (c % 4, c // 4) if stg == "f2" else (0, c)
            m = mats[stg][:, D * k:D * k + D, 256 * n:256 * n + 256]
            wall[:, ci] = m.reshape(L, 8, 128, 256).transpose(0, 2, 1, 3)
    wall = wall.reshape(L, NCH, 128, 2048)

    x = np.concatenate([a["x_prompt"][0], a["x_sample"][0]], 0)
    arrays = {
        "wall": wall, "lw_in": lw, "vec_in": vec, "cst_in": _constants(a["norm_final"]),
        "x_in": rows(np.ascontiguousarray(x.T)), "mem_in": rows(np.ascontiguousarray(a["mem_prompt"][0].T)),
        "mks_in": a["cache_mem_k"][:, 0].reshape(L, MEM, 8, 128).transpose(0, 3, 2, 1),
        "mvs_in": a["cache_mem_v"][:, 0].reshape(L, 2, 128, D).transpose(0, 2, 1, 3),
    }
    arrays = {k: np.ascontiguousarray(v) for k, v in arrays.items()}
    nc = bacc.Bacc("TRN2", target_bir_lowering=False, num_devices=1)
    F32 = mybir.dt.float32
    ins = [nc.dram_tensor(k, v.shape, F32, kind="ExternalInput").ap() for k, v in arrays.items()]
    outs = {k: nc.dram_tensor(k, shape, F32, kind="ExternalOutput").ap() for k, shape in OUTS}
    build(nc, *ins, outs)
    r = run_bass_kernel_spmd(nc, [arrays], core_ids=[0]).results[0]
    o = {k: np.asarray(r[k]).reshape(shape) for k, shape in OUTS}

    y = o["y_out"].transpose(2, 1, 0).reshape(T, D)
    last = o["last_out"]
    shift = last[:, :, 0:14].reshape(L, 128, RWT, 2).transpose(3, 0, 2, 1).reshape(2, L, 1, RWT * 128)
    conv = last[:, :, 14:26].reshape(L, 128, 2, 2, 3).transpose(3, 0, 4, 2, 1).reshape(2, L, 1, 3, 256)
    h = last[:, :, 26:30].reshape(L, 128, 2, 2).transpose(3, 0, 2, 1).reshape(2, L, 1, 256)
    wkv = np.zeros((2, L, 1, 4, 64, 64), f)
    for i in range(4):
        r_ = slice(64 * (i % 2), 64 * (i % 2) + 64)
        wkv[:, :, 0, i] = o["wkv_out"][:, r_, :, i // 2, r_].transpose(2, 0, 3, 1)
    ckv = o["ckv_out"].transpose(0, 2, 1)[:, None]
    kr = o["kr_out"].transpose(0, 2, 1)[:, None]
    mk = o["memk_out"].transpose(0, 3, 2, 1).reshape(L, 1, MEM, 4, 256)
    mv = o["memv_out"].transpose(0, 2, 1, 3).reshape(L, 1, MEM, 4, 256)
    got = (y[None, :SEQ], y[None, SEQ:], conv[0], h[0], shift[0], wkv[0], ckv[:, :, :SEQ], kr[:, :, :SEQ], mk, mv,
           conv[1], h[1], shift[1], wkv[1], ckv[:, :, SEQ:], kr[:, :, SEQ:])
    return tuple(np.ascontiguousarray(g) for g in got)
```

```python
import numpy as np
import concourse.bass as bass
from concourse import mybir
from contextlib import ExitStack

DEPTH, SEQ, DEC, PAST, D = 2, 512, 32, 256, 1024
T = SEQ + DEC
HALF = T // 2
KT = D // 128
MEM, MHEADS = 256, 4
RG_COLS, CONV = 2, 4
RGW = (CONV - 1) + SEQ + (CONV - 1) + DEC
XCW = RGW - (CONV - 1)
XH = XCW // 2 + 1
RWT = 7
RWW = 1 + SEQ + 1 + DEC
CH = 64
GRP = 128
NG = SEQ // GRP + 1
FR = NG * GRP
HEADS, NOPE, ROPE = 8, 64, 32
QKD = NOPE + ROPE
KEYS = T + PAST
MLA_SCALE = float(QKD) ** -0.5
MEM_SCALE = 256.0 ** -0.5
FF = 32
EPS, GN_EPS, L2_EPS = 1e-6, 64e-5, 1e-12
EXP_HALF = float(np.exp(-0.5))
GELU_C = float(np.sqrt(2.0 / np.pi))
NEG = -1e30

VEC = {}
_n = 0
for _name, _w in (("g_mix", 8), ("g_mem", 8), ("g_memkv", 8), ("g_ffn", 8), ("conv_w", 8), ("conv_b", 2),
                  ("rg_ba", 2), ("rg_bx", 2), ("w0", 2), ("a0", 2), ("lam", 2), ("mu", 7), ("k_k", 2), ("k_a", 2),
                  ("r_k", 2), ("gn_w", 2), ("gn_b", 2), ("q_norm", 2), ("kv_norm", 1), ("h0", 2),
                  ("shift", 7), ("conv_s", 6)):
    VEC[_name] = _n
    _n += _w
NV = _n

LW = {}
_n = 0
for _name, _w in (("wa", 256), ("wx", 256), ("low", 256), ("uq", 2 * HEADS * QKD), ("uqs", 2 * HEADS * ROPE),
                  ("uk", HEADS * NOPE), ("uv", HEADS * 64), ("ckv", PAST), ("kr", PAST), ("S0", 256)):
    LW[_name] = _n
    _n += _w
NLW = _n

CST = {}
_n = 0
for _name, _w in (("ident", 128), ("ones", 128), ("bones", 128), ("mask2", 256), ("maskL", 128), ("lev", 6 * 128),
                  ("lev1t", 128), ("cos", T), ("sin", T), ("reset", GRP), ("maskq", 128), ("maskk", 128), ("g_final", 8)):
    CST[_name] = _n
    _n += _w
NCST = _n

STREAM = [(st, i) for st, n in (("in", 16), ("out", 8), ("mk", 8), ("mv", 8), ("mq", 8), ("mo", 8)) for i in range(n)]
for _g in (0, 1, 2, 3, 4):
    if _g < 4:
        STREAM += [("f1", 8 * _g + i) for i in range(8)]
    if _g > 0:
        STREAM += [("f2", 8 * (_g - 1) + i) for i in range(8)]
NT = len(STREAM)
TILE = {t: i for i, t in enumerate(STREAM)}
RING = 3
SPLIT = 3
EVAC_ENGINE = {st: "act" if st in ("mk", "mv") else "dve" for st, _ in STREAM}
EVAC_PER_LAYER = {e: sum(EVAC_ENGINE[t[0]] == e for t in STREAM) for e in ("act", "dve")}
RUNS = [(0, 16), (16, NT + 16), (NT + 16, 2 * NT)]


def evac_value(layer, tile):
    eng = EVAC_ENGINE[STREAM[tile][0]]
    return eng, layer * EVAC_PER_LAYER[eng] + sum(EVAC_ENGINE[t[0]] == eng for t in STREAM[:tile + 1])


OUTS = [("y_out", (128, 8, T)), ("last_out", (DEPTH, 128, 30)), ("wkv_out", (DEPTH, 128, 2, 2, 128)),
        ("ckv_out", (DEPTH, 128, T)), ("kr_out", (DEPTH, ROPE, T)),
        ("memk_out", (DEPTH, 128, 8, MEM)), ("memv_out", (DEPTH, 128, 2, D))]

OUT_TILES_SPLIT = (14, 24)
MIXED_AT = (6, 8, 9, 10, 12, 22, 32, 41)

NSTATE = 2 * NG - 1
PER_LAYER = {
    "sq_ready": 24, "sq_added": 21, "rms_sum": 3, "rms_rstd": 3, "h_hi": 40, "h_ready": 40,
    "frames_zeroed": 1, "rows_kept": 2,
    "rg_conv": 1, "rg_z": 4, "rg_gates": 1, "rg_gelu_in": 1, "rg_gelu": 1, "rg_ix": 1, "rg_ln": 1, "rg_q": 1,
    "rg_sq": 1, "rg_done": 1,
    "low_ready": 1, "low_tanh": 1, "low_z": 4, "low_gate": 4, "kk_raw": 1, "kk_sq": 1, "kk_sum": 2,
    "kk_rstd": 1, "rk_ready": 1, "rk_sum": 2,
    "decay_cum": NG, "decay_exp": NG, "factors": NG, "masked": NG, "tok_T": NG, "tok_out": NG, "scores": NG,
    "scores_out": NG, "mv": NG, "mv_out": NG, "lev_T": 5 * NG, "lev_P": 5 * NG, "lev_P_out": 5 * NG,
    "lev_X": 5 * NG, "lev_X_out": 5 * NG, "xr": NG, "xr_out": NG, "ab": NG, "ab_out": NG,
    "state_mm": NSTATE, "state_out": NSTATE, "y_out": NG,
    "gn_sum": 4, "gn_mean": 1, "gn_sq": 1, "gn_rstd": 1, "g_out": 1, "rw_y": 1,
    "lat_sq": 1, "lat_sum": 2, "lat_rstd": 2, "cq_n": 1, "ckv_n": 1, "kr_ready": 1,
    "v_mm": 7, "v_out": 7, "q_mm": HEADS, "q_out": 2 * HEADS, "k_mm": HEADS, "k_out": HEADS,
    "a_score": 40, "a_max": 40, "a_exp": 40, "a_norm": 40, "a_T": 40, "a_T_out": 40, "a_pv": 40, "a_o": 40,
    "m_score": 20, "m_max": 20, "m_exp": 20, "m_norm": 20, "m_T": 20, "m_T_out": 20, "m_pv": 16, "m_o": 16,
    "mem_scaled": 1, "mem_hi": 1, "memn": 1, "hid_sq": 32, "hid_hi": 32, "hid_lo": 32,
}


def build(nc, wall, lw_d, vec_d, cst_d, x_d, mem_d, mks_d, mvs_d, outs):
    F32, F32R = mybir.dt.float32, mybir.dt.float32r
    ALU = mybir.AluOpType
    ACT = mybir.ActivationFunctionType
    AX = mybir.AxisListType.X
    ctx = ExitStack()
    with ctx:
        base = nc.sbuf_base + -nc.sbuf_base % 32

        def place(name, col, shape, dtype):
            return nc.alloc_sbuf_tensor_at(name, shape, dtype, offset=base + 4 * col)

        def sem(name):
            return ctx.enter_context(nc.semaphore(name))

        ARENA = 53200
        col = {}

        def carve(at, limit, **shapes):
            got = []
            for name, shape in shapes.items():
                col[name] = at
                got.append(place(name, at, (128,) + shape, F32)[(slice(None),) * (len(shape) + 1)])
                at += int(np.prod(shape))
                at += -at % 8
            assert at <= limit, (at, limit)
            col["end"] = at
            return got

        xT, hT, ring, lw, vec, derv, cst, rs, stat, last_rows, mrs = carve(
            0, ARENA, xT=(8, T), hT=(8, T), ring=(RING, 8, 128), lw=(NLW,), vec=(DEPTH, NV), derv=(DEPTH, 12),
            cst=(NCST,), rs=(T,), stat=(64,), last_rows=(30,), mrs=(MEM,))
        FIX = col["end"]
        hL = place("hL", col["hT"], [128, 8, T], F32R)
        hH = place("hH", FIX, [128, 8, T], F32R)
        wH = place("wH", FIX + 8 * T, [128, SPLIT, 8, 128], F32R)
        wL = place("wL", FIX + 8 * T + SPLIT * 1024, [128, SPLIT, 8, 128], F32R)
        MIX = FIX + 8 * T + 2 * SPLIT * 1024
        xs, kk, cq, ckv, kr, rg, gate, raw, ell, bneg, aq, ak, aP, aPT = carve(
            MIX, ARENA, xs=(RWT, FR), kk=(2, FR), cq=(2, T), ckv=(T,), kr=(T,), rg=(2, RGW), gate=(2, T),
            raw=(RWT, RWW), ell=(2, FR), bneg=(2, FR), aq=(2, T), ak=(2, KEYS), aP=(3, 512), aPT=(2, 512))
        av, bonus = carve(col["rg"], col["ell"], av=(7, 512), bonus=(2, T))
        ra, ru, rln, rix, gx, rh = carve(FIX, MIX, ra=(2, XCW), ru=(2, XCW), rln=(2, XCW), rix=(2, XCW),
                                         gx=(2, T), rh=(2, T))
        xc, = carve(col["ak"], ARENA, xc=(2, XCW))
        en1, en, ep, ee, bf, be, AR, LG, MG, X, XT, P, TT, BE, KE, S, Rt, Vm, Wm, Ym, yl = carve(
            FIX, MIX, en1=(2, 128), en=(2, 128), ep=(2, 128), ee=(2, 128), bf=(2, 128), be=(2, 128),
            AR=(4, 256), LG=(4, 256), MG=(4, 256), X=(4, 128), XT=(4, 128), P=(4, 128), TT=(4, 128),
            BE=(2, 2, 128), KE=(2, 2, 128), S=(2, 2, 128), Rt=(4, 128), Vm=(2, 192), Wm=(2, 192), Ym=(2, 192),
            yl=(2, 128))
        af, rf, kf, ke, Lc, dm, le, rp = en1, en, ep, ee, en, en1, ee, bf
        Abd, Bbd = (m.rearrange("p (a c) n -> p a c n", a=2) for m in (TT, P))
        yrw = hT[:, 2:4, :]
        e1, e2 = hT[:, 4:6, :], hT[:, 6:8, :]
        mem32, = carve(MIX, ARENA, mem32=(8, MEM))
        msq, = carve(col["kk"], col["cq"], msq=(2, MEM))
        memL = place("memL", MIX, [128, 8, MEM], F32R)
        memH = place("memH", MIX + 8 * MEM, [128, 8, MEM], F32R)
        mq, mks, mvs, mkp, mvp, mP, mPT, sq = carve(
            MIX + 16 * MEM, ARENA, mq=(8, T), mks=(8, MEM), mvs=(2, D), mkp=(8, MEM), mvp=(2, D), mP=(3, 256),
            mPT=(2, 2, T), sq=(2, T))
        hid, = carve(MIX, col["sq"], hid=(2, 8, T))
        hidL = place("hidL", MIX, [128, 2, 8, T], F32R)
        hidH = place("hidH", MIX + 16 * T, [128, 2, 8, T], F32R)
        PS = ctx.enter_context(nc.psum_tensor("PS", [128, 8 * 512], F32))

        def C(name, a, b, rows=slice(0, 128)):
            return cst[rows, CST[name] + a:CST[name] + b]

        def V(l, name, i=0):
            return vec[:, l, VEC[name] + i:VEC[name] + i + 1]

        def W(name, a, b, rows=slice(0, 128)):
            return lw[rows, LW[name] + a:LW[name] + b]

        def bc(ap, n):
            return ap.unsqueeze(1).to_broadcast([128, n, ap.shape[-1]])

        def plain(ap):
            return ap.bitcast(F32)

        def pair(ap, n=2):
            return ap.rearrange("p (a b) -> p a b", a=n)

        ident, ones, bones = (C(n, 0, 128) for n in ("ident", "ones", "bones"))
        rows_of = [slice(0, 64), slice(64, 128)]
        rope = slice(64, 96)
        C_TINY, C_EPS, C_L2, C_GN, C_ONE = 59, 60, 61, 62, 63

        def K(i):
            return stat[:, i:i + 1]

        def Q(q, n=T):
            return PS[:, q * 1024 + 512 - (n + 1) // 2:q * 1024 + 512 - (n + 1) // 2 + n]

        def bank(i, a=0, b=512):
            return PS[:, i * 512 + a:i * 512 + b]

        w_load = [sem(f"w_load{i}") for i in range(RING)]
        pe_done = sem("pe_done")
        w_hi, w_lo = sem("w_hi"), sem("w_lo")
        evac = {"act": sem("evac_act"), "dve": sem("evac_dve")}
        vec_ld, cst_ld, x_ld = sem("vec_ld"), sem("cst_ld"), [sem("x_ld0"), sem("x_ld1")]
        lw_ld, mem_ld, tokens_ld = sem("lw_ld"), sem("mem_ld"), sem("tokens_ld")
        msq_ready, msq_added, mem_sum, mem_rstd = (sem(n) for n in ("msq_ready", "msq_added", "mem_sum", "mem_rstd"))
        stored = {n: sem("stored_" + n) for n in ("last", "wkv", "latent", "mem", "y")}
        y_ready = sem("y_ready")
        vstep, astep, setup_abs, setup_exp, setup_vec = (
            sem(n) for n in ("vstep", "astep", "setup_abs", "setup_exp", "setup_vec"))
        s = {n: sem(n) for n in PER_LAYER}
        before = dict(sq_ready=8, sq_added=7, rms_sum=1, rms_rstd=1)

        def at(l, name, i=1):
            return before.get(name, 0) + l * PER_LAYER[name] + i

        def tile_no(l, st, i=0):
            return l * NT + TILE[(st, i)]

        def wait_tile(e, l, st, i):
            e.wait_ge(pe_done, tile_no(l, st, i) + 1)

        def wait_evac(e, l, st, i):
            eng, v = evac_value(l, TILE[(st, i)])
            e.wait_ge(evac[eng], v)

        def split_now(n):
            return any(a + 2 <= n < b for a, b in RUNS)

        block = ctx.enter_context(nc.Block())

        @block.sync
        def _(e):
            def load(n):
                if n >= RING:
                    e.wait_ge(w_lo, n - RING + 1)
                e.dma_start(ring[:, n % RING, :, :].rearrange("p a b -> p (a b)"),
                            wall[n // NT, n % NT]).then_inc(w_load[n % RING], 16)

            e.dma_start(vec[:, :, :], vec_d).then_inc(vec_ld, 16)
            e.dma_start(xT[:, 0:4, :], x_d[:, 0:4, :]).then_inc(x_ld[0], 16)
            load(0)
            e.dma_start(xT[:, 4:8, :], x_d[:, 4:8, :]).then_inc(x_ld[1], 16)
            load(1)
            e.dma_start(cst[:, :], cst_d).then_inc(cst_ld, 16)
            for n in range(2, DEPTH * NT):
                load(n)
            for k in range(8):
                e.wait_ge(y_ready, k + 1)
                e.dma_start(outs["y_out"][:, k, :], hT[:, k, :]).then_inc(stored["y"], 16)
            e.wait_ge(stored["y"], 16 * 8)

        @block.gpsimd
        def _(e):
            e.dma_start(lw[:, :], lw_d[0]).then_inc(lw_ld, 16)

            def put(kind, out, src):
                e.dma_start(out, src).then_inc(stored[kind], 16)

            def add_squares(r):
                for k in range(1, 8):
                    e.wait_ge(s["sq_ready"], 8 * r + k + 1)
                    if k > 1:
                        e.wait_ge(s["sq_added"], 7 * r + k - 1)
                    e.tensor_tensor(sq[:, 0, :], sq[:, 0, :], sq[:, 1, :], ALU.add).then_inc(s["sq_added"], 1)

            add_squares(0)
            for l in range(DEPTH):
                if l:
                    e.wait_ge(pe_done, l * NT)
                    e.wait_ge(stored["last"], 16 * l)
                e.memset(xs[:, :, T:FR], 0.0)
                e.memset(ell[:, :, T:FR], 0.0)
                e.memset(bneg[:, :, T:FR], 0.0)
                e.memset(kk[:, :, T:FR], 0.0)
                wait_evac(e, l, "in", 15)
                e.tensor_copy(pair(last_rows[:, 0:14], 7), raw[:, :, SEQ:RWW:RWW - 1 - SEQ])\
                    .then_inc(s["rows_kept"], 1)
                for c, a in ((0, SEQ), (3, RGW - 3)):
                    e.tensor_copy(pair(last_rows[:, 14:26])[:, :, c:c + 3], rg[:, :, a:a + 3])
                e.wait_ge(s["rg_done"], at(l, "rg_done"))
                e.tensor_copy(pair(last_rows[:, 26:30]), rh[:, :, SEQ - 1:T:DEC]).then_inc(s["rows_kept"], 1)
                e.wait_ge(s["rows_kept"], at(l, "rows_kept", 2))
                put("last", outs["last_out"][l], last_rows[:, :])
                for m in (AR, BE, KE):
                    e.memset(m, 0.0)
                for m in (Vm, Wm, Ym):
                    e.memset(m[:, :, 64:128], 0.0)
                e.memset(S[:, 0, :, :], 0.0).then_inc(s["frames_zeroed"], 1)
                e.wait_ge(s["state_out"], at(l, "state_out", NSTATE - 1))
                put("wkv", outs["wkv_out"][l, :, 0], S[:, 0, :, :])
                e.wait_ge(s["state_out"], at(l, "state_out", NSTATE))
                put("wkv", outs["wkv_out"][l, :, 1], S[:, 1, :, :])
                e.wait_ge(s["kr_ready"], at(l, "kr_ready"))
                put("latent", outs["kr_out"][l], kr[rope, :])
                e.wait_ge(s["rw_y"], at(l, "rw_y"))
                e.dma_start(mem32, mem_d).then_inc(tokens_ld, 16)
                e.wait_ge(s["ckv_n"], at(l, "ckv_n"))
                put("latent", outs["ckv_out"][l], ckv)
                if l == 0:
                    for k in range(1, 8):
                        e.wait_ge(msq_ready, k + 1)
                        if k > 1:
                            e.wait_ge(msq_added, k - 1)
                        e.tensor_tensor(msq[:, 0, :], msq[:, 0, :], msq[:, 1, :], ALU.add).then_inc(msq_added, 1)
                wait_tile(e, l, "out", 0)
                e.wait_ge(stored["latent"], 32 * (l + 1))
                if l + 1 < DEPTH:
                    e.dma_start(lw[:, :], lw_d[l + 1]).then_inc(lw_ld, 16)
                e.dma_start(mks[:, :, :], mks_d[l]).then_inc(mem_ld, 16)
                e.dma_start(mvs[:, :, :], mvs_d[l]).then_inc(mem_ld, 16)
                add_squares(3 * l + 1)
                wait_evac(e, l, "mk", 7)
                put("mem", outs["memk_out"][l], mkp)
                wait_evac(e, l, "mv", 7)
                put("mem", outs["memv_out"][l], mvp)
                add_squares(3 * l + 2)
                add_squares(3 * l + 3)
            for kind, n in (("last", 1), ("wkv", 2), ("latent", 2), ("mem", 2)):
                e.wait_ge(stored[kind], 16 * n * DEPTH)

        @block.tensor
        def _(e):
            def mm(out, a, b, start=True, stop=True):
                return e.matmul(out, lhsT=a, rhs=b, start=start, stop=stop)

            def halves(out, a, b, start=True, stop=True, n=T):
                h = (n + 1) // 2
                mm(out[:, 0:h], a, b[:, 0:h], start, stop)
                return mm(out[:, h:n], a, b[:, h:n], start, stop)

            def rms(r):
                e.wait_ge(s["sq_added"], 7 * (r + 1))
                halves(Q(2), ones, sq[:, 0, :]).then_inc(s["rms_sum"], 1)

            def three(product, out, a, b, first, last):
                product(out, a[0], b[0], first, False)
                product(out, a[0], b[1], False, False)
                return product(out, a[1], b[0], False, last)

            def dense(l, st, group=None, h_from=0):
                for i in range(*((0, {"in": 16}.get(st, 8)) if group is None else (8 * group, 8 * group + 8))):
                    t = TILE[(st, i)]
                    n = l * NT + t
                    slot = n % SPLIT
                    e.wait_ge(w_lo, n + 1)
                    if n >= 2:
                        eng, v = evac_value((n - 2) // NT, (n - 2) % NT)
                        e.wait_ge(evac[eng], v)
                    if st == "f2" and i % 8 == 0:
                        e.wait_ge(s["hid_lo"], at(l, "hid_lo", i + 8))
                    out = Q(t % 2)
                    if st == "mv":
                        for m in range(2):
                            for k in range(8):
                                last = three(mm, bank(2 * (t % 2), 128 * m, 128 * m + 128),
                                             [p[:, k, 128 * m:128 * m + 128] for p in (memH, memL)],
                                             [p[:, slot, k, :] for p in (wH, wL)], k == 0, k == 7)
                        last.then_inc(pe_done, 1)
                        continue
                    for k in range(8):
                        w = [p[:, slot, k, :] for p in (wH, wL)]
                        if st == "mk":
                            last = three(mm, bank(2 * (t % 2), 0, MEM), w, [p[:, k, :] for p in (memH, memL)],
                                         k == 0, k == 7)
                        elif st == "f2":
                            last = three(halves, out, w, [p[:, i // 8 % 2, k, :] for p in (hidH, hidL)],
                                         k == 0, k == 7)
                        else:
                            if i == 0:
                                e.wait_ge(s["h_ready"], at(l, "h_ready", h_from + k + 1))
                            last = three(halves, out, w, [p[:, k, :] for p in (hH, hL)], k == 0, k == 7)
                    last.then_inc(pe_done, 1)
                    if (st, i) == ("in", 0):
                        rms(3 * l)
                    if (st, i) == ("out", 1) and l == 0:
                        e.wait_ge(msq_added, 7)
                        mm(bank(6, 0, MEM), ones, msq[:, 0, :]).then_inc(mem_sum, 1)
                    if (st, i) == ("mk", 3):
                        rms(3 * l + 1)
                    if (st, i) == ("f1", 0):
                        rms(3 * l + 2)

            e.wait_ge(cst_ld, 16)
            for l in range(DEPTH):
                dense(l, "in", h_from=0)

                e.wait_ge(lw_ld, 16 * (l + 1))
                e.wait_ge(s["rg_conv"], at(l, "rg_conv"))
                wait_evac(e, l, "in", 15)
                for g, name in enumerate(("wa", "wx")):
                    for t in range(2):
                        halves(Q(2 * g + t, XCW), W(name, 128 * t, 128 * t + 128), xc[:, t, :],
                               n=XCW).then_inc(s["rg_z"], 1)

                e.wait_ge(s["rg_gates"], at(l, "rg_gates"))
                e.wait_ge(s["low_tanh"], at(l, "low_tanh"))
                for m in range(2):
                    rows = slice(32 * m, 32 * m + 32)
                    for t in range(2):
                        halves(Q(2 * m + t), W("low", 128 * t, 128 * t + 128, rows),
                               xs[rows, 6, 0:T]).then_inc(s["low_z"], 1)
                e.wait_ge(s["low_gate"], at(l, "low_gate", 4))
                e.wait_ge(s["kk_sq"], at(l, "kk_sq"))
                for t in range(2):
                    halves(Q(t), bones, e1[:, t, :]).then_inc(s["kk_sum"], 1)
                e.wait_ge(s["rk_ready"], at(l, "rk_ready"))
                for t in range(2):
                    halves(Q(2 + t), bones, e2[:, t, :]).then_inc(s["rk_sum"], 1)

                e.wait_ge(s["rg_done"], at(l, "rg_done"))
                for g in range(NG):
                    e.wait_ge(s["factors"], at(l, "factors", g + 1))
                    if g:
                        e.wait_ge(s["y_out"], at(l, "y_out", g))
                    for t in range(2):
                        e.transpose(bank(0, 128 * t, 128 * t + 128), xs[:, 4 + t, GRP * g:GRP * g + GRP], ident)
                        e.transpose(bank(0, 256 + 128 * t, 384 + 128 * t), af[:, t, :], ident)
                        e.transpose(bank(1, 128 * t, 128 * t + 128), be[:, t, :], ident)
                        last = e.transpose(bank(1, 256 + 128 * t, 384 + 128 * t), ke[:, t, :], ident)
                    last.then_inc(s["tok_T"], 1)
                    e.wait_ge(s["masked"], at(l, "masked", g + 1))
                    for u in range(4):
                        mm(PS[:, 1024 + 256 * u:1280 + 256 * u], bf[:, u // 2, :], AR[:, u, :])
                        mm(PS[:, 2048 + 256 * u:2304 + 256 * u], kf[:, u // 2, :], AR[:, u, :])
                        last = mm(bank(6, 128 * u, 128 * u + 128), AR[:, u, 0:128], bf[:, u // 2, :])
                    last.then_inc(s["scores"], 1)
                    e.wait_ge(s["tok_out"], at(l, "tok_out", g + 1))
                    e.wait_ge(s["scores_out"], at(l, "scores_out", g + 1))
                    for u in range(4):
                        last = mm(bank(7, 64 * u, 64 * u + 64), MG[:, u, 0:128],
                                  Vm[:, u // 2, 128 * (u % 2):128 * (u % 2) + 64])
                    last.then_inc(s["mv"], 1)
                    for b in range(5):
                        n = 5 * g + b
                        e.wait_ge(s["lev_T"], at(l, "lev_T", n + 1))
                        if b:
                            e.wait_ge(s["lev_X_out"], at(l, "lev_X_out", n))
                        for u in range(4):
                            last = mm(bank(0, 128 * u, 128 * u + 128), TT[:, u, :], X[:, u, :])
                        last.then_inc(s["lev_P"], 1)
                        e.wait_ge(s["lev_P_out"], at(l, "lev_P_out", n + 1))
                        for u in range(4):
                            if b < 4:
                                mm(bank(1, 128 * u, 128 * u + 128), XT[:, u, :], P[:, u, :])
                            last = mm(bank(2, 128 * u, 128 * u + 128), P[:, u, :], XT[:, u, :])
                        last.then_inc(s["lev_X"], 1)
                    e.wait_ge(s["lev_X_out"], at(l, "lev_X_out", 5 * g + 5))
                    e.wait_ge(s["mv_out"], at(l, "mv_out", g + 1))
                    for u in range(4):
                        last = mm(bank(3, 128 * u, 128 * u + 128), XT[:, u, :], Rt[:, u, :])
                    last.then_inc(s["xr"], 1)
                    e.wait_ge(s["xr_out"], at(l, "xr_out", g + 1))

                    def both(m, t):
                        return m[:, t, :].rearrange("p (a b) -> p a b", a=3)[:, 0:3:2, :]

                    for t in range(2):
                        for h in range(2):
                            mm(bank(4, 256 * t, 256 * t + 256)[rows_of[h], :], Wm[:, t, 128 * h:128 * h + 64],
                               BE[:, t, :, :].rearrange("p a b -> p (a b)"))
                    for t in range(2):
                        for c in range(2):
                            o = pair(bank(5, 256 * t + 128 * c, 256 * t + 128 * c + 128))
                            mm(o, KE[:, t, c, :], both(Vm, t), True, False)
                            mm(o, BE[:, t, c, :], both(Ym, t), False, True)
                    for t in range(2):
                        o = bank(6, 128 * t, 128 * t + 128)
                        mm(o, Wm[:, t, 0:128], LG[:, 2 * t, 128:256], True, False)
                        mm(o, Wm[:, t, 64:192], LG[:, 2 * t + 1, 128:256], False, True)
                    for t in range(2):
                        o = bank(6, 256 + 128 * t, 384 + 128 * t)
                        mm(o, Vm[:, t, 0:128], MG[:, 2 * t, 128:256], True, False)
                        mm(o, Vm[:, t, 64:192], MG[:, 2 * t + 1, 128:256], False, False)
                        mm(o, Ym[:, t, 0:128], LG[:, 2 * t, 128:256], False, False)
                        last = mm(o, Ym[:, t, 64:192], LG[:, 2 * t + 1, 128:256], False, True)
                    last.then_inc(s["ab"], 1)
                    e.wait_ge(s["ab_out"], at(l, "ab_out", g + 1))
                    for c in range(2 if g < NG - 1 else 1):
                        n = 2 * g + c
                        src = pair(W("S0", 0, 256)) if g == NG - 1 else S[:, c, :, :]
                        if n:
                            e.wait_ge(s["state_out"], at(l, "state_out", n))
                        for t in range(2):
                            mm(bank(0, 128 * t + 64 * c, 128 * t + 64 * c + 64), src[:, t, :],
                               rp[:, t, 64 * c:64 * c + 64])
                        for t in range(2):
                            last = mm(bank(7, 128 * t, 128 * t + 128), Abd[:, t, c, :], src[:, t, :])
                        last.then_inc(s["state_mm"], 1)

                e.wait_ge(s["y_out"], at(l, "y_out", NG))
                for t in range(2):
                    halves(Q(t), bones, yrw[:, t, 0:T]).then_inc(s["gn_sum"], 1)
                for t in range(2):
                    last = halves(Q(2 + t), W("low", 128 * t, 128 * t + 128, rows_of[1]), xs[64:128, 6, 0:T])
                last.then_inc(s["g_out"], 1)
                e.wait_ge(s["gn_sq"], at(l, "gn_sq"))
                for t in range(2):
                    halves(Q(t), bones, ell[:, t, 0:T]).then_inc(s["gn_sum"], 1)

                e.wait_ge(s["rw_y"], at(l, "rw_y"))
                e.wait_ge(s["lat_sq"], at(l, "lat_sq"))
                for t in range(2):
                    last = halves(Q(0), ones, kk[:, t, 0:T], t == 0, t == 1)
                last.then_inc(s["lat_sum"], 1)
                halves(Q(1), ones, bneg[:, 0, 0:T]).then_inc(s["lat_sum"], 1)
                e.wait_ge(s["ckv_n"], at(l, "ckv_n"))
                for j in range(7):
                    src = ckv[:, 128 * j:128 * j + (128 if j < 4 else DEC)] if j < 5 else \
                        W("ckv", 128 * (j - 5), 128 * (j - 4))
                    if j >= 2:
                        e.wait_ge(s["v_out"], at(l, "v_out", j - 1))
                    mm(bank(4 + j % 2)[0:src.shape[-1], :], src, W("uv", 0, 512)).then_inc(s["v_mm"], 1)
                e.wait_ge(s["cq_n"], at(l, "cq_n"))
                e.wait_ge(s["v_out"], at(l, "v_out", 7))

                units = [(h, b) for h in range(HEADS) for b in range(5)]

                def project(h):
                    if h:
                        e.wait_ge(s["k_out"], at(l, "k_out", h))
                    for k in range(2):
                        halves(Q(0)[0:QKD, :], W("uq", (k * HEADS + h) * QKD, (k * HEADS + h + 1) * QKD),
                               cq[:, k, :], k == 0, k == 1)
                    for k in range(2):
                        last = halves(Q(1)[rope, :], W("uqs", (k * HEADS + h) * ROPE, (k * HEADS + h + 1) * ROPE),
                                      cq[:, k, :], k == 0, k == 1)
                    last.then_inc(s["q_mm"], 1)
                    e.wait_ge(s["q_out"], at(l, "q_out", 2 * h + 1))
                    halves(Q(0)[0:64, :], W("uk", 64 * h, 64 * h + 64), ckv)
                    mm(bank(2, 0, PAST)[0:64, :], W("uk", 64 * h, 64 * h + 64),
                       W("ckv", 0, PAST)).then_inc(s["k_mm"], 1)

                def score(u):
                    h, b = units[u]
                    if b == 0:
                        e.wait_ge(s["q_out"], at(l, "q_out", 2 * h + 2))
                        e.wait_ge(s["k_out"], at(l, "k_out", h + 1))
                    if u >= 2:
                        e.wait_ge(s["a_exp"], at(l, "a_exp", u - 1))
                    o = bank(4 + u % 2)
                    if b < 4:
                        nk = 128 * b + 128
                        mm(o[:, 0:nk], aq[0:QKD, h % 2, 128 * b:128 * b + 128], ak[0:QKD, h % 2, 0:nk], True, False)
                        mm(o[:, nk - 128:nk], C("maskq", 0, 128, slice(0, 1)), C("maskk", 0, 128, slice(0, 1)),
                           False, True).then_inc(s["a_score"], 1)
                    else:
                        mm(o[0:DEC, 0:KEYS - SEQ], aq[0:QKD, h % 2, SEQ:T],
                           ak[0:QKD, h % 2, SEQ:KEYS]).then_inc(s["a_score"], 1)

                def tail(u):
                    h, b = units[u]
                    e.wait_ge(s["a_norm"], at(l, "a_norm", u + 1))
                    if u:
                        e.wait_ge(s["a_T_out"], at(l, "a_T_out", u))
                    if b < 4:
                        for j in range(b + 1):
                            last = e.transpose(bank(6, 128 * j, 128 * j + 128),
                                               aP[:, u % 2, 128 * j:128 * j + 128], ident)
                    else:
                        e.transpose(bank(6, 0, DEC)[0:DEC, :], aP[0:DEC, u % 2, 0:DEC], ident[0:DEC, 0:DEC])
                        for j in range(2):
                            last = e.transpose(bank(6, 128 * j + 128, 128 * j + 128 + DEC),
                                               aP[0:DEC, u % 2, DEC + 128 * j:DEC + 128 * j + 128],
                                               ident[0:DEC, 0:DEC])
                    last.then_inc(s["a_T"], 1)

                def pv(u):
                    h, b = units[u]
                    e.wait_ge(s["a_T_out"], at(l, "a_T_out", u + 1))
                    if u >= 1:
                        e.wait_ge(s["a_o"], at(l, "a_o", u))
                    rows = rows_of[h % 2]
                    if b < 4:
                        o = bank(7, 0, 128)[rows, :]
                        for j in range(b + 1):
                            last = mm(o, av[:, j, 64 * h:64 * h + 64], aPT[:, u % 2, 128 * j:128 * j + 128],
                                      j == 0, j == b)
                    else:
                        o = bank(7, 0, DEC)[rows, :]
                        mm(o, av[0:DEC, 4, 64 * h:64 * h + 64], aPT[0:DEC, u % 2, 0:DEC], True, False)
                        for j in range(2):
                            last = mm(o, av[:, 5 + j, 64 * h:64 * h + 64],
                                      aPT[:, u % 2, 128 * j + 128:128 * j + 128 + DEC], False, j == 1)
                    last.then_inc(s["a_pv"], 1)

                project(0)
                for u in range(len(units) + 2):
                    if u < len(units):
                        if units[u][1] == 2 and units[u][0] + 1 < HEADS:
                            project(units[u][0] + 1)
                        score(u)
                    if u >= 2:
                        pv(u - 2)
                    if 1 <= u <= len(units):
                        tail(u - 1)

                dense(l, "out", h_from=8)
                e.wait_ge(s["memn"], at(l, "memn"))
                dense(l, "mk")
                dense(l, "mv")
                dense(l, "mq", h_from=16)
                wait_evac(e, l, "mv", 7)
                wait_evac(e, l, "mq", 7)
                e.wait_ge(mem_ld, 32 * (l + 1))

                munits = [(h, b) for h in range(MHEADS) for b in range(5)]

                def mscore(u):
                    h, b = munits[u]
                    if u >= 2:
                        e.wait_ge(s["m_exp"], at(l, "m_exp", u - 1))
                    n = 128 if b < 4 else DEC
                    keys = mkp if b < 4 else mks
                    for j in range(2):
                        last = mm(bank(4 + u % 2, 0, MEM)[0:n, :], mq[:, 2 * h + j, 128 * b:128 * b + n],
                                  keys[:, 2 * h + j, :], j == 0, j == 1)
                    last.then_inc(s["m_score"], 1)

                def mtail(u):
                    h, b = munits[u]
                    n = 128 if b < 4 else DEC
                    e.wait_ge(s["m_norm"], at(l, "m_norm", u + 1))
                    if u:
                        e.wait_ge(s["m_T_out"], at(l, "m_T_out", u))
                    for j in range(2):
                        last = e.transpose(bank(6, 128 * j, 128 * j + n), mP[0:n, u % 2, 128 * j:128 * j + 128],
                                           ident[0:n, 0:n])
                    last.then_inc(s["m_T"], 1)

                def mpv(h):
                    e.wait_ge(s["m_T_out"], at(l, "m_T_out", 5 * h + 5))
                    for i in range(2):
                        if h:
                            e.wait_ge(s["m_o"], at(l, "m_o", 4 * (h - 1) + 2 * i + 2))
                        for k, (va, a, b) in enumerate(((mvp, 0, SEQ), (mvs, SEQ, T))):
                            for j in range(2):
                                last = mm(bank(2 * k + i, 0, b - a),
                                          va[:, j, 256 * h + 128 * i:256 * h + 128 * i + 128],
                                          mPT[:, h % 2, j, a:b], j == 0, j == 1)
                            last.then_inc(s["m_pv"], 1)

                for u in range(len(munits) + 2):
                    if u < len(munits):
                        mscore(u)
                    if 1 <= u <= len(munits):
                        mtail(u - 1)
                    if u >= 2 and (u - 2) % 5 == 4:
                        mpv((u - 2) // 5)
                e.wait_ge(s["m_o"], at(l, "m_o", 16))
                dense(l, "mo", h_from=24)
                for g in range(5):
                    if g < 4:
                        dense(l, "f1", g, h_from=32)
                    if g:
                        dense(l, "f2", g - 1)
            rms(3 * DEPTH)

        @block.scalar
        def _(e):
            steps = 0

            def act(out, in_, f, **kw):
                return e.activation(out, in_, f, **kw)

            def link(ins):
                nonlocal steps
                steps += 1
                ins.then_inc(astep, 1)
                e.wait_ge(astep, steps)

            def split(n):
                e.wait_ge(w_load[n % RING], 16 * (n // RING + 1))
                if n >= SPLIT:
                    e.wait_ge(pe_done, n - SPLIT + 1)
                act(wH[:, n % SPLIT], ring[:, n % RING], ACT.Copy).then_inc(w_hi, 1)

            def ahead(l, st, i):
                n = tile_no(l, st, i) + 2
                if split_now(n):
                    split(n)

            def square(r, k):
                if k == 0 and r:
                    e.wait_ge(s["rms_sum"], r)
                if k > 1:
                    e.wait_ge(s["sq_added"], 7 * r + k - 1)
                act(sq[:, min(k, 1), :], xT[:, k, :], ACT.Square).then_inc(s["sq_ready"], 1)

            def rstd(r):
                e.wait_ge(s["rms_sum"], r + 1)
                link(act(rs, Q(2), ACT.Ln, scale=1.0 / D, bias=K(C_EPS)))
                act(rs, rs, ACT.Exp, scale=-0.5).then_inc(s["rms_rstd"], 1)

            def scaled_hi(l, gain, k):
                act(hH[:, k, :], xT[:, k, :], ACT.Copy, scale=V(l, gain, k)).then_inc(s["h_hi"], 1)

            def mixed_hi(k):
                act(hH[:, k, :], hT[:, k, :], ACT.Copy).then_inc(s["h_hi"], 1)

            e.wait_ge(vec_ld, 16)
            for k in range(8):
                e.wait_ge(x_ld[k // 4], 16)
                if k in (1, 4):
                    split(k // 4)
                scaled_hi(0, "g_mix", k)
                square(0, k)
            e.wait_ge(setup_abs, 1)
            act(stat[:, 0:4], stat[:, 4:8], ACT.Exp, scale=-1.0).then_inc(setup_exp, 1)
            for l in range(DEPTH):
                for i in range(16):
                    ahead(l, "in", i)
                    if i == 0:
                        rstd(3 * l)
                if l == 0:
                    e.wait_ge(setup_vec, 1)

                for t in range(2):
                    e.wait_ge(s["rg_z"], at(l, "rg_z", t + 1))
                    act(ra[:, t, :], Q(t, XCW), ACT.Tanh, scale=0.5, bias=derv[:, l, t:t + 1])
                for t in range(2):
                    e.wait_ge(s["rg_z"], at(l, "rg_z", t + 3))
                    last = act(rix[:, t, :], Q(2 + t, XCW), ACT.Tanh, scale=0.5, bias=derv[:, l, 2 + t:3 + t])
                last.then_inc(s["rg_gates"], 1)
                e.wait_ge(s["rg_gates"], at(l, "rg_gates"))
                for t in range(2):
                    last = act(ru[:, t, :], ra[:, t, :], ACT.Tanh, scale=derv[:, l, 8 + t:9 + t],
                               bias=derv[:, l, 8 + t:9 + t])
                link(last)
                for t in range(2):
                    act(ra[:, t, :], ra[:, t, :], ACT.Exp, scale=derv[:, l, 10 + t:11 + t],
                        bias=derv[:, l, 10 + t:11 + t])
                e.wait_ge(s["low_ready"], at(l, "low_ready"))
                act(xs[0:32, 6, 0:T], xs[0:32, 6, 0:T], ACT.Tanh)
                act(xs[64:128, 6, 0:T], xs[64:128, 6, 0:T], ACT.Tanh, scale=0.5).then_inc(s["low_tanh"], 1)
                e.wait_ge(s["rg_gelu_in"], at(l, "rg_gelu_in"))
                act(gx, gx, ACT.Tanh, scale=GELU_C).then_inc(s["rg_gelu"], 1)
                for t in range(4):
                    e.wait_ge(s["low_z"], at(l, "low_z", t + 1))
                    act((ell if t < 2 else bneg)[:, t % 2, 0:T], Q(t), ACT.Tanh, scale=0.5,
                        bias=derv[:, l, 4 + t:5 + t]).then_inc(s["low_gate"], 1)
                e.wait_ge(s["kk_raw"], at(l, "kk_raw"))
                act(e1, kk[:, :, 0:T], ACT.Square).then_inc(s["kk_sq"], 1)
                e.wait_ge(s["rg_ix"], at(l, "rg_ix"))
                act(xc, ru, ACT.Ln, bias=K(C_ONE))
                act(rln, ru, ACT.Ln, scale=2.0, bias=K(C_TINY)).then_inc(s["rg_ln"], 1)
                for t in range(2):
                    e.wait_ge(s["kk_sum"], at(l, "kk_sum", t + 1))
                    last = act(e1[:, t, :], Q(t), ACT.Ln, bias=K(C_L2))
                link(last)
                act(e1, e1, ACT.Exp, scale=-0.5).then_inc(s["kk_rstd"], 1)
                e.wait_ge(s["rg_q"], at(l, "rg_q"))
                act(ru, ru, ACT.Exp, scale=0.5).then_inc(s["rg_sq"], 1)

                e.wait_ge(s["frames_zeroed"], at(l, "frames_zeroed"))
                for g in range(NG):
                    e.wait_ge(s["decay_cum"], at(l, "decay_cum", g + 1))
                    act(stat[:, 8:12], Lc.rearrange("p a (c n) -> p (a c) n", c=2)[:, :, CH - 1], ACT.Exp,
                        scale=-1.0)
                    act(ep, Lc, ACT.Exp)
                    act(ee, le, ACT.Exp)
                    link(act(en1, dm, ACT.Exp, scale=-1.0))
                    act(en, Lc, ACT.Exp, scale=-1.0).then_inc(s["decay_exp"], 1)
                    e.wait_ge(s["tok_T"], at(l, "tok_T", g + 1))
                    for t in range(2):
                        act(Vm[:, t, :].rearrange("p (a b) -> p a b", a=3)[:, 0:3:2, :],
                            pair(bank(0, 128 * t, 128 * t + 128)), ACT.Copy)
                        act(Rt[:, 2 * t:2 * t + 2, 0:64], pair(bank(0, 256 + 128 * t, 384 + 128 * t)), ACT.Copy)
                    for c in range(2):
                        act(BE[rows_of[c], :, c, :], pair(bank(1, 0, 256))[rows_of[c]], ACT.Copy)
                        last = act(KE[rows_of[c], :, c, :], pair(bank(1, 256, 512))[rows_of[c]], ACT.Copy)
                    last.then_inc(s["tok_out"], 1)
                    e.wait_ge(s["mv"], at(l, "mv", g + 1))
                    act(Rt[:, :, 64:128], pair(bank(7, 0, 256), 4), ACT.Copy).then_inc(s["mv_out"], 1)
                    e.wait_ge(s["xr"], at(l, "xr", g + 1))
                    for t in range(2):
                        o = pair(bank(3, 256 * t, 256 * t + 256))
                        act(Wm[:, t, :].rearrange("p (a b) -> p a b", a=3)[:, 0:3:2, :], o[:, :, 0:64], ACT.Copy)
                        last = act(Ym[:, t, :].rearrange("p (a b) -> p a b", a=3)[:, 0:3:2, :], o[:, :, 64:128],
                                   ACT.Copy)
                    last.then_inc(s["xr_out"], 1)

                e.wait_ge(s["gn_mean"], at(l, "gn_mean"))
                act(ell[:, :, 0:T], yrw[:, :, 0:T], ACT.Square).then_inc(s["gn_sq"], 1)
                for t in range(2):
                    e.wait_ge(s["gn_sum"], at(l, "gn_sum", 3 + t))
                    last = act(ell[:, t, 0:T], Q(t), ACT.Ln, scale=1.0 / 64, bias=K(C_GN))
                link(last)
                act(ell[:, :, 0:T], ell[:, :, 0:T], ACT.Exp, scale=-0.5).then_inc(s["gn_rstd"], 1)
                act(kk[:, :, 0:T], cq, ACT.Square)
                act(bneg[:, 0, 0:T], ckv, ACT.Square).then_inc(s["lat_sq"], 1)
                e.wait_ge(s["rw_y"], at(l, "rw_y"))
                for t, n in enumerate((256, 128)):
                    e.wait_ge(s["lat_sum"], at(l, "lat_sum", t + 1))
                    link(act(ell[:, t, 0:T], Q(t), ACT.Ln, scale=1.0 / n, bias=K(C_EPS)))
                    act(ell[:, t, 0:T], ell[:, t, 0:T], ACT.Exp, scale=-0.5).then_inc(s["lat_rstd"], 1)
                e.wait_ge(stored["wkv"], 32 * (l + 1))
                for j in range(7):
                    n = DEC if j == 4 else 128
                    e.wait_ge(s["v_mm"], at(l, "v_mm", j + 1))
                    act(av[0:n, j, :], bank(4 + j % 2)[0:n, :], ACT.Copy).then_inc(s["v_out"], 1)

                units = [(h, b) for h in range(HEADS) for b in range(5)]

                def keys_out(h):
                    if h >= 2:
                        e.wait_ge(s["a_score"], at(l, "a_score", 5 * (h - 1)))
                    e.wait_ge(s["k_mm"], at(l, "k_mm", h + 1))
                    act(ak[0:64, h % 2, 0:T], Q(0)[0:64, :], ACT.Copy)
                    act(ak[0:64, h % 2, T:KEYS], bank(2, 0, PAST)[0:64, :], ACT.Copy).then_inc(s["k_out"], 1)

                keys_out(0)
                for u in range(len(units) + 2):
                    if u in OUT_TILES_SPLIT:
                        split(tile_no(l, "out", OUT_TILES_SPLIT.index(u)))
                    if u < len(units):
                        h, b = units[u]
                        if b == 2 and h + 1 < HEADS:
                            keys_out(h + 1)
                        n, nk = (128, 128 * b + 128) if b < 4 else (DEC, KEYS - SEQ)
                        e.wait_ge(s["a_max"], at(l, "a_max", u + 1))
                        act(aP[0:n, u % 2, 0:nk], bank(4 + u % 2, 0, nk)[0:n, :], ACT.Exp, scale=MLA_SCALE,
                            bias=stat[0:n, 18 + u % 2:19 + u % 2],
                            accum_out=stat[0:n, 20 + u % 2:21 + u % 2]).then_inc(s["a_exp"], 1)
                    if 1 <= u <= len(units):
                        h, b = units[u - 1]
                        e.wait_ge(s["a_T"], at(l, "a_T", u))
                        if b < 4:
                            last = act(aPT[:, (u - 1) % 2, 0:128 * b + 128], bank(6, 0, 128 * b + 128), ACT.Copy)
                        else:
                            act(aPT[0:DEC, (u - 1) % 2, 0:DEC], bank(6, 0, DEC)[0:DEC, :], ACT.Copy)
                            last = act(pair(aPT[:, (u - 1) % 2, 128:384])[:, :, 0:DEC],
                                       pair(bank(6, 128, 384))[:, :, 0:DEC], ACT.Copy)
                        last.then_inc(s["a_T_out"], 1)
                    if u >= 2:
                        h, b = units[u - 2]
                        n = 128 if b < 4 else DEC
                        e.wait_ge(s["a_pv"], at(l, "a_pv", u - 1))
                        rows = rows_of[h % 2]
                        act(hT[rows, 4 + h // 2, 128 * b:128 * b + n], bank(7, 0, n)[rows, :],
                            ACT.Copy).then_inc(s["a_o"], 1)
                    for k in range(8):
                        if u == MIXED_AT[k]:
                            if k > 3:
                                e.wait_ge(s["a_o"], at(l, "a_o", u - 1))
                            mixed_hi(k)

                for i in range(8):
                    ahead(l, "out", i)
                    if l == 0 and i == 0:
                        e.wait_ge(tokens_ld, 16)
                        for k in range(8):
                            if k > 1:
                                e.wait_ge(msq_added, k - 1)
                            act(msq[:, min(k, 1), :], mem32[:, k, :], ACT.Square).then_inc(msq_ready, 1)
                    if l == 0 and i == 2:
                        e.wait_ge(mem_sum, 1)
                        link(act(mrs, bank(6, 0, MEM), ACT.Ln, scale=1.0 / D, bias=K(C_EPS)))
                        act(mrs, mrs, ACT.Exp, scale=-0.5).then_inc(mem_rstd, 1)
                    if i == 5:
                        e.wait_ge(s["mem_scaled"], at(l, "mem_scaled"))
                        act(memH[:, :, :], mem32, ACT.Copy).then_inc(s["mem_hi"], 1)
                    wait_evac(e, l, "out", i)
                    square(3 * l + 1, i)
                for st, dst in (("mk", mkp), ("mv", mvp)):
                    for i in range(8):
                        ahead(l, st, i)
                        if st == "mk":
                            if i == 0:
                                wait_tile(e, l, "out", 7)
                            scaled_hi(l, "g_mem", i)
                        if (st, i) == ("mv", 3):
                            rstd(3 * l + 1)
                        wait_tile(e, l, st, i)
                        to = dst[:, i, :] if st == "mk" else dst[:, :, 128 * i:128 * i + 128]
                        t = TILE[(st, i)]
                        o = bank(2 * (t % 2), 0, 256)
                        act(to, o if st == "mk" else pair(o), ACT.Copy).then_inc(evac["act"], 1)
                for i in range(8):
                    ahead(l, "mq", i)
                munits = [(h, b) for h in range(MHEADS) for b in range(5)]

                def out_tiles(h):
                    for i in range(2):
                        for k, (a, b) in enumerate(((0, SEQ), (SEQ, T))):
                            e.wait_ge(s["m_pv"], at(l, "m_pv", 4 * h + 2 * i + k + 1))
                            act(hT[:, 2 * h + i, a:b], bank(2 * k + i, 0, b - a), ACT.Copy).then_inc(s["m_o"], 1)

                for u in range(len(munits) + 2):
                    if u < len(munits):
                        h, b = munits[u]
                        n = 128 if b < 4 else DEC
                        e.wait_ge(s["m_max"], at(l, "m_max", u + 1))
                        act(mP[0:n, u % 2, :], bank(4 + u % 2, 0, MEM)[0:n, :], ACT.Exp, scale=MEM_SCALE,
                            bias=stat[0:n, 18 + u % 2:19 + u % 2],
                            accum_out=stat[0:n, 20 + u % 2:21 + u % 2]).then_inc(s["m_exp"], 1)
                    if 1 <= u <= len(munits):
                        h, b = munits[u - 1]
                        n = 128 if b < 4 else DEC
                        e.wait_ge(s["m_T"], at(l, "m_T", u))
                        act(mPT[:, h % 2, :, 128 * b:128 * b + n], pair(bank(6, 0, 256))[:, :, 0:n],
                            ACT.Copy).then_inc(s["m_T_out"], 1)
                    if u >= 2 and (u - 2) % 5 == 4:
                        h = (u - 2) // 5
                        out_tiles(h)
                        e.wait_ge(s["m_o"], at(l, "m_o", 4 * h + 4))
                        mixed_hi(2 * h)
                        mixed_hi(2 * h + 1)
                for i in range(8):
                    ahead(l, "mo", i)
                    if i == 7:
                        wait_tile(e, l, "mo", 7)
                        for k in range(7):
                            scaled_hi(l, "g_ffn", k)
                    wait_evac(e, l, "mo", i)
                    square(3 * l + 2, i)
                scaled_hi(l, "g_ffn", 7)
                for g in range(5):
                    if g < 4:
                        for i in range(8 * g, 8 * g + 8):
                            ahead(l, "f1", i)
                            if i == 0:
                                rstd(3 * l + 2)
                            e.wait_ge(s["hid_sq"], at(l, "hid_sq", i + 1))
                            act(hidH[:, g % 2, i % 8, :], hid[:, g % 2, i % 8, :], ACT.Copy)\
                                .then_inc(s["hid_hi"], 1)
                    if g:
                        for i in range(8 * g - 8, 8 * g):
                            ahead(l, "f2", i)
                            if g == 4:
                                wait_evac(e, l, "f2", i)
                                square(3 * l + 3, i % 8)
                                if l + 1 < DEPTH:
                                    scaled_hi(l + 1, "g_mix", i % 8)
            rstd(3 * DEPTH)

        @block.vector
        def _(e):
            steps = 0

            def link(ins):
                nonlocal steps
                steps += 1
                ins.then_inc(vstep, 1)
                e.wait_ge(vstep, steps)

            tt, stt, ts = e.tensor_tensor, e.scalar_tensor_tensor, e.tensor_scalar

            def split(n):
                e.wait_ge(w_hi, n + 1)
                tt(wL[:, n % SPLIT], ring[:, n % RING], plain(wH[:, n % SPLIT]), ALU.subtract).then_inc(w_lo, 1)

            def ahead(l, st, i):
                n = tile_no(l, st, i) + 2
                if split_now(n):
                    split(n)

            def scaled_lo(l, h_from, gain, k):
                e.wait_ge(s["h_hi"], at(l, "h_hi", h_from + k + 1))
                stt(hL[:, k, :], xT[:, k, :], V(l, gain, k), plain(hH[:, k, :]), ALU.mult, ALU.subtract)\
                    .then_inc(s["h_ready"], 1)

            def mixed_lo(l, h_from, k):
                e.wait_ge(s["h_hi"], at(l, "h_hi", h_from + k + 1))
                tt(hL[:, k, :], hT[:, k, :], plain(hH[:, k, :]), ALU.subtract).then_inc(s["h_ready"], 1)

            def take_tile(l, st, i):
                wait_tile(e, l, st, i)
                return Q(TILE[(st, i)] % 2)

            def residual(l, st, i):
                ps = take_tile(l, st, i)
                k = i % 8
                if i >= 8:
                    wait_evac(e, l, st, i - 8)
                tt(xT[:, k, :], ps, xT[:, k, :], ALU.add).then_inc(evac["dve"], 1)

            for c, v in ((C_TINY, 1e-37), (C_EPS, EPS), (C_L2, L2_EPS), (C_GN, GN_EPS), (C_ONE, 1.0)):
                e.memset(K(c), v)
            e.wait_ge(vec_ld, 16)
            for k in range(8):
                if k in (1, 4):
                    split(k // 4)
                scaled_lo(0, 0, "g_mix", k)
            lam = vec[:, :, VEC["lam"]:VEC["lam"] + 2]
            four = lambda a: pair(stat[:, a:a + 4])
            stt(four(4), lam, -1.0, lam, ALU.mult, ALU.max).then_inc(setup_abs, 1)
            link(ts(four(24), lam, -1.0, 0.0, ALU.mult, ALU.max))
            e.wait_ge(setup_exp, 1)
            link(ts(four(28), four(0), 2.0, None, ALU.add))
            link(e.reciprocal(four(32), four(28)))
            link(tt(four(28), four(0), four(32), ALU.mult))
            link(tt(four(32), four(28), four(28), ALU.mult))
            link(ts(four(36), four(32), 1.0 / 15, None, ALU.mult))
            for k in (13, 11, 9, 7, 5, 3):
                link(stt(four(36), four(36), 1.0 / k, four(32), ALU.add, ALU.mult))
            link(stt(four(36), four(36), 1.0, four(28), ALU.add, ALU.mult))
            link(stt(four(36), four(36), 2.0, four(24), ALU.mult, ALU.add))
            ts(derv[:, :, 8:10], four(36), 4.0, None, ALU.mult)
            ts(derv[:, :, 10:12], four(36), -4.0, None, ALU.mult)
            ts(derv[:, :, 0:8], vec[:, :, VEC["rg_ba"]:VEC["rg_ba"] + 8], 0.5, None,
               ALU.mult).then_inc(setup_vec, 1)
            for l in range(DEPTH):
                if l:
                    e.wait_ge(stored["mem"], 32 * l)
                e.memset(raw[:, :, 0:1], 0.0)
                e.tensor_copy(raw[:, :, SEQ + 1], vec[:, l, VEC["shift"]:VEC["shift"] + 7])
                e.memset(rg[:, :, 0:3], 0.0)
                link(e.tensor_copy(rg[:, :, 3 + SEQ:6 + SEQ], pair(vec[:, l, VEC["conv_s"]:VEC["conv_s"] + 6])))
                for i in range(16):
                    ahead(l, "in", i)
                    if i == 0:
                        e.wait_ge(s["rms_rstd"], 3 * l + 1)
                    ps = take_tile(l, "in", i)
                    if i < RWT:
                        tt(raw[:, i, 1:1 + SEQ], ps[:, 0:SEQ], rs[:, 0:SEQ], ALU.mult)
                        tt(raw[:, i, 2 + SEQ:RWW], ps[:, SEQ:T], rs[:, SEQ:T], ALU.mult).then_inc(evac["dve"], 1)
                        wait_evac(e, l, "in", i)
                        tt(xs[:, i, 0:SEQ], raw[:, i, 0:SEQ], raw[:, i, 1:1 + SEQ], ALU.subtract)
                        link(tt(xs[:, i, SEQ:T], raw[:, i, 1 + SEQ:RWW - 1], raw[:, i, 2 + SEQ:RWW], ALU.subtract))
                        stt(xs[:, i, 0:SEQ], xs[:, i, 0:SEQ], V(l, "mu", i), raw[:, i, 1:1 + SEQ], ALU.mult, ALU.add)
                        ins = stt(xs[:, i, SEQ:T], xs[:, i, SEQ:T], V(l, "mu", i), raw[:, i, 2 + SEQ:RWW],
                                  ALU.mult, ALU.add)
                        if i == 6:
                            ins.then_inc(s["low_ready"], 1)
                        else:
                            link(ins)
                        if i in (2, 3):
                            ins = ts(kk[:, i - 2, 0:T], xs[:, i, 0:T], V(l, "k_k", i - 2), None, ALU.mult)
                            if i == 3:
                                ins.then_inc(s["kk_raw"], 1)
                    elif i < 9:
                        tt(cq[:, i - 7, :], ps, rs, ALU.mult).then_inc(evac["dve"], 1)
                    elif i == 9:
                        tt(ckv, ps, rs, ALU.mult).then_inc(evac["dve"], 1)
                    elif i == 10:
                        tt(kr[rope, :], ps[rope, :], C("cos", 0, T, rope), ALU.mult).then_inc(evac["dve"], 1)
                    elif i == 11:
                        tt(aq[rope, 0, :], ps[rope, :], C("sin", 0, T, rope), ALU.mult).then_inc(evac["dve"], 1)
                        wait_evac(e, l, "in", 11)
                        link(tt(kr[rope, :], kr[rope, :], aq[rope, 0, :], ALU.add))
                        tt(kr[rope, :], kr[rope, :], rs[rope, :], ALU.mult).then_inc(s["kr_ready"], 1)
                    elif i < 14:
                        t = i - 12
                        tt(rg[:, t, 3:3 + SEQ], ps[:, 0:SEQ], rs[:, 0:SEQ], ALU.mult)
                        tt(rg[:, t, 6 + SEQ:RGW], ps[:, SEQ:T], rs[:, SEQ:T], ALU.mult).then_inc(evac["dve"], 1)
                        wait_evac(e, l, "in", i)
                        link(ts(xc[:, t, :], rg[:, t, 0:XCW], V(l, "conv_w", t), V(l, "conv_b", t),
                                ALU.mult, ALU.add))
                        for j in range(1, CONV):
                            ins = stt(xc[:, t, :], rg[:, t, j:j + XCW], V(l, "conv_w", 2 * j + t), xc[:, t, :],
                                      ALU.mult, ALU.add)
                            if j < CONV - 1 or t == 0:
                                link(ins)
                        if t:
                            ins.then_inc(s["rg_conv"], 1)
                    else:
                        tt(gate[:, i - 14, :], ps, rs, ALU.mult).then_inc(evac["dve"], 1)
                wait_evac(e, l, "in", 15)

                link(tt(gx, gate, gate, ALU.mult))
                link(ts(gx, gx, 0.044715, 1.0, ALU.mult, ALU.add))
                tt(gx, gx, gate, ALU.mult).then_inc(s["rg_gelu_in"], 1)
                e.wait_ge(s["rg_gates"], at(l, "rg_gates"))
                stt(rix, rix, 1.0, xc, ALU.add, ALU.mult).then_inc(s["rg_ix"], 1)
                e.wait_ge(s["rg_gelu"], at(l, "rg_gelu"))
                link(stt(gate, gx, 1.0, gate, ALU.add, ALU.mult))

                e.wait_ge(s["low_gate"], at(l, "low_gate", 4))
                ts(ell[:, :, 0:T], ell[:, :, 0:T], 0.5 * EXP_HALF, 0.5 * EXP_HALF, ALU.mult, ALU.add)
                ts(xs[64:128, 6, 0:T], xs[64:128, 6, 0:T], 0.5, 0.5, ALU.mult, ALU.add)
                link(ts(bneg[:, :, 0:T], bneg[:, :, 0:T], 0.5, 0.5, ALU.mult, ALU.add))
                for t in range(2):
                    link(ts(e2[:, t, :], bneg[:, t, 0:T], -1.0, V(l, "k_a", t), ALU.add, ALU.mult))
                    link(stt(xs[:, 2 + t, 0:T], e2[:, t, :], 1.0, xs[:, 2 + t, 0:T], ALU.add, ALU.mult))
                    ins = stt(e2[:, t, :], xs[:, t, 0:T], V(l, "r_k", t), xs[:, 2 + t, 0:T], ALU.mult, ALU.mult)
                ins.then_inc(s["rk_ready"], 1)
                e.wait_ge(s["rg_ln"], at(l, "rg_ln"))
                tt(ru, rln, xc, ALU.subtract).then_inc(s["rg_q"], 1)
                e.wait_ge(s["kk_rstd"], at(l, "kk_rstd"))
                link(tt(kk[:, :, 0:T], kk[:, :, 0:T], e1, ALU.mult))
                link(stt(bneg[:, :, 0:T], kk[:, :, 0:T], -1.0, bneg[:, :, 0:T], ALU.mult, ALU.mult))
                e.wait_ge(s["rows_kept"], at(l, "rows_kept", 1))
                for t in range(2):
                    e.wait_ge(s["rk_sum"], at(l, "rk_sum", t + 1))
                    link(tt(bonus[:, t, :], Q(2 + t), xs[:, 4 + t, 0:T], ALU.mult))

                e.wait_ge(s["rg_sq"], at(l, "rg_sq"))
                link(stt(rix, ru, 0.5, rix, ALU.mult, ALU.mult))
                for t in range(2):
                    e.tensor_tensor_scan(rh[:, t, 0:SEQ], ra[:, t, 0:SEQ], rix[:, t, 0:SEQ], 0.0, ALU.mult, ALU.add)
                    ins = e.tensor_tensor_scan(rh[:, t, SEQ:T], ra[:, t, SEQ + 3:XCW], rix[:, t, SEQ + 3:XCW],
                                               V(l, "h0", t), ALU.mult, ALU.add)
                link(ins)
                stt(hT[:, 0:2, :], gate, 0.5, rh, ALU.mult, ALU.mult).then_inc(s["rg_done"], 1)

                e.wait_ge(s["frames_zeroed"], at(l, "frames_zeroed"))
                chunks = lambda m: m.rearrange("p a (c n) -> p (a c) n", c=2)
                for g in range(NG):
                    cols = slice(GRP * g, GRP * g + GRP)
                    for t in range(2):
                        ins = e.tensor_tensor_scan(Lc[:, t, :], C("reset", 0, GRP), ell[:, t, cols], 0.0,
                                                   ALU.mult, ALU.add)
                    link(ins)
                    tt(dm, Lc, ell[:, :, cols], ALU.subtract)
                    end = chunks(Lc)[:, :, CH - 1:CH].to_broadcast([128, 4, CH])
                    tt(chunks(le), chunks(Lc), end, ALU.subtract).then_inc(s["decay_cum"], 1)
                    e.wait_ge(s["decay_exp"], at(l, "decay_exp", g + 1))
                    tt(af, kk[:, :, cols], en1, ALU.mult)
                    tt(rf, xs[:, 0:2, cols], en, ALU.mult)
                    tt(bf, bneg[:, :, cols], ep, ALU.mult)
                    tt(kf, xs[:, 2:4, cols], ep, ALU.mult)
                    tt(be, bneg[:, :, cols], ee, ALU.mult)
                    tt(ke, xs[:, 2:4, cols], ee, ALU.mult).then_inc(s["factors"], 1)
                    e.wait_ge(s["factors"], at(l, "factors", g + 1))
                    for h in range(2):
                        e.tensor_copy(AR[rows_of[h], h:4:2, 0:128], af[rows_of[h]])
                        ins = e.tensor_copy(AR[rows_of[h], h:4:2, 128:256], rf[rows_of[h]])
                    ins.then_inc(s["masked"], 1)
                    e.wait_ge(s["scores"], at(l, "scores", g + 1))
                    mask2 = bc(C("mask2", 0, 256), 4)
                    tt(X, pair(bank(6), 4), bc(C("lev1t", 0, 128), 4), ALU.mult)
                    tt(LG, pair(PS[:, 1024:2048], 4), mask2, ALU.mult)
                    tt(MG, pair(PS[:, 2048:3072], 4), mask2, ALU.mult).then_inc(s["scores_out"], 1)
                    e.wait_ge(s["scores_out"], at(l, "scores_out", g + 1))

                    def level(b):
                        return bc(C("lev", 128 * b, 128 * b + 128), 4)

                    LT = LG[:, :, 0:128]
                    link(tt(XT, LT, level(0), ALU.mult))
                    tt(X, X, bc(ident, 4), ALU.add)
                    tt(XT, XT, bc(ident, 4), ALU.add)
                    tt(TT, LT, level(1), ALU.mult).then_inc(s["lev_T"], 1)
                    for b in range(5):
                        n = 5 * g + b
                        e.wait_ge(s["lev_P"], at(l, "lev_P", n + 1))
                        e.tensor_copy(P, pair(bank(0), 4)).then_inc(s["lev_P_out"], 1)
                        if b < 4:
                            tt(TT, LT, level(b + 2), ALU.mult).then_inc(s["lev_T"], 1)
                        e.wait_ge(s["lev_X"], at(l, "lev_X", n + 1))
                        if b < 4:
                            tt(X, X, pair(bank(1), 4), ALU.add)
                        tt(XT, XT, pair(bank(2), 4), ALU.add).then_inc(s["lev_X_out"], 1)
                        e.wait_ge(s["lev_X_out"], at(l, "lev_X_out", n + 1))
                    e.wait_ge(s["ab"], at(l, "ab", g + 1))
                    flat2 = lambda m: m.rearrange("p a c n -> p (a c) n")
                    link(tt(flat2(Abd), pair(bank(4), 4), bc(bones, 4), ALU.mult))
                    for i in range(4):
                        m = flat2(Abd)[:, i, :]
                        stt(m, ident, K(8 + i), m, ALU.mult, ALU.add)
                    tt(flat2(Bbd), pair(bank(5), 4), bc(bones, 4), ALU.mult)
                    tt(rp, pair(bank(6, 0, 256)), rf, ALU.add)
                    e.tensor_copy(yl, pair(bank(6, 256, 512))).then_inc(s["ab_out"], 1)
                    e.wait_ge(s["ab_out"], at(l, "ab_out", g + 1))
                    nc_ = 2 if g < NG - 1 else 1
                    for c in range(nc_):
                        n = 2 * g + c
                        e.wait_ge(s["state_mm"], at(l, "state_mm", n + 1))
                        tt(S[:, 1 - c, :, :], pair(bank(7, 0, 256)), Bbd[:, :, c, :], ALU.add)\
                            .then_inc(s["state_out"], 1)
                    n = min(GRP, T - GRP * g)
                    tt(yrw[:, :, GRP * g:GRP * g + n], pair(bank(0, 0, 256))[:, :, 0:n], yl[:, :, 0:n], ALU.add).then_inc(s["y_out"], 1)

                for t in range(2):
                    e.wait_ge(s["gn_sum"], at(l, "gn_sum", t + 1))
                    ins = stt(yrw[:, t, 0:T], Q(t), -1.0 / 64, yrw[:, t, 0:T], ALU.mult, ALU.add)
                ins.then_inc(s["gn_mean"], 1)
                e.wait_ge(s["gn_rstd"], at(l, "gn_rstd"))
                link(tt(yrw[:, :, 0:T], yrw[:, :, 0:T], ell[:, :, 0:T], ALU.mult))
                for t in range(2):
                    ins = ts(yrw[:, t, 0:T], yrw[:, t, 0:T], V(l, "gn_w", t), V(l, "gn_b", t), ALU.mult, ALU.add)
                link(ins)
                link(tt(yrw[:, :, 0:T], yrw[:, :, 0:T], bonus, ALU.add))
                e.wait_ge(s["g_out"], at(l, "g_out"))
                for t in range(2):
                    ins = tt(hT[:, 2 + t, :], Q(2 + t), yrw[:, t, 0:T], ALU.mult)
                ins.then_inc(s["rw_y"], 1)

                e.wait_ge(stored["wkv"], 32 * (l + 1))
                for j in range(2):
                    e.tensor_copy(ak[rope, j, 0:T], kr[rope, :])
                    e.tensor_copy(ak[rope, j, T:KEYS], W("kr", 0, PAST, rope))
                e.wait_ge(s["lat_rstd"], at(l, "lat_rstd", 2))
                stt(ckv, ckv, V(l, "kv_norm"), ell[:, 1, 0:T], ALU.mult, ALU.mult).then_inc(s["ckv_n"], 1)
                for t in range(2):
                    ins = stt(cq[:, t, :], cq[:, t, :], V(l, "q_norm", t), ell[:, 0, 0:T], ALU.mult, ALU.mult)
                ins.then_inc(s["cq_n"], 1)

                units = [(h, b) for h in range(HEADS) for b in range(5)]

                def queries_out(h):
                    if h >= 2:
                        e.wait_ge(s["a_score"], at(l, "a_score", 5 * (h - 1)))
                    e.wait_ge(s["q_mm"], at(l, "q_mm", h + 1))
                    q = aq[:, h % 2, :]
                    e.tensor_copy(q[0:64, :], Q(0)[0:64, :])
                    tt(q[rope, :], Q(0)[rope, :], C("cos", 0, T, rope), ALU.mult)
                    tt(rs[rope, :], Q(1)[rope, :], C("sin", 0, T, rope), ALU.mult).then_inc(s["q_out"], 1)
                    e.wait_ge(s["q_out"], at(l, "q_out", 2 * h + 1))
                    tt(q[rope, :], q[rope, :], rs[rope, :], ALU.add).then_inc(s["q_out"], 1)
                    e.wait_ge(s["q_out"], at(l, "q_out", 2 * h + 2))

                def maximum(u, name, n, nk, scale):
                    e.wait_ge(s[name + "_score"], at(l, name + "_score", u + 1))
                    link(e.reduce_max(stat[0:n, 16 + u % 2:17 + u % 2], bank(4 + u % 2, 0, nk)[0:n, :], AX))
                    ts(stat[0:n, 18 + u % 2:19 + u % 2], stat[0:n, 16 + u % 2:17 + u % 2], -scale, None,
                       ALU.mult).then_inc(s[name + "_max"], 1)

                def normalise(u, name, p, n, nk):
                    e.wait_ge(s[name + "_exp"], at(l, name + "_exp", u + 1))
                    r = stat[0:n, 22 + u % 2:23 + u % 2]
                    link(e.reciprocal(r, stat[0:n, 20 + u % 2:21 + u % 2]))
                    m = p[0:n, u % 2, 0:nk]
                    ts(m, m, r, None, ALU.mult).then_inc(s[name + "_norm"], 1)

                def size(b):
                    return (128, 128 * b + 128) if b < 4 else (DEC, KEYS - SEQ)

                queries_out(0)
                for u in range(len(units) + 1):
                    if u < len(units):
                        h, b = units[u]
                        if b == 2 and h + 1 < HEADS:
                            queries_out(h + 1)
                        maximum(u, "a", *size(b), MLA_SCALE)
                    if u:
                        normalise(u - 1, "a", aP, *size(units[u - 1][1]))
                    if u in OUT_TILES_SPLIT:
                        split(tile_no(l, "out", OUT_TILES_SPLIT.index(u)))
                    for k in range(8):
                        if u == MIXED_AT[k] + 2:
                            mixed_lo(l, 8, k)
                mixed_lo(l, 8, 7)

                for i in range(8):
                    ahead(l, "out", i)
                    if i == 4:
                        e.wait_ge(mem_rstd, 1)
                        e.wait_ge(tokens_ld, 16 * (l + 1))
                        for k in range(8):
                            ins = stt(mem32[:, k, :], mem32[:, k, :], V(l, "g_memkv", k), mrs, ALU.mult, ALU.mult)
                        ins.then_inc(s["mem_scaled"], 1)
                    if i == 6:
                        e.wait_ge(s["mem_hi"], at(l, "mem_hi"))
                        tt(memL[:, :, :], mem32, plain(memH[:, :, :]), ALU.subtract).then_inc(s["memn"], 1)
                    residual(l, "out", i)
                for st in ("mk", "mv"):
                    for i in range(8):
                        ahead(l, st, i)
                        if st == "mk":
                            scaled_lo(l, 16, "g_mem", i)
                e.wait_ge(s["rms_rstd"], 3 * l + 2)
                for i in range(8):
                    ahead(l, "mq", i)
                    ps = take_tile(l, "mq", i)
                    tt(mq[:, i, :], ps, rs, ALU.mult).then_inc(evac["dve"], 1)
                munits = [(h, b) for h in range(MHEADS) for b in range(5)]
                for u in range(len(munits) + 1):
                    if u < len(munits):
                        maximum(u, "m", 128 if munits[u][1] < 4 else DEC, MEM, MEM_SCALE)
                    if u:
                        normalise(u - 1, "m", mP, 128 if munits[u - 1][1] < 4 else DEC, MEM)
                    if u >= 8 and (u - 8) % 5 == 0:
                        for k in (0, 1):
                            mixed_lo(l, 24, 2 * (u - 8) // 5 + k)
                for k in (6, 7):
                    mixed_lo(l, 24, k)

                for i in range(8):
                    ahead(l, "mo", i)
                    residual(l, "mo", i)
                for k in range(8):
                    scaled_lo(l, 32, "g_ffn", k)
                e.wait_ge(stored["mem"], 32 * (l + 1))

                def hid_lo(i):
                    e.wait_ge(s["hid_hi"], at(l, "hid_hi", i + 1))
                    g, k = i // 8 % 2, i % 8
                    tt(hidL[:, g, k, :], hid[:, g, k, :], plain(hidH[:, g, k, :]), ALU.subtract)\
                        .then_inc(s["hid_lo"], 1)

                for g in range(5):
                    if g < 4:
                        for i in range(8 * g, 8 * g + 8):
                            ahead(l, "f1", i)
                            if i == 0:
                                e.wait_ge(s["rms_rstd"], 3 * l + 3)
                            if i >= 16 and i % 8 == 0:
                                wait_tile(e, l, "f2", i - 9)
                            ps, m = take_tile(l, "f1", i), hid[:, g % 2, i % 8, :]
                            tt(m, ps, rs, ALU.mult).then_inc(evac["dve"], 1)
                            wait_evac(e, l, "f1", i)
                            stt(m, m, 0.0, m, ALU.max, ALU.mult).then_inc(s["hid_sq"], 1)
                            if i:
                                hid_lo(i - 1)
                        if g == 3:
                            hid_lo(31)
                    if g:
                        for i in range(8 * g - 8, 8 * g):
                            ahead(l, "f2", i)
                            residual(l, "f2", i)
                            if g == 4 and i % 8 and l + 1 < DEPTH:
                                scaled_lo(l + 1, 0, "g_mix", i % 8 - 1)
                if l + 1 < DEPTH:
                    scaled_lo(l + 1, 0, "g_mix", 7)
            e.wait_ge(s["rms_rstd"], 3 * DEPTH + 1)
            for k in range(8):
                stt(hT[:, k, :], xT[:, k, :], C("g_final", k, k + 1), rs, ALU.mult, ALU.mult).then_inc(y_ready, 1)


_VECTORS = {"g_mix": "norm_mix", "g_mem": "norm_mem", "g_memkv": "norm_mem_kv", "g_ffn": "norm_ffn",
            "conv_w": "rg_conv_w", "conv_b": "rg_conv_b", "rg_ba": "rg_ba", "rg_bx": "rg_bx", "w0": "rw_w0",
            "a0": "rw_a0", "lam": "rg_lambda", "mu": "rw_mu", "k_k": "rw_k_k", "k_a": "rw_k_a", "r_k": "rw_r_k",
            "gn_w": "rw_gn_w", "gn_b": "rw_gn_b", "q_norm": "mla_q_norm", "kv_norm": "mla_kv_norm",
            "h0": "state_rg_h", "shift": "state_rw_shift"}


def _constants(norm_final):
    f = np.float32
    c = np.zeros((128, NCST), f)

    def put(name, a, rows=slice(0, 128)):
        c[rows, CST[name]:CST[name] + a.shape[1]] = a

    i = np.arange(128)
    row, col = i[:, None], i[None, :]
    same = row // CH == col // CH
    put("ident", np.eye(128, dtype=f))
    put("ones", np.ones((128, 128), f))
    put("bones", same.astype(f))
    put("mask2", np.concatenate([same & (row < col), same & (row <= col)], 1).astype(f))
    put("maskL", (same & (col < row)).astype(f))
    levels = []
    for b in range(6):
        n = 1 << b
        levels.append((row // (2 * n) == col // (2 * n)) & (row // n % 2 == 0) & (col // n % 2 == 1))
    put("lev", np.concatenate(levels, 1).astype(f))
    put("lev1t", levels[0].T.astype(f))
    half = ROPE // 2
    inv = f(10000.0) ** (-np.arange(half, dtype=f) / f(half))
    pos = np.concatenate([np.arange(SEQ), PAST + np.arange(DEC)]).astype(f)
    ang = inv[:, None] * pos[None, :]
    put("cos", np.concatenate([np.cos(ang)] * 2).astype(f), slice(64, 96))
    put("sin", np.concatenate([-np.sin(ang), np.sin(ang)]).astype(f), slice(64, 96))
    put("reset", np.broadcast_to((i % CH != 0).astype(f), (128, 128)))
    put("maskq", (i < CH).astype(f)[None, :], slice(0, 1))
    put("maskk", np.where(i >= CH, f(NEG), f(0))[None, :], slice(0, 1))
    put("g_final", np.asarray(norm_final).reshape(8, 128).T)
    return c


def kernel(**inputs):
    import concourse.bacc as bacc
    from concourse.bass_utils import run_bass_kernel_spmd

    a = {k: np.asarray(v) for k, v in inputs.items()}
    f = np.float32
    L = DEPTH

    def rows(m):
        return np.moveaxis(m.reshape((-1, 128) + m.shape[1:]), 0, 1)

    vec = np.zeros((128, L, NV), f)
    for name, src in _VECTORS.items():
        v = a[src].reshape(L, -1, 128)
        vec[:, :, VEC[name]:VEC[name] + v.shape[1]] = v.transpose(2, 0, 1)
    conv = a["state_rg_conv"].reshape(L, 3, 2, 128).transpose(3, 0, 2, 1).reshape(128, L, 6)
    vec[:, :, VEC["conv_s"]:VEC["conv_s"] + 6] = conv

    lw = np.zeros((L, 128, NLW), f)

    def put(name, at, m, r=slice(0, 128)):
        lw[:, r, LW[name] + at:LW[name] + at + m.shape[-1]] = m

    for name, src in (("wa", "rg_wa"), ("wx", "rg_wx")):
        for b in range(4):
            put(name, 64 * b, a[src][:, b], slice(64 * (b % 2), 64 * (b % 2) + 64))
    put("low", 0, a["rw_w2"], slice(0, 32))
    put("low", 0, a["rw_a2"], slice(32, 64))
    put("low", 0, a["rw_g2"], slice(64, 128))
    uq = a["mla_w_uq"].reshape(L, 2, 128, HEADS, QKD).transpose(0, 2, 1, 3, 4)
    put("uq", 0, uq.reshape(L, 128, -1))
    half = ROPE // 2
    uqs = np.concatenate([uq[..., NOPE + half:], uq[..., NOPE:NOPE + half]], -1)
    put("uqs", 0, uqs.reshape(L, 128, -1))
    put("uk", 0, a["mla_w_uk"].reshape(L, 128, -1))
    put("uv", 0, a["mla_w_uv"].reshape(L, 128, -1))
    put("ckv", 0, a["cache_mla_ckv"][:, 0].transpose(0, 2, 1))
    put("kr", 0, a["cache_mla_krope"][:, 0].transpose(0, 2, 1), slice(64, 96))
    st = a["state_rw_wkv"][:, 0].transpose(0, 1, 3, 2)
    for h in range(4):
        put("S0", 128 * (h // 2) + 64 * (h % 2), st[:, h], slice(64 * (h % 2), 64 * (h % 2) + 64))

    wall = np.zeros((L, NT, 128, 8, 128), f)
    w_in = a["w_in"]
    rw0, mla0 = 512, 512 + 896
    order = [(rw0 + 128 * i, 128) for i in range(7)] + [(mla0, 128), (mla0 + 128, 128), (mla0 + 256, 128),
             (mla0 + 384, ROPE), (None, ROPE), (0, 128), (128, 128), (256, 128), (384, 128)]
    swapped = np.concatenate([w_in[:, :, mla0 + 384 + half:mla0 + 416], w_in[:, :, mla0 + 384:mla0 + 384 + half]], 2)
    mats = {"out": a["w_out"], "mk": a["mem_w_k"].reshape(L, D, D), "mv": a["mem_w_v"].reshape(L, D, D),
            "mq": a["mem_w_q"].reshape(L, D, D), "mo": a["mem_w_o"].reshape(L, D, D), "f1": a["ffn_w1"],
            "f2": a["ffn_w2"]}
    for t, (stg, i) in enumerate(STREAM):
        w, first, k = 128, 0, 0
        if stg == "in":
            at, w = order[i]
            m = swapped if at is None else w_in[:, :, at:at + w]
            first = NOPE if w == ROPE else 0
        else:
            i, k = (i % 8, i // 8) if stg == "f2" else (i, 0)
            m = mats[stg][:, D * k:D * k + D, 128 * i:128 * i + 128]
        wall[:, t, :, :, first:first + w] = m.reshape(L, 8, 128, w).transpose(0, 2, 1, 3)
    wall = wall.reshape(L, NT, 128, 1024)

    x = np.concatenate([a["x_prompt"][0], a["x_sample"][0]], 0)
    arrays = {
        "wall": wall, "lw_in": lw, "vec_in": vec, "cst_in": _constants(a["norm_final"]),
        "x_in": rows(np.ascontiguousarray(x.T)), "mem_in": rows(np.ascontiguousarray(a["mem_prompt"][0].T)),
        "mks_in": a["cache_mem_k"][:, 0].reshape(L, MEM, 8, 128).transpose(0, 3, 2, 1),
        "mvs_in": a["cache_mem_v"][:, 0].reshape(L, 2, 128, D).transpose(0, 2, 1, 3),
    }
    arrays = {k: np.ascontiguousarray(v) for k, v in arrays.items()}
    nc = bacc.Bacc("TRN2", target_bir_lowering=False, num_devices=1)
    F32 = mybir.dt.float32
    ins = [nc.dram_tensor(k, v.shape, F32, kind="ExternalInput").ap() for k, v in arrays.items()]
    outs = {k: nc.dram_tensor(k, shape, F32, kind="ExternalOutput").ap() for k, shape in OUTS}
    build(nc, *ins, outs)
    r = run_bass_kernel_spmd(nc, [arrays], core_ids=[0]).results[0]
    o = {k: np.asarray(r[k]).reshape(shape) for k, shape in OUTS}

    y = o["y_out"].transpose(2, 1, 0).reshape(T, D)
    last = o["last_out"]
    shift = last[:, :, 0:14].reshape(L, 128, RWT, 2).transpose(3, 0, 2, 1).reshape(2, L, 1, RWT * 128)
    conv = last[:, :, 14:26].reshape(L, 128, 2, 2, 3).transpose(3, 0, 4, 2, 1).reshape(2, L, 1, 3, 256)
    h = last[:, :, 26:30].reshape(L, 128, 2, 2).transpose(3, 0, 2, 1).reshape(2, L, 1, 256)
    wkv = np.zeros((2, L, 1, 4, 64, 64), f)
    for i in range(4):
        r_ = slice(64 * (i % 2), 64 * (i % 2) + 64)
        wkv[:, :, 0, i] = o["wkv_out"][:, r_, :, i // 2, r_].transpose(2, 0, 3, 1)
    ckv = o["ckv_out"].transpose(0, 2, 1)[:, None]
    kr = o["kr_out"].transpose(0, 2, 1)[:, None]
    mk = o["memk_out"].transpose(0, 3, 2, 1).reshape(L, 1, MEM, 4, 256)
    mv = o["memv_out"].transpose(0, 2, 1, 3).reshape(L, 1, MEM, 4, 256)
    got = (y[None, :SEQ], y[None, SEQ:], conv[0], h[0], shift[0], wkv[0], ckv[:, :, :SEQ], kr[:, :, :SEQ], mk, mv,
           conv[1], h[1], shift[1], wkv[1], ckv[:, :, SEQ:], kr[:, :, SEQ:])
    return tuple(np.ascontiguousarray(g) for g in got)
```

```python
import numpy as np
import concourse.bass as bass
from concourse import mybir
from contextlib import ExitStack

DEPTH, SEQ, DEC, PAST, D = 2, 512, 32, 256, 1024
T = SEQ + DEC
HALF = T // 2
KT = D // 128
MEM, MHEADS = 256, 4
RG_COLS, CONV = 2, 4
RGW = (CONV - 1) + SEQ + (CONV - 1) + DEC
XCW = RGW - (CONV - 1)
XH = XCW // 2 + 1
RWT = 7
RWW = 1 + SEQ + 1 + DEC
CH = 64
GRP = 128
NG = SEQ // GRP + 1
FR = NG * GRP
HEADS, NOPE, ROPE = 8, 64, 32
QKD = NOPE + ROPE
KEYS = T + PAST
MLA_SCALE = float(QKD) ** -0.5
MEM_SCALE = 256.0 ** -0.5
FF = 32
EPS, GN_EPS, L2_EPS = 1e-6, 64e-5, 1e-12
EXP_HALF = float(np.exp(-0.5))
GELU_C = float(np.sqrt(2.0 / np.pi))
NEG = -1e30

VEC = {}
_n = 0
for _name, _w in (("g_mix", 8), ("g_mem", 8), ("g_memkv", 8), ("g_ffn", 8), ("conv_w", 8), ("conv_b", 2),
                  ("rg_ba", 2), ("rg_bx", 2), ("w0", 2), ("a0", 2), ("lam", 2), ("mu", 7), ("k_k", 2), ("k_a", 2),
                  ("r_k", 2), ("gn_w", 2), ("gn_b", 2), ("q_norm", 2), ("kv_norm", 1), ("h0", 2),
                  ("shift", 7), ("conv_s", 6)):
    VEC[_name] = _n
    _n += _w
NV = _n

LW = {}
_n = 0
for _name, _w in (("wa", 256), ("wx", 256), ("low", 256), ("uq", 2 * HEADS * 128),
                  ("uk", HEADS * NOPE), ("uv", HEADS * 64), ("ckv", PAST), ("kr", PAST), ("S0", 256)):
    LW[_name] = _n
    _n += _w
NLW = _n

CST = {}
_n = 0
for _name, _w in (("ident", 128), ("ones", 128), ("bones", 128), ("mask2", 256), ("maskL", 128), ("lev", 6 * 128),
                  ("lev1t", 128), ("cos", T), ("sin", T), ("reset", GRP), ("maskq", 128), ("maskk", 128), ("g_final", 8)):
    CST[_name] = _n
    _n += _w
NCST = _n

N_IN = 15
STREAM = [(st, i) for st, n in (("in", N_IN), ("out", 8), ("mk", 8), ("mv", 8), ("mq", 8), ("mo", 8)) for i in range(n)]
for _g in (0, 1, 2, 3, 4):
    if _g < 4:
        STREAM += [("f1", 8 * _g + i) for i in range(8)]
    if _g > 0:
        STREAM += [("f2", 8 * (_g - 1) + i) for i in range(8)]
NT = len(STREAM)
TILE = {t: i for i, t in enumerate(STREAM)}
RING = 3
SPLIT = 3
EVAC_ENGINE = {st: "act" if st in ("mk", "mv") else "dve" for st, _ in STREAM}
EVACUATED = [t for t in STREAM if t[0] != "mv" or t[1] % 2]
EVAC_PER_LAYER = {e: sum(EVAC_ENGINE[t[0]] == e for t in EVACUATED) for e in ("act", "dve")}
RUNS = [(0, N_IN), (N_IN, NT + N_IN), (NT + N_IN, 2 * NT)]


def evac_value(layer, tile):
    eng = EVAC_ENGINE[STREAM[tile][0]]
    return eng, layer * EVAC_PER_LAYER[eng] + sum(
        EVAC_ENGINE[t[0]] == eng and t in EVACUATED for t in STREAM[:tile + 1])


OUTS = [("y_out", (128, 8, T)), ("last_out", (DEPTH, 128, 30)), ("wkv_out", (DEPTH, 128, 2, 2, 128)),
        ("ckv_out", (DEPTH, 128, T)), ("kr_out", (DEPTH, ROPE, T)),
        ("memk_out", (DEPTH, 128, 8, MEM)), ("memv_out", (DEPTH, 128, 2, D))]

UNITS = [(h, b) for h in range(HEADS) for b in range(5)]
PIECES = [(0, 256), (256, 512), (512, T)]
USES = [("v", j) for j in range(7)] + [("p", 5 * 0 + p) for p in range(5)]
for _u, (_h, _b) in enumerate(UNITS):
    USES.append(("s", _u))
    if _h + 1 < HEADS:
        USES.append(("p", 5 * (_h + 1) + _b))

MUNITS = [(h, b) for h in range(MHEADS) for b in range(5)]
MEM_STEPS = [("", 0)] * 18
for _u, (_h, _b) in enumerate(MUNITS):
    MEM_STEPS += [("score", _u), ("turn", _u - 1) if _u else ("", 0),
                  ("weigh", 4 * (_h - 1) + _b) if _h and _b < 4 else ("", 0)] + [("", 0)] * (_b == 4)
MEM_STEPS += [("turn", len(MUNITS) - 1)] + [("weigh", 4 * MHEADS - 4 + _i) for _i in range(4)]

NSTATE = 2 * NG - 1
PER_LAYER = {
    "sq_ready": 24, "sq_added": 21, "rms_sum": 3, "rms_rstd": 3, "h_hi": 40, "h_ready": 40,
    "frames_zeroed": 1, "rows_kept": 2,
    "rg_conv": 1, "rg_z": 4, "rg_gates": 1, "rg_gelu_in": 1, "rg_gelu": 1, "rg_ix": 1, "rg_ln": 1, "rg_q": 1,
    "rg_sq": 1, "rg_done": 1,
    "low_ready": 1, "low_tanh": 1, "low_z": 4, "low_gate": 4, "kk_raw": 1, "kk_sq": 1, "kk_sum": 2,
    "kk_rstd": 1, "rk_ready": 1, "rk_sum": 2,
    "decay_cum": NG, "decay_exp": NG, "factors": NG, "masked": NG, "tok_T": NG, "tok_out": NG, "scores_t": NG,
    "scores_t_out": NG, "scores": NG,
    "scores_out": NG, "mv": NG, "mv_out": NG, "lev_T": 5 * NG, "lev_P": 5 * NG, "lev_P_out": 5 * NG,
    "lev_X": 5 * NG, "lev_X_out": 5 * NG, "xr": NG, "xr_out": NG, "ab": NG, "ab_out": NG,
    "state_mm": NSTATE, "state_out": NSTATE, "y_out": NG,
    "gn_sum": 4, "gn_mean": 1, "gn_sq": 1, "gn_rstd": 1, "g_out": 1, "rw_y": 1,
    "lat_sq": 1, "lat_sum": 1, "lat_rstd": 1, "cq_n": 1, "ckv_n": 1, "kr_ready": 1,
    "v_mm": 7, "v_out": 7, "q_mm": 3 * HEADS, "q_read": 3 * HEADS, "nope_out": 3 * HEADS, "q_out": 3 * HEADS, "k_mm": 2 * HEADS,
    "k_out": 2 * HEADS,
    "a_score": 40, "a_max": 40, "a_exp": 40, "a_norm": 40, "a_T": 40, "a_T_out": 40, "a_pv": 40, "a_o": 40,
    "m_score": 20, "m_max": 20, "m_exp": 20, "m_norm": 20, "m_T": 20, "m_T_out": 20, "m_pv": 16, "m_o": 16,
    "mem_scaled": 1, "mem_hi": 1, "memn": 1, "hid_sq": 32, "hid_hi": 32, "hid_lo": 32,
}


def build(nc, wall, lw_d, vec_d, cst_d, x_d, mem_d, mks_d, mvs_d, outs):
    F32, F32R = mybir.dt.float32, mybir.dt.float32r
    ALU = mybir.AluOpType
    ACT = mybir.ActivationFunctionType
    AX = mybir.AxisListType.X
    ctx = ExitStack()
    with ctx:
        base = nc.sbuf_base + -nc.sbuf_base % 32

        def place(name, col, shape, dtype):
            return nc.alloc_sbuf_tensor_at(name, shape, dtype, offset=base + 4 * col)

        def sem(name):
            return ctx.enter_context(nc.semaphore(name))

        ARENA = 53200
        col = {}

        def carve(at, limit, **shapes):
            got = []
            for name, shape in shapes.items():
                col[name] = at
                got.append(place(name, at, (128,) + shape, F32)[(slice(None),) * (len(shape) + 1)])
                at += int(np.prod(shape))
                at += -at % 8
            assert at <= limit, (at, limit)
            col["end"] = at
            return got

        xT, hT, ring, lw, vec, derv, cst, rs, stat, last_rows, mrs = carve(
            0, ARENA, xT=(8, T), hT=(8, T), ring=(RING, 8, 128), lw=(NLW,), vec=(DEPTH, NV), derv=(DEPTH, 12),
            cst=(NCST,), rs=(T,), stat=(64,), last_rows=(30,), mrs=(MEM,))
        FIX = col["end"]
        hL = place("hL", col["hT"], [128, 8, T], F32R)
        hH = place("hH", FIX, [128, 8, T], F32R)
        wH = place("wH", FIX + 8 * T, [128, SPLIT, 8, 128], F32R)
        wL = place("wL", FIX + 8 * T + SPLIT * 1024, [128, SPLIT, 8, 128], F32R)
        MIX = FIX + 8 * T + 2 * SPLIT * 1024
        xs, kk, cq, ckv, kr, rg, gate, raw, ell, bneg, aq, ak, aP, aPT = carve(
            MIX, ARENA, xs=(RWT, FR), kk=(2, FR), cq=(2, T), ckv=(T,), kr=(T,), rg=(2, RGW), gate=(2, T),
            raw=(RWT, RWW), ell=(2, FR), bneg=(2, FR), aq=(2, T), ak=(2, KEYS), aP=(3, 512), aPT=(2, 512))
        av, bonus = carve(col["rg"], col["ell"], av=(7, 512), bonus=(2, T))
        ra, ru, rln, rix, gx, rh = carve(FIX, MIX, ra=(2, XCW), ru=(2, XCW), rln=(2, XCW), rix=(2, XCW),
                                         gx=(2, T), rh=(2, T))
        lat_sq, lat_r = carve(col["aP"], ARENA, lat_sq=(3, T), lat_r=(2, T))
        xc, = carve(col["ak"], ARENA, xc=(2, XCW))
        en1, en, ep, ee, bf, be, AR, LG, MG, X, XT, P, TT, BE, KE, S, Rt, Vm, Wm, Ym, yl = carve(
            FIX, MIX, en1=(2, 128), en=(2, 128), ep=(2, 128), ee=(2, 128), bf=(2, 128), be=(2, 128),
            AR=(4, 256), LG=(4, 256), MG=(4, 256), X=(4, 128), XT=(4, 128), P=(4, 128), TT=(4, 128),
            BE=(2, 2, 128), KE=(2, 2, 128), S=(2, 2, 128), Rt=(4, 128), Vm=(2, 192), Wm=(2, 192), Ym=(2, 192),
            yl=(2, 128))
        af, rf, kf, ke, Lc, dm, le, rp = en1, en, ep, ee, en, en1, ee, bf
        Abd, Bbd = (m.rearrange("p (a c) n -> p a c n", a=2) for m in (TT, P))
        yrw = hT[:, 2:4, :]
        e1, e2 = hT[:, 4:6, :], hT[:, 6:8, :]
        mem32, = carve(MIX, ARENA, mem32=(8, MEM))
        msq, = carve(col["kk"], col["cq"], msq=(2, MEM))
        memL = place("memL", MIX, [128, 8, MEM], F32R)
        memH = place("memH", MIX + 8 * MEM, [128, 8, MEM], F32R)
        oT, mq, mks, mvs, mkp, mvp, mP, mPT, sq = carve(
            MIX, ARENA, oT=(8, T), mq=(8, T), mks=(8, MEM), mvs=(2, D), mkp=(8, MEM), mvp=(2, D), mP=(3, 256),
            mPT=(2, 2, T), sq=(2, T))
        hid, = carve(MIX, col["sq"], hid=(2, 8, T))
        hidL = place("hidL", MIX, [128, 2, 8, T], F32R)
        hidH = place("hidH", MIX + 16 * T, [128, 2, 8, T], F32R)
        PS = ctx.enter_context(nc.psum_tensor("PS", [128, 8 * 512], F32))

        def C(name, a, b, rows=slice(0, 128)):
            return cst[rows, CST[name] + a:CST[name] + b]

        def V(l, name, i=0):
            return vec[:, l, VEC[name] + i:VEC[name] + i + 1]

        def W(name, a, b, rows=slice(0, 128)):
            return lw[rows, LW[name] + a:LW[name] + b]

        def bc(ap, n):
            return ap.unsqueeze(1).to_broadcast([128, n, ap.shape[-1]])

        def plain(ap):
            return ap.bitcast(F32)

        def pair(ap, n=2):
            return ap.rearrange("p (a b) -> p a b", a=n)

        ident, ones, bones = (C(n, 0, 128) for n in ("ident", "ones", "bones"))
        rows_of = [slice(0, 64), slice(64, 128)]
        rope, swap = slice(64, 96), slice(96, 128)
        C_TINY, C_EPS, C_L2, C_GN, C_ONE = 59, 60, 61, 62, 63

        def K(i):
            return stat[:, i:i + 1]

        def Q(q, n=T):
            return PS[:, q * 1024 + 512 - (n + 1) // 2:q * 1024 + 512 - (n + 1) // 2 + n]

        def bank(i, a=0, b=512):
            return PS[:, i * 512 + a:i * 512 + b]

        w_load = [sem(f"w_load{i}") for i in range(RING)]
        pe_done = sem("pe_done")
        w_hi, w_lo = sem("w_hi"), sem("w_lo")
        evac = {"act": sem("evac_act"), "dve": sem("evac_dve")}
        vec_ld, cst_ld, x_ld = sem("vec_ld"), sem("cst_ld"), [sem(f"x_ld{i}") for i in range(4)]
        lw_ld, mem_ld, tokens_ld = sem("lw_ld"), sem("mem_ld"), sem("tokens_ld")
        msq_ready, msq_added, mem_sum, mem_rstd = (sem(n) for n in ("msq_ready", "msq_added", "mem_sum", "mem_rstd"))
        stored = {n: sem("stored_" + n) for n in ("last", "wkv", "latent", "mem", "y")}
        y_ready = sem("y_ready")
        vstep, astep, setup_abs, setup_exp, setup_vec = (
            sem(n) for n in ("vstep", "astep", "setup_abs", "setup_exp", "setup_vec"))
        s = {n: sem(n) for n in PER_LAYER}
        before = dict(sq_ready=8, sq_added=7, rms_sum=1, rms_rstd=1)

        def at(l, name, i=1):
            return before.get(name, 0) + l * PER_LAYER[name] + i

        def tile_no(l, st, i=0):
            return l * NT + TILE[(st, i)]

        def wait_tile(e, l, st, i):
            e.wait_ge(pe_done, tile_no(l, st, i) + 1)

        def wait_evac(e, l, st, i):
            eng, v = evac_value(l, TILE[(st, i)])
            e.wait_ge(evac[eng], v)

        def bank_of(use):
            return 4 + USES.index(use) % 2

        def wait_bank(e, l, use):
            i = USES.index(use)
            if i < 2:
                return
            kind, n = USES[i - 2]
            if kind == "v":
                e.wait_ge(s["v_out"], at(l, "v_out", n + 1))
            elif kind == "s":
                e.wait_ge(s["a_exp"], at(l, "a_exp", n + 1))
            elif n % 5 < 3:
                e.wait_ge(s["q_read"], at(l, "q_read", 3 * (n // 5) + n % 5 + 1))
                e.wait_ge(s["nope_out"], at(l, "nope_out", 3 * (n // 5) + n % 5 + 1))
            else:
                e.wait_ge(s["k_out"], at(l, "k_out", 2 * (n // 5) + n % 5 - 2))

        def in_turn(*programs):
            left = list(programs)
            while left:
                left = [p for p in left if next(p, "end") != "end"]

        def values_bank(l, i):
            return 6 if i // 2 % 2 else 2 * (tile_no(l, "mv") % 2)

        def split_now(n):
            return any(a + 2 <= n < b for a, b in RUNS)

        block = ctx.enter_context(nc.Block())

        @block.sync
        def _(e):
            def load(n):
                if n >= RING:
                    e.wait_ge(w_lo, n - RING + 1)
                e.dma_start(ring[:, n % RING, :, :].rearrange("p a b -> p (a b)"),
                            wall[n // NT, n % NT]).then_inc(w_load[n % RING], 16)

            e.dma_start(vec[:, :, :], vec_d).then_inc(vec_ld, 16)
            load(0)
            for i in range(4):
                e.dma_start(xT[:, 2 * i:2 * i + 2, :], x_d[:, 2 * i:2 * i + 2, :]).then_inc(x_ld[i], 16)
            load(1)
            e.dma_start(cst[:, :], cst_d).then_inc(cst_ld, 16)
            for n in range(2, DEPTH * NT):
                load(n)
            for k in range(8):
                e.wait_ge(y_ready, k + 1)
                e.dma_start(outs["y_out"][:, k, :], hT[:, k, :]).then_inc(stored["y"], 16)
            e.wait_ge(stored["y"], 16 * 8)

        @block.gpsimd
        def _(e):
            def put(kind, out, src):
                e.dma_start(out, src).then_inc(stored[kind], 16)

            def add_squares(r):
                for k in range(1, 8):
                    e.wait_ge(s["sq_ready"], 8 * r + k + 1)
                    if k > 1:
                        e.wait_ge(s["sq_added"], 7 * r + k - 1)
                    e.tensor_tensor(sq[:, 0, :], sq[:, 0, :], sq[:, 1, :], ALU.add).then_inc(s["sq_added"], 1)

            add_squares(0)
            e.dma_start(lw[:, :], lw_d[0]).then_inc(lw_ld, 16)
            for l in range(DEPTH):
                if l:
                    e.wait_ge(pe_done, l * NT)
                    e.wait_ge(stored["last"], 16 * l)
                e.memset(xs[:, :, T:FR], 0.0)
                e.memset(ell[:, :, T:FR], 0.0)
                e.memset(bneg[:, :, T:FR], 0.0)
                e.memset(kk[:, :, T:FR], 0.0)
                wait_evac(e, l, "in", N_IN - 1)
                e.tensor_copy(pair(last_rows[:, 0:14], 7), raw[:, :, SEQ:RWW:RWW - 1 - SEQ])\
                    .then_inc(s["rows_kept"], 1)
                for c, a in ((0, SEQ), (3, RGW - 3)):
                    e.tensor_copy(pair(last_rows[:, 14:26])[:, :, c:c + 3], rg[:, :, a:a + 3])
                e.wait_ge(s["rg_done"], at(l, "rg_done"))
                e.tensor_copy(pair(last_rows[:, 26:30]), rh[:, :, SEQ - 1:T:DEC]).then_inc(s["rows_kept"], 1)
                e.wait_ge(s["rows_kept"], at(l, "rows_kept", 2))
                put("last", outs["last_out"][l], last_rows[:, :])
                for m in (AR, BE, KE):
                    e.memset(m, 0.0)
                for m in (Vm, Wm, Ym):
                    e.memset(m[:, :, 64:128], 0.0)
                e.memset(S[:, 0, :, :], 0.0).then_inc(s["frames_zeroed"], 1)
                e.wait_ge(s["kr_ready"], at(l, "kr_ready"))
                put("latent", outs["kr_out"][l], kr[rope, :])
                e.wait_ge(s["ckv_n"], at(l, "ckv_n"))
                put("latent", outs["ckv_out"][l], ckv)
                for g in range(NG):
                    e.wait_ge(s["scores_t_out"], at(l, "scores_t_out", g + 1))
                    for b in range(5):
                        n = 5 * g + b
                        if b:
                            e.wait_ge(s["lev_P"], at(l, "lev_P", n))
                        elif g:
                            e.wait_ge(s["y_out"], at(l, "y_out", g))
                        e.tensor_tensor(TT, LG[:, :, 0:128], bc(C("lev", 128 * b + 128, 128 * b + 256), 4),
                                        ALU.mult).then_inc(s["lev_T"], 1)
                e.wait_ge(s["state_out"], at(l, "state_out", NSTATE - 1))
                put("wkv", outs["wkv_out"][l, :, 0], S[:, 0, :, :])
                e.wait_ge(s["state_out"], at(l, "state_out", NSTATE))
                put("wkv", outs["wkv_out"][l, :, 1], S[:, 1, :, :])
                e.wait_ge(s["rw_y"], at(l, "rw_y"))
                e.dma_start(mem32, mem_d).then_inc(tokens_ld, 16)
                if l == 0:
                    for k in range(1, 8):
                        e.wait_ge(msq_ready, k + 1)
                        if k > 1:
                            e.wait_ge(msq_added, k - 1)
                        e.tensor_tensor(msq[:, 0, :], msq[:, 0, :], msq[:, 1, :], ALU.add).then_inc(msq_added, 1)
                wait_tile(e, l, "out", 0)
                e.wait_ge(stored["latent"], 32 * (l + 1))
                if l + 1 < DEPTH:
                    e.dma_start(lw[:, :], lw_d[l + 1]).then_inc(lw_ld, 16)
                e.dma_start(mks[:, :, :], mks_d[l]).then_inc(mem_ld, 16)
                e.dma_start(mvs[:, :, :], mvs_d[l]).then_inc(mem_ld, 16)
                add_squares(3 * l + 1)
                wait_evac(e, l, "mk", 7)
                put("mem", outs["memk_out"][l], mkp)
                wait_evac(e, l, "mv", 7)
                put("mem", outs["memv_out"][l], mvp)
                add_squares(3 * l + 2)
                add_squares(3 * l + 3)
            for kind, n in (("last", 1), ("wkv", 2), ("latent", 2), ("mem", 2)):
                e.wait_ge(stored[kind], 16 * n * DEPTH)

        @block.tensor
        def _(e):
            def mm(out, a, b, start=True, stop=True):
                return e.matmul(out, lhsT=a, rhs=b, start=start, stop=stop)

            def halves(out, a, b, start=True, stop=True, n=T):
                h = (n + 1) // 2
                mm(out[:, 0:h], a, b[:, 0:h], start, stop)
                return mm(out[:, h:n], a, b[:, h:n], start, stop)

            def rms(r):
                e.wait_ge(s["sq_added"], 7 * (r + 1))
                halves(Q(2), ones, sq[:, 0, :]).then_inc(s["rms_sum"], 1)

            def three(product, out, a, b, first, last):
                product(out, a[0], b[0], first, False)
                product(out, a[0], b[1], False, False)
                return product(out, a[1], b[0], False, last)

            def dense(*args, **kw):
                for _ in dense_steps(*args, **kw):
                    pass

            def dense_steps(l, st, group=None, h_from=0):
                for i in range(*((0, {"in": N_IN}.get(st, 8)) if group is None else (8 * group, 8 * group + 8))):
                    t = TILE[(st, i)]
                    n = l * NT + t
                    slot = n % SPLIT
                    e.wait_ge(w_lo, n + 1)
                    if n >= 2:
                        eng, v = evac_value((n - 2) // NT, (n - 2) % NT)
                        e.wait_ge(evac[eng], v)
                    if st == "f2" and i % 8 == 0:
                        e.wait_ge(s["hid_lo"], at(l, "hid_lo", i + 8))
                    out = Q(n % 2)
                    if st == "mv":
                        w = [p[:, slot].rearrange("p (a b) n -> p a (b n)", b=2) for p in (wH, wL)]
                        for m in range(2):
                            for k in range(4 * (i % 2), 4 * (i % 2) + 4):
                                last = three(mm, bank(values_bank(l, i) + m, 0, 256),
                                             [p[:, k, 128 * m:128 * m + 128] for p in (memH, memL)],
                                             [p[:, k % 4, :] for p in w], k == 0, k == 7)
                        last.then_inc(pe_done, 1)
                        continue
                    for k in range(8):
                        w = [p[:, slot, k, :] for p in (wH, wL)]
                        if st == "mk":
                            last = three(mm, bank(2 * (n % 2), 0, MEM), w, [p[:, k, :] for p in (memH, memL)],
                                         k == 0, k == 7)
                        elif st == "f2":
                            last = three(halves, out, w, [p[:, i // 8 % 2, k, :] for p in (hidH, hidL)],
                                         k == 0, k == 7)
                        else:
                            if i == 0:
                                e.wait_ge(s["h_ready"], at(l, "h_ready", h_from + k + 1))
                            last = three(halves, out, w, [p[:, k, :] for p in (hH, hL)], k == 0, k == 7)
                        if k == 7:
                            last.then_inc(pe_done, 1)
                        yield
                    if (st, i) == ("in", 0):
                        rms(3 * l)
                    if (st, i) == ("in", 12):
                        e.wait_ge(s["lat_sq"], at(l, "lat_sq"))
                        for t in range(2):
                            halves(Q(2), ones, lat_sq[:, t, :], t == 0, t == 1)
                        halves(Q(3), ones, lat_sq[:, 2, :]).then_inc(s["lat_sum"], 1)
                    if (st, i) == ("out", 1) and l == 0:
                        e.wait_ge(msq_added, 7)
                        mm(bank(6, 0, MEM), ones, msq[:, 0, :]).then_inc(mem_sum, 1)
                    if (st, i) == ("mk", 3):
                        rms(3 * l + 1)
                    if (st, i) == ("f1", 0):
                        rms(3 * l + 2)

            e.wait_ge(cst_ld, 16)
            for l in range(DEPTH):
                dense(l, "in", h_from=0)

                e.wait_ge(lw_ld, 16 * (l + 1))
                e.wait_ge(s["rg_conv"], at(l, "rg_conv"))
                wait_evac(e, l, "in", N_IN - 1)
                e.wait_ge(s["lat_rstd"], at(l, "lat_rstd"))
                for g, name in enumerate(("wa", "wx")):
                    for t in range(2):
                        halves(Q(2 * g + t, XCW), W(name, 128 * t, 128 * t + 128), xc[:, t, :],
                               n=XCW).then_inc(s["rg_z"], 1)

                e.wait_ge(s["rg_gates"], at(l, "rg_gates"))
                e.wait_ge(s["low_tanh"], at(l, "low_tanh"))
                for m in range(2):
                    rows = slice(32 * m, 32 * m + 32)
                    for t in range(2):
                        halves(Q(2 * m + t), W("low", 128 * t, 128 * t + 128, rows),
                               xs[rows, 6, 0:T]).then_inc(s["low_z"], 1)
                e.wait_ge(s["low_gate"], at(l, "low_gate", 4))
                e.wait_ge(s["kk_sq"], at(l, "kk_sq"))
                for t in range(2):
                    halves(Q(t), bones, e1[:, t, :]).then_inc(s["kk_sum"], 1)
                e.wait_ge(s["rk_ready"], at(l, "rk_ready"))
                for t in range(2):
                    halves(Q(2 + t), bones, e2[:, t, :]).then_inc(s["rk_sum"], 1)

                e.wait_ge(s["rg_done"], at(l, "rg_done"))
                def recurrence():
                    for g in range(NG):
                        e.wait_ge(s["masked"], at(l, "masked", g + 1))
                        if g:
                            e.wait_ge(s["y_out"], at(l, "y_out", g))
                        for t in range(2):
                            e.transpose(bank(0, 128 * t, 128 * t + 128), xs[:, 4 + t, GRP * g:GRP * g + GRP], ident)
                            e.transpose(bank(0, 256 + 128 * t, 384 + 128 * t), af[:, t, :], ident)
                            e.transpose(bank(1, 128 * t, 128 * t + 128), be[:, t, :], ident)
                            last = e.transpose(bank(1, 256 + 128 * t, 384 + 128 * t), ke[:, t, :], ident)
                        last.then_inc(s["tok_T"], 1)
                        for u in range(4):
                            last = mm(PS[:, 1024 + 256 * u:1280 + 256 * u], bf[:, u // 2, :], AR[:, u, :])
                        last.then_inc(s["scores_t"], 1)
                        yield
                        e.wait_ge(s["tok_out"], at(l, "tok_out", g + 1))
                        for u in range(4):
                            mm(PS[:, 256 * u:256 * u + 256], kf[:, u // 2, :], AR[:, u, :])
                        e.wait_ge(s["scores_t_out"], at(l, "scores_t_out", g + 1))
                        for u in range(4):
                            last = mm(bank(2, 128 * u, 128 * u + 128), AR[:, u, 0:128], bf[:, u // 2, :])
                        last.then_inc(s["scores"], 1)
                        yield
                        e.wait_ge(s["scores_out"], at(l, "scores_out", g + 1))
                        for u in range(4):
                            last = mm(bank(3, 64 * u, 64 * u + 64), MG[:, u, 0:128],
                                      Vm[:, u // 2, 128 * (u % 2):128 * (u % 2) + 64])
                        last.then_inc(s["mv"], 1)
                        for b in range(5):
                            n = 5 * g + b
                            e.wait_ge(s["lev_T"], at(l, "lev_T", n + 1))
                            if b:
                                e.wait_ge(s["lev_X_out"], at(l, "lev_X_out", n))
                            for u in range(4):
                                last = mm(bank(0, 128 * u, 128 * u + 128), TT[:, u, :], X[:, u, :])
                            last.then_inc(s["lev_P"], 1)
                            yield
                            e.wait_ge(s["lev_P_out"], at(l, "lev_P_out", n + 1))
                            for u in range(4):
                                if b < 4:
                                    mm(bank(1, 128 * u, 128 * u + 128), XT[:, u, :], P[:, u, :])
                                last = mm(bank(2, 128 * u, 128 * u + 128), P[:, u, :], XT[:, u, :])
                            last.then_inc(s["lev_X"], 1)
                            yield
                        e.wait_ge(s["lev_X_out"], at(l, "lev_X_out", 5 * g + 5))
                        e.wait_ge(s["mv_out"], at(l, "mv_out", g + 1))
                        for u in range(4):
                            last = mm(bank(3, 128 * u, 128 * u + 128), XT[:, u, :], Rt[:, u, :])
                        last.then_inc(s["xr"], 1)
                        yield
                        e.wait_ge(s["xr_out"], at(l, "xr_out", g + 1))

                        def both(m, t):
                            return m[:, t, :].rearrange("p (a b) -> p a b", a=3)[:, 0:3:2, :]

                        for t in range(2):
                            for h in range(2):
                                mm(bank(0, 256 * t, 256 * t + 256)[rows_of[h], :], Wm[:, t, 128 * h:128 * h + 64],
                                   BE[:, t, :, :].rearrange("p a b -> p (a b)"))
                        for t in range(2):
                            for c in range(2):
                                o = pair(bank(1, 256 * t + 128 * c, 256 * t + 128 * c + 128))
                                mm(o, KE[:, t, c, :], both(Vm, t), True, False)
                                mm(o, BE[:, t, c, :], both(Ym, t), False, True)
                        for t in range(2):
                            o = bank(2, 128 * t, 128 * t + 128)
                            mm(o, Wm[:, t, 0:128], LG[:, 2 * t, 128:256], True, False)
                            mm(o, Wm[:, t, 64:192], LG[:, 2 * t + 1, 128:256], False, True)
                        for t in range(2):
                            o = bank(2, 256 + 128 * t, 384 + 128 * t)
                            mm(o, Vm[:, t, 0:128], MG[:, 2 * t, 128:256], True, False)
                            mm(o, Vm[:, t, 64:192], MG[:, 2 * t + 1, 128:256], False, False)
                            mm(o, Ym[:, t, 0:128], LG[:, 2 * t, 128:256], False, False)
                            last = mm(o, Ym[:, t, 64:192], LG[:, 2 * t + 1, 128:256], False, True)
                        last.then_inc(s["ab"], 1)
                        yield
                        e.wait_ge(s["ab_out"], at(l, "ab_out", g + 1))
                        for c in range(2 if g < NG - 1 else 1):
                            n = 2 * g + c
                            src = pair(W("S0", 0, 256)) if g == NG - 1 else S[:, c, :, :]
                            if n:
                                e.wait_ge(s["state_out"], at(l, "state_out", n))
                            for t in range(2):
                                mm(bank(0, 128 * t + 64 * c, 128 * t + 64 * c + 64), src[:, t, :],
                                   rp[:, t, 64 * c:64 * c + 64])
                            for t in range(2):
                                last = mm(bank(3, 128 * t, 128 * t + 128), Abd[:, t, c, :], src[:, t, :])
                            last.then_inc(s["state_mm"], 1)
                            yield

                    e.wait_ge(s["y_out"], at(l, "y_out", NG))
                    for t in range(2):
                        halves(Q(t), bones, yrw[:, t, 0:T]).then_inc(s["gn_sum"], 1)
                    yield
                    e.wait_ge(s["gn_sq"], at(l, "gn_sq"))
                    for t in range(2):
                        halves(Q(t), bones, ell[:, t, 0:T]).then_inc(s["gn_sum"], 1)
                    yield
                    e.wait_ge(s["gn_rstd"], at(l, "gn_rstd"))
                    for t in range(2):
                        last = halves(Q(t), W("low", 128 * t, 128 * t + 128, rows_of[1]), xs[64:128, 6, 0:T])
                    last.then_inc(s["g_out"], 1)
                    yield

                def project(n):
                    h, p = n // 5, n % 5
                    wait_bank(e, l, ("p", n))
                    o = bank(bank_of(("p", n)))
                    if p < 3:
                        a, b = PIECES[p]
                        for k in range(2):
                            last = mm(o[:, 0:b - a], W("uq", (k * HEADS + h) * 128, (k * HEADS + h + 1) * 128),
                                      cq[:, k, a:b], k == 0, k == 1)
                        last.then_inc(s["q_mm"], 1)
                    elif p == 3:
                        mm(o[0:64, :], W("uk", 64 * h, 64 * h + 64), ckv[:, 0:SEQ]).then_inc(s["k_mm"], 1)
                    else:
                        mm(o[0:64, 0:DEC], W("uk", 64 * h, 64 * h + 64), ckv[:, SEQ:T])
                        mm(o[0:64, DEC:DEC + PAST], W("uk", 64 * h, 64 * h + 64),
                           W("ckv", 0, PAST)).then_inc(s["k_mm"], 1)

                def score(u):
                    h, b = UNITS[u]
                    if b == 0:
                        e.wait_ge(s["q_out"], at(l, "q_out", 3 * h + 3))
                        e.wait_ge(s["nope_out"], at(l, "nope_out", 3 * h + 3))
                        e.wait_ge(s["k_out"], at(l, "k_out", 2 * h + 2))
                    wait_bank(e, l, ("s", u))
                    o = bank(bank_of(("s", u)))
                    if b < 4:
                        nk = 128 * b + 128
                        mm(o[:, 0:nk], aq[0:QKD, h % 2, 128 * b:128 * b + 128], ak[0:QKD, h % 2, 0:nk], True, False)
                        mm(o[:, nk - 128:nk], C("maskq", 0, 128, slice(0, 1)), C("maskk", 0, 128, slice(0, 1)),
                           False, True).then_inc(s["a_score"], 1)
                    else:
                        mm(o[0:DEC, 0:KEYS - SEQ], aq[0:QKD, h % 2, SEQ:T],
                           ak[0:QKD, h % 2, SEQ:KEYS]).then_inc(s["a_score"], 1)

                def turn(u):
                    h, b = UNITS[u]
                    e.wait_ge(s["a_norm"], at(l, "a_norm", u + 1))
                    if u:
                        e.wait_ge(s["a_T_out"], at(l, "a_T_out", u))
                    if b < 4:
                        for j in range(b + 1):
                            last = e.transpose(bank(6, 128 * j, 128 * j + 128),
                                               aP[:, u % 2, 128 * j:128 * j + 128], ident)
                    else:
                        e.transpose(bank(6, 0, DEC)[0:DEC, :], aP[0:DEC, u % 2, 0:DEC], ident[0:DEC, 0:DEC])
                        for j in range(2):
                            last = e.transpose(bank(6, 128 * j + 128, 128 * j + 128 + DEC),
                                               aP[0:DEC, u % 2, DEC + 128 * j:DEC + 128 * j + 128],
                                               ident[0:DEC, 0:DEC])
                    last.then_inc(s["a_T"], 1)

                def weigh(u):
                    h, b = UNITS[u]
                    e.wait_ge(s["a_T_out"], at(l, "a_T_out", u + 1))
                    if u >= 1:
                        e.wait_ge(s["a_o"], at(l, "a_o", u))
                    rows = rows_of[h % 2]
                    if b < 4:
                        o = bank(7, 0, 128)[rows, :]
                        for j in range(b + 1):
                            last = mm(o, av[:, j, 64 * h:64 * h + 64], aPT[:, u % 2, 128 * j:128 * j + 128],
                                      j == 0, j == b)
                    else:
                        o = bank(7, 0, DEC)[rows, :]
                        mm(o, av[0:DEC, 4, 64 * h:64 * h + 64], aPT[0:DEC, u % 2, 0:DEC], True, False)
                        for j in range(2):
                            last = mm(o, av[:, 5 + j, 64 * h:64 * h + 64],
                                      aPT[:, u % 2, 128 * j + 128:128 * j + 128 + DEC], False, j == 1)
                    last.then_inc(s["a_pv"], 1)

                def attention():
                    e.wait_ge(s["ckv_n"], at(l, "ckv_n"))
                    for j in range(7):
                        src = ckv[:, 128 * j:128 * j + (128 if j < 4 else DEC)] if j < 5 else \
                            W("ckv", 128 * (j - 5), 128 * (j - 4))
                        wait_bank(e, l, ("v", j))
                        mm(bank(bank_of(("v", j)))[0:src.shape[-1], :], src, W("uv", 0, 512)).then_inc(s["v_mm"], 1)
                        yield
                    e.wait_ge(s["cq_n"], at(l, "cq_n"))
                    for p in range(5):
                        project(p)
                        yield
                    for u, (h, b) in enumerate(UNITS):
                        if u:
                            turn(u - 1)
                        score(u)
                        yield
                        if h + 1 < HEADS:
                            project(5 * (h + 1) + b)
                        if u:
                            weigh(u - 1)
                        yield
                    turn(len(UNITS) - 1)
                    yield
                    weigh(len(UNITS) - 1)

                in_turn(recurrence(), attention())

                dense(l, "out", h_from=8)
                e.wait_ge(s["memn"], at(l, "memn"))
                dense(l, "mk")
                dense(l, "mv")
                def attention_mem():
                    for kind, n in MEM_STEPS:
                        if kind == "score":
                            u, (h, b) = n, MUNITS[n]
                            if u == 0:
                                wait_evac(e, l, "mv", 7)
                                e.wait_ge(mem_ld, 32 * (l + 1))
                            if b == 0:
                                wait_evac(e, l, "mq", 2 * h + 1)
                            if u >= 2:
                                e.wait_ge(s["m_exp"], at(l, "m_exp", u - 1))
                            m = 128 if b < 4 else DEC
                            keys = mkp if b < 4 else mks
                            for j in range(2):
                                last = mm(bank(4 + u % 2, 0, MEM)[0:m, :], mq[:, 2 * h + j, 128 * b:128 * b + m],
                                          keys[:, 2 * h + j, :], j == 0, j == 1)
                            last.then_inc(s["m_score"], 1)
                        elif kind == "turn":
                            u, m = n, 128 if MUNITS[n][1] < 4 else DEC
                            e.wait_ge(s["m_norm"], at(l, "m_norm", u + 1))
                            if u:
                                e.wait_ge(s["m_T_out"], at(l, "m_T_out", u))
                            for j in range(2):
                                last = e.transpose(bank(6, 128 * j, 128 * j + m),
                                                   mP[0:m, u % 2, 128 * j:128 * j + 128], ident[0:m, 0:m])
                            last.then_inc(s["m_T"], 1)
                        elif kind == "weigh":
                            h, i = n // 4, n % 4 // 2
                            va, a, b = ((mvp, 0, SEQ), (mvs, SEQ, T))[n % 2]
                            e.wait_ge(s["m_T_out"], at(l, "m_T_out", 5 * h + 5))
                            if n:
                                e.wait_ge(s["m_o"], at(l, "m_o", n))
                            for j in range(2):
                                last = mm(bank(7, 0, b - a), va[:, j, 256 * h + 128 * i:256 * h + 128 * i + 128],
                                          mPT[:, h % 2, j, a:b], j == 0, j == 1)
                            last.then_inc(s["m_pv"], 1)
                        yield

                in_turn(dense_steps(l, "mq", h_from=16), attention_mem())
                dense(l, "mo", h_from=24)
                for g in range(5):
                    if g < 4:
                        dense(l, "f1", g, h_from=32)
                    if g:
                        dense(l, "f2", g - 1)
            rms(3 * DEPTH)

        @block.scalar
        def _(e):
            steps = 0

            def act(out, in_, f, **kw):
                return e.activation(out, in_, f, **kw)

            def link(ins):
                nonlocal steps
                steps += 1
                ins.then_inc(astep, 1)
                e.wait_ge(astep, steps)

            def split(n):
                e.wait_ge(w_load[n % RING], 16 * (n // RING + 1))
                if n >= SPLIT:
                    e.wait_ge(pe_done, n - SPLIT + 1)
                act(wH[:, n % SPLIT], ring[:, n % RING], ACT.Copy).then_inc(w_hi, 1)

            def ahead(l, st, i):
                n = tile_no(l, st, i) + 2
                if split_now(n):
                    split(n)

            def square(r, k):
                if k == 0 and r:
                    e.wait_ge(s["rms_sum"], r)
                if k > 1:
                    e.wait_ge(s["sq_added"], 7 * r + k - 1)
                act(sq[:, min(k, 1), :], xT[:, k, :], ACT.Square).then_inc(s["sq_ready"], 1)

            def rstd(r):
                e.wait_ge(s["rms_sum"], r + 1)
                link(act(rs, Q(2), ACT.Ln, scale=1.0 / D, bias=K(C_EPS)))
                act(rs, rs, ACT.Exp, scale=-0.5).then_inc(s["rms_rstd"], 1)

            def scaled_hi(l, gain, k):
                act(hH[:, k, :], xT[:, k, :], ACT.Copy, scale=V(l, gain, k)).then_inc(s["h_hi"], 1)

            def mixed_hi(src, k):
                act(hH[:, k, :], src[:, k, :], ACT.Copy).then_inc(s["h_hi"], 1)

            e.wait_ge(vec_ld, 16)
            for k in range(8):
                e.wait_ge(x_ld[k // 2], 16)
                if k in (1, 7):
                    split(k // 7)
                scaled_hi(0, "g_mix", k)
                square(0, k)
            e.wait_ge(setup_abs, 1)
            act(stat[:, 0:4], stat[:, 4:8], ACT.Exp, scale=-1.0).then_inc(setup_exp, 1)
            for l in range(DEPTH):
                for i in range(N_IN):
                    ahead(l, "in", i)
                    if i == 0:
                        rstd(3 * l)
                    if i == 11:
                        wait_evac(e, l, "in", 9)
                        act(lat_sq[:, 0:2, :], cq, ACT.Square)
                        act(lat_sq[:, 2, :], ckv, ACT.Square).then_inc(s["lat_sq"], 1)
                    if i == 13:
                        e.wait_ge(s["lat_sum"], at(l, "lat_sum"))
                        act(lat_r[:, 0, :], Q(2), ACT.Ln, scale=1.0 / 256, bias=K(C_EPS))
                        link(act(lat_r[:, 1, :], Q(3), ACT.Ln, scale=1.0 / 128, bias=K(C_EPS)))
                        act(lat_r, lat_r, ACT.Exp, scale=-0.5).then_inc(s["lat_rstd"], 1)
                if l == 0:
                    e.wait_ge(setup_vec, 1)

                for t in range(2):
                    e.wait_ge(s["rg_z"], at(l, "rg_z", t + 1))
                    act(ra[:, t, :], Q(t, XCW), ACT.Tanh, scale=0.5, bias=derv[:, l, t:t + 1])
                for t in range(2):
                    e.wait_ge(s["rg_z"], at(l, "rg_z", t + 3))
                    last = act(rix[:, t, :], Q(2 + t, XCW), ACT.Tanh, scale=0.5, bias=derv[:, l, 2 + t:3 + t])
                last.then_inc(s["rg_gates"], 1)
                e.wait_ge(s["rg_gates"], at(l, "rg_gates"))
                for t in range(2):
                    last = act(ru[:, t, :], ra[:, t, :], ACT.Tanh, scale=derv[:, l, 8 + t:9 + t],
                               bias=derv[:, l, 8 + t:9 + t])
                link(last)
                for t in range(2):
                    act(ra[:, t, :], ra[:, t, :], ACT.Exp, scale=derv[:, l, 10 + t:11 + t],
                        bias=derv[:, l, 10 + t:11 + t])
                e.wait_ge(s["low_ready"], at(l, "low_ready"))
                act(xs[0:32, 6, 0:T], xs[0:32, 6, 0:T], ACT.Tanh)
                act(xs[64:128, 6, 0:T], xs[64:128, 6, 0:T], ACT.Tanh, scale=0.5).then_inc(s["low_tanh"], 1)
                e.wait_ge(s["rg_gelu_in"], at(l, "rg_gelu_in"))
                act(gx, gx, ACT.Tanh, scale=GELU_C).then_inc(s["rg_gelu"], 1)
                for t in range(4):
                    e.wait_ge(s["low_z"], at(l, "low_z", t + 1))
                    act((ell if t < 2 else bneg)[:, t % 2, 0:T], Q(t), ACT.Tanh, scale=0.5,
                        bias=derv[:, l, 4 + t:5 + t]).then_inc(s["low_gate"], 1)
                e.wait_ge(s["kk_raw"], at(l, "kk_raw"))
                act(e1, kk[:, :, 0:T], ACT.Square).then_inc(s["kk_sq"], 1)
                e.wait_ge(s["rg_ix"], at(l, "rg_ix"))
                act(xc, ru, ACT.Ln, bias=K(C_ONE))
                act(rln, ru, ACT.Ln, scale=2.0, bias=K(C_TINY)).then_inc(s["rg_ln"], 1)
                for t in range(2):
                    e.wait_ge(s["kk_sum"], at(l, "kk_sum", t + 1))
                    last = act(e1[:, t, :], Q(t), ACT.Ln, bias=K(C_L2))
                link(last)
                act(e1, e1, ACT.Exp, scale=-0.5).then_inc(s["kk_rstd"], 1)
                e.wait_ge(s["rg_q"], at(l, "rg_q"))
                act(ru, ru, ACT.Exp, scale=0.5).then_inc(s["rg_sq"], 1)

                e.wait_ge(s["frames_zeroed"], at(l, "frames_zeroed"))
                def decays(g):
                    e.wait_ge(s["decay_cum"], at(l, "decay_cum", g + 1))
                    act(stat[:, 8:12], Lc.rearrange("p a (c n) -> p (a c) n", c=2)[:, :, CH - 1], ACT.Exp,
                        scale=-1.0)
                    act(ep, Lc, ACT.Exp)
                    act(ee, le, ACT.Exp)
                    link(act(en1, dm, ACT.Exp, scale=-1.0))
                    act(en, Lc, ACT.Exp, scale=-1.0).then_inc(s["decay_exp"], 1)

                def recurrence():
                    for g in range(NG):
                        e.wait_ge(s["tok_T"], at(l, "tok_T", g + 1))
                        for t in range(2):
                            act(Vm[:, t, :].rearrange("p (a b) -> p a b", a=3)[:, 0:3:2, :],
                                pair(bank(0, 128 * t, 128 * t + 128)), ACT.Copy)
                            act(Rt[:, 2 * t:2 * t + 2, 0:64], pair(bank(0, 256 + 128 * t, 384 + 128 * t)), ACT.Copy)
                        for c in range(2):
                            act(BE[rows_of[c], :, c, :], pair(bank(1, 0, 256))[rows_of[c]], ACT.Copy)
                            last = act(KE[rows_of[c], :, c, :], pair(bank(1, 256, 512))[rows_of[c]], ACT.Copy)
                        last.then_inc(s["tok_out"], 1)
                        yield
                        yield
                        e.wait_ge(s["mv"], at(l, "mv", g + 1))
                        act(Rt[:, :, 64:128], pair(bank(3, 0, 256), 4), ACT.Copy).then_inc(s["mv_out"], 1)
                        for b in range(5):
                            n = 5 * g + b
                            e.wait_ge(s["lev_P"], at(l, "lev_P", n + 1))
                            act(P, pair(bank(0), 4), ACT.Copy).then_inc(s["lev_P_out"], 1)
                            yield
                            yield
                        e.wait_ge(s["xr"], at(l, "xr", g + 1))
                        for t in range(2):
                            o = pair(bank(3, 256 * t, 256 * t + 256))
                            act(Wm[:, t, :].rearrange("p (a b) -> p a b", a=3)[:, 0:3:2, :], o[:, :, 0:64], ACT.Copy)
                            last = act(Ym[:, t, :].rearrange("p (a b) -> p a b", a=3)[:, 0:3:2, :],
                                       o[:, :, 64:128], ACT.Copy)
                        last.then_inc(s["xr_out"], 1)
                        yield
                        if g + 1 < NG:
                            decays(g + 1)
                        yield
                        yield
                        if g < NG - 1:
                            yield

                    e.wait_ge(s["gn_mean"], at(l, "gn_mean"))
                    act(ell[:, :, 0:T], yrw[:, :, 0:T], ACT.Square).then_inc(s["gn_sq"], 1)
                    yield
                    for t in range(2):
                        e.wait_ge(s["gn_sum"], at(l, "gn_sum", 3 + t))
                        last = act(ell[:, t, 0:T], Q(t), ACT.Ln, scale=1.0 / 64, bias=K(C_GN))
                    link(last)
                    act(ell[:, :, 0:T], ell[:, :, 0:T], ACT.Exp, scale=-0.5).then_inc(s["gn_rstd"], 1)
                    yield
                    e.wait_ge(stored["wkv"], 32 * (l + 1))
                    split(tile_no(l, "out", 0))
                    split(tile_no(l, "out", 1))
                    yield

                def nope_out(n):
                    h, p = n // 5, n % 5
                    if h >= 2:
                        e.wait_ge(s["a_score"], at(l, "a_score", 5 * (h - 1)))
                    e.wait_ge(s["q_mm"], at(l, "q_mm", 3 * h + p + 1))
                    a, b = PIECES[p]
                    act(aq[0:64, h % 2, a:b], bank(bank_of(("p", n)), 0, b - a)[0:64, :],
                        ACT.Copy).then_inc(s["nope_out"], 1)

                def keys_out(n):
                    h = n // 5
                    if h >= 2:
                        e.wait_ge(s["a_score"], at(l, "a_score", 5 * (h - 1)))
                    e.wait_ge(s["k_mm"], at(l, "k_mm", 2 * h + n % 5 - 2))
                    a, b = (0, SEQ) if n % 5 == 3 else (SEQ, KEYS)
                    act(ak[0:64, h % 2, a:b], bank(bank_of(("p", n)), 0, b - a)[0:64, :],
                        ACT.Copy).then_inc(s["k_out"], 1)

                def turned_out(u):
                    h, b = UNITS[u]
                    e.wait_ge(s["a_T"], at(l, "a_T", u + 1))
                    if b < 4:
                        last = act(aPT[:, u % 2, 0:128 * b + 128], bank(6, 0, 128 * b + 128), ACT.Copy)
                    else:
                        act(aPT[0:DEC, u % 2, 0:DEC], bank(6, 0, DEC)[0:DEC, :], ACT.Copy)
                        last = act(pair(aPT[:, u % 2, 128:384])[:, :, 0:DEC],
                                   pair(bank(6, 128, 384))[:, :, 0:DEC], ACT.Copy)
                    last.then_inc(s["a_T_out"], 1)

                def head_out(u):
                    h, b = UNITS[u]
                    n = 128 if b < 4 else DEC
                    e.wait_ge(s["a_pv"], at(l, "a_pv", u + 1))
                    rows = rows_of[h % 2]
                    act(hT[rows, 4 + h // 2, 128 * b:128 * b + n], bank(7, 0, n)[rows, :],
                        ACT.Copy).then_inc(s["a_o"], 1)

                def attention():
                    for j in range(7):
                        n = DEC if j == 4 else 128
                        e.wait_ge(s["v_mm"], at(l, "v_mm", j + 1))
                        act(av[0:n, j, :], bank(bank_of(("v", j)))[0:n, :], ACT.Copy).then_inc(s["v_out"], 1)
                        yield
                    for p in range(5):
                        (nope_out if p < 3 else keys_out)(p)
                        yield
                    for u, (h, b) in enumerate(UNITS):
                        if u:
                            turned_out(u - 1)
                        n, nk = (128, 128 * b + 128) if b < 4 else (DEC, KEYS - SEQ)
                        e.wait_ge(s["a_max"], at(l, "a_max", u + 1))
                        act(aP[0:n, u % 2, 0:nk], bank(bank_of(("s", u)), 0, nk)[0:n, :], ACT.Exp, scale=MLA_SCALE,
                            bias=stat[0:n, 18 + u % 2:19 + u % 2],
                            accum_out=stat[0:n, 20 + u % 2:21 + u % 2]).then_inc(s["a_exp"], 1)
                        yield
                        if h + 1 < HEADS:
                            (nope_out if b < 3 else keys_out)(5 * (h + 1) + b)
                        if u:
                            head_out(u - 1)
                        yield
                    turned_out(len(UNITS) - 1)
                    yield
                    head_out(len(UNITS) - 1)

                decays(0)
                in_turn(recurrence(), attention())
                e.wait_ge(s["rw_y"], at(l, "rw_y"))
                e.wait_ge(s["a_o"], at(l, "a_o", 40))
                for k in range(8):
                    mixed_hi(hT, k)

                for i in range(8):
                    ahead(l, "out", i)
                    if l == 0 and i == 0:
                        e.wait_ge(tokens_ld, 16)
                        for k in range(8):
                            if k > 1:
                                e.wait_ge(msq_added, k - 1)
                            act(msq[:, min(k, 1), :], mem32[:, k, :], ACT.Square).then_inc(msq_ready, 1)
                    if l == 0 and i == 2:
                        e.wait_ge(mem_sum, 1)
                        link(act(mrs, bank(6, 0, MEM), ACT.Ln, scale=1.0 / D, bias=K(C_EPS)))
                        act(mrs, mrs, ACT.Exp, scale=-0.5).then_inc(mem_rstd, 1)
                    if i == 5:
                        e.wait_ge(s["mem_scaled"], at(l, "mem_scaled"))
                        act(memH[:, :, :], mem32, ACT.Copy).then_inc(s["mem_hi"], 1)
                    wait_evac(e, l, "out", i)
                    square(3 * l + 1, i)
                for st in ("mk", "mv"):
                    for i in range(8):
                        ahead(l, st, i)
                        if st == "mk":
                            if i == 0:
                                wait_tile(e, l, "out", 7)
                            scaled_hi(l, "g_mem", i)
                        if (st, i) == ("mv", 3):
                            rstd(3 * l + 1)
                        if st == "mv" and i % 2 == 0:
                            continue
                        wait_tile(e, l, st, i)
                        if st == "mk":
                            act(mkp[:, i, :], bank(2 * (tile_no(l, st, i) % 2), 0, 256),
                                ACT.Copy).then_inc(evac["act"], 1)
                        else:
                            o = values_bank(l, i) * 512
                            act(mvp[:, :, 128 * i - 128:128 * i + 128], pair(PS[:, o:o + 1024])[:, :, 0:256],
                                ACT.Copy).then_inc(evac["act"], 1)

                def queries_mem():
                    for i in range(8):
                        for k in range(8):
                            if k == 0:
                                ahead(l, "mq", i)
                            yield

                def attention_mem():
                    for kind, n in MEM_STEPS:
                        if kind == "score":
                            u, m = n, 128 if MUNITS[n][1] < 4 else DEC
                            e.wait_ge(s["m_max"], at(l, "m_max", u + 1))
                            act(mP[0:m, u % 2, :], bank(4 + u % 2, 0, MEM)[0:m, :], ACT.Exp, scale=MEM_SCALE,
                                bias=stat[0:m, 18 + u % 2:19 + u % 2],
                                accum_out=stat[0:m, 20 + u % 2:21 + u % 2]).then_inc(s["m_exp"], 1)
                        elif kind == "turn":
                            u, (h, b) = n, MUNITS[n]
                            m = 128 if b < 4 else DEC
                            e.wait_ge(s["m_T"], at(l, "m_T", u + 1))
                            act(mPT[:, h % 2, :, 128 * b:128 * b + m], pair(bank(6, 0, 256))[:, :, 0:m],
                                ACT.Copy).then_inc(s["m_T_out"], 1)
                        elif kind == "weigh":
                            a, b = ((0, SEQ), (SEQ, T))[n % 2]
                            e.wait_ge(s["m_pv"], at(l, "m_pv", n + 1))
                            act(oT[:, n // 2, a:b], bank(7, 0, b - a), ACT.Copy).then_inc(s["m_o"], 1)
                        yield

                in_turn(queries_mem(), attention_mem())
                for k in range(8):
                    if k % 2 == 0:
                        e.wait_ge(s["m_o"], at(l, "m_o", 2 * k + 4))
                    mixed_hi(oT, k)
                for i in range(8):
                    ahead(l, "mo", i)
                    if i == 7:
                        wait_tile(e, l, "mo", 7)
                        for k in range(7):
                            scaled_hi(l, "g_ffn", k)
                    wait_evac(e, l, "mo", i)
                    square(3 * l + 2, i)
                scaled_hi(l, "g_ffn", 7)
                for g in range(5):
                    if g < 4:
                        for i in range(8 * g, 8 * g + 8):
                            ahead(l, "f1", i)
                            if i == 0:
                                rstd(3 * l + 2)
                            e.wait_ge(s["hid_sq"], at(l, "hid_sq", i + 1))
                            act(hidH[:, g % 2, i % 8, :], hid[:, g % 2, i % 8, :], ACT.Copy)\
                                .then_inc(s["hid_hi"], 1)
                    if g:
                        for i in range(8 * g - 8, 8 * g):
                            ahead(l, "f2", i)
                            if g == 4:
                                wait_evac(e, l, "f2", i)
                                square(3 * l + 3, i % 8)
                                if l + 1 < DEPTH:
                                    scaled_hi(l + 1, "g_mix", i % 8)
            rstd(3 * DEPTH)

        @block.vector
        def _(e):
            steps = 0

            def link(ins):
                nonlocal steps
                steps += 1
                ins.then_inc(vstep, 1)
                e.wait_ge(vstep, steps)

            tt, stt, ts = e.tensor_tensor, e.scalar_tensor_tensor, e.tensor_scalar

            def split(n):
                e.wait_ge(w_hi, n + 1)
                tt(wL[:, n % SPLIT], ring[:, n % RING], plain(wH[:, n % SPLIT]), ALU.subtract).then_inc(w_lo, 1)

            def ahead(l, st, i):
                n = tile_no(l, st, i) + 2
                if split_now(n):
                    split(n)

            def scaled_lo(l, h_from, gain, k):
                e.wait_ge(s["h_hi"], at(l, "h_hi", h_from + k + 1))
                stt(hL[:, k, :], xT[:, k, :], V(l, gain, k), plain(hH[:, k, :]), ALU.mult, ALU.subtract)\
                    .then_inc(s["h_ready"], 1)

            def mixed_lo(l, h_from, src, k):
                e.wait_ge(s["h_hi"], at(l, "h_hi", h_from + k + 1))
                tt(hL[:, k, :], src[:, k, :], plain(hH[:, k, :]), ALU.subtract).then_inc(s["h_ready"], 1)

            def take_tile(l, st, i):
                wait_tile(e, l, st, i)
                return Q(tile_no(l, st, i) % 2)

            def residual(l, st, i):
                ps = take_tile(l, st, i)
                k = i % 8
                if i >= 8:
                    wait_evac(e, l, st, i - 8)
                tt(xT[:, k, :], ps, xT[:, k, :], ALU.add).then_inc(evac["dve"], 1)

            for c, v in ((C_TINY, 1e-37), (C_EPS, EPS), (C_L2, L2_EPS), (C_GN, GN_EPS), (C_ONE, 1.0)):
                e.memset(K(c), v)
            e.wait_ge(vec_ld, 16)
            for k in range(8):
                if k in (1, 7):
                    split(k // 7)
                scaled_lo(0, 0, "g_mix", k)
            lam = vec[:, :, VEC["lam"]:VEC["lam"] + 2]
            four = lambda a: pair(stat[:, a:a + 4])
            stt(four(4), lam, -1.0, lam, ALU.mult, ALU.max).then_inc(setup_abs, 1)
            link(ts(four(24), lam, -1.0, 0.0, ALU.mult, ALU.max))
            e.wait_ge(setup_exp, 1)
            link(ts(four(28), four(0), 2.0, None, ALU.add))
            link(e.reciprocal(four(32), four(28)))
            link(tt(four(28), four(0), four(32), ALU.mult))
            link(tt(four(32), four(28), four(28), ALU.mult))
            link(ts(four(36), four(32), 1.0 / 15, None, ALU.mult))
            for k in (13, 11, 9, 7, 5, 3):
                link(stt(four(36), four(36), 1.0 / k, four(32), ALU.add, ALU.mult))
            link(stt(four(36), four(36), 1.0, four(28), ALU.add, ALU.mult))
            link(stt(four(36), four(36), 2.0, four(24), ALU.mult, ALU.add))
            ts(derv[:, :, 8:10], four(36), 4.0, None, ALU.mult)
            ts(derv[:, :, 10:12], four(36), -4.0, None, ALU.mult)
            ts(derv[:, :, 0:8], vec[:, :, VEC["rg_ba"]:VEC["rg_ba"] + 8], 0.5, None,
               ALU.mult).then_inc(setup_vec, 1)
            for l in range(DEPTH):
                if l:
                    e.wait_ge(stored["mem"], 32 * l)
                e.memset(raw[:, :, 0:1], 0.0)
                e.tensor_copy(raw[:, :, SEQ + 1], vec[:, l, VEC["shift"]:VEC["shift"] + 7])
                e.memset(rg[:, :, 0:3], 0.0)
                link(e.tensor_copy(rg[:, :, 3 + SEQ:6 + SEQ], pair(vec[:, l, VEC["conv_s"]:VEC["conv_s"] + 6])))
                for i in range(N_IN):
                    ahead(l, "in", i)
                    if i == 0:
                        e.wait_ge(s["rms_rstd"], 3 * l + 1)
                    ps = take_tile(l, "in", i)
                    if i < RWT:
                        tt(raw[:, i, 1:1 + SEQ], ps[:, 0:SEQ], rs[:, 0:SEQ], ALU.mult)
                        tt(raw[:, i, 2 + SEQ:RWW], ps[:, SEQ:T], rs[:, SEQ:T], ALU.mult).then_inc(evac["dve"], 1)
                        wait_evac(e, l, "in", i)
                        tt(xs[:, i, 0:SEQ], raw[:, i, 0:SEQ], raw[:, i, 1:1 + SEQ], ALU.subtract)
                        link(tt(xs[:, i, SEQ:T], raw[:, i, 1 + SEQ:RWW - 1], raw[:, i, 2 + SEQ:RWW], ALU.subtract))
                        stt(xs[:, i, 0:SEQ], xs[:, i, 0:SEQ], V(l, "mu", i), raw[:, i, 1:1 + SEQ], ALU.mult, ALU.add)
                        ins = stt(xs[:, i, SEQ:T], xs[:, i, SEQ:T], V(l, "mu", i), raw[:, i, 2 + SEQ:RWW],
                                  ALU.mult, ALU.add)
                        if i == 6:
                            ins.then_inc(s["low_ready"], 1)
                        else:
                            link(ins)
                        if i in (2, 3):
                            ins = ts(kk[:, i - 2, 0:T], xs[:, i, 0:T], V(l, "k_k", i - 2), None, ALU.mult)
                            if i == 3:
                                ins.then_inc(s["kk_raw"], 1)
                    elif i < 9:
                        tt(cq[:, i - 7, :], ps, rs, ALU.mult).then_inc(evac["dve"], 1)
                    elif i == 9:
                        tt(ckv, ps, rs, ALU.mult).then_inc(evac["dve"], 1)
                    elif i == 10:
                        tt(kr[rope, :], ps[rope, :], C("cos", 0, T, rope), ALU.mult)
                        tt(aq[rope, 0, :], ps[swap, :], C("sin", 0, T, swap), ALU.mult).then_inc(evac["dve"], 1)
                        wait_evac(e, l, "in", 10)
                        link(tt(kr[rope, :], kr[rope, :], aq[rope, 0, :], ALU.add))
                        tt(kr[rope, :], kr[rope, :], rs[rope, :], ALU.mult).then_inc(s["kr_ready"], 1)
                    elif i < 13:
                        t = i - 11
                        tt(rg[:, t, 3:3 + SEQ], ps[:, 0:SEQ], rs[:, 0:SEQ], ALU.mult)
                        tt(rg[:, t, 6 + SEQ:RGW], ps[:, SEQ:T], rs[:, SEQ:T], ALU.mult).then_inc(evac["dve"], 1)
                        wait_evac(e, l, "in", i)
                        link(ts(xc[:, t, :], rg[:, t, 0:XCW], V(l, "conv_w", t), V(l, "conv_b", t),
                                ALU.mult, ALU.add))
                        for j in range(1, CONV):
                            ins = stt(xc[:, t, :], rg[:, t, j:j + XCW], V(l, "conv_w", 2 * j + t), xc[:, t, :],
                                      ALU.mult, ALU.add)
                            if j < CONV - 1 or t == 0:
                                link(ins)
                        if t:
                            ins.then_inc(s["rg_conv"], 1)
                    else:
                        tt(gate[:, i - 13, :], ps, rs, ALU.mult).then_inc(evac["dve"], 1)
                wait_evac(e, l, "in", N_IN - 1)

                e.wait_ge(s["lat_rstd"], at(l, "lat_rstd"))
                stt(ckv, ckv, V(l, "kv_norm"), lat_r[:, 1, :], ALU.mult, ALU.mult).then_inc(s["ckv_n"], 1)
                for t in range(2):
                    ins = stt(cq[:, t, :], cq[:, t, :], V(l, "q_norm", t), lat_r[:, 0, :], ALU.mult, ALU.mult)
                ins.then_inc(s["cq_n"], 1)

                link(tt(gx, gate, gate, ALU.mult))
                link(ts(gx, gx, 0.044715, 1.0, ALU.mult, ALU.add))
                tt(gx, gx, gate, ALU.mult).then_inc(s["rg_gelu_in"], 1)
                e.wait_ge(s["rg_gates"], at(l, "rg_gates"))
                stt(rix, rix, 1.0, xc, ALU.add, ALU.mult).then_inc(s["rg_ix"], 1)
                e.wait_ge(s["rg_gelu"], at(l, "rg_gelu"))
                link(stt(gate, gx, 1.0, gate, ALU.add, ALU.mult))

                e.wait_ge(s["low_gate"], at(l, "low_gate", 4))
                ts(ell[:, :, 0:T], ell[:, :, 0:T], 0.5 * EXP_HALF, 0.5 * EXP_HALF, ALU.mult, ALU.add)
                ts(xs[64:128, 6, 0:T], xs[64:128, 6, 0:T], 0.5, 0.5, ALU.mult, ALU.add)
                link(ts(bneg[:, :, 0:T], bneg[:, :, 0:T], 0.5, 0.5, ALU.mult, ALU.add))
                for t in range(2):
                    link(ts(e2[:, t, :], bneg[:, t, 0:T], -1.0, V(l, "k_a", t), ALU.add, ALU.mult))
                    link(stt(xs[:, 2 + t, 0:T], e2[:, t, :], 1.0, xs[:, 2 + t, 0:T], ALU.add, ALU.mult))
                    ins = stt(e2[:, t, :], xs[:, t, 0:T], V(l, "r_k", t), xs[:, 2 + t, 0:T], ALU.mult, ALU.mult)
                ins.then_inc(s["rk_ready"], 1)
                e.wait_ge(s["rg_ln"], at(l, "rg_ln"))
                tt(ru, rln, xc, ALU.subtract).then_inc(s["rg_q"], 1)
                e.wait_ge(s["kk_rstd"], at(l, "kk_rstd"))
                link(tt(kk[:, :, 0:T], kk[:, :, 0:T], e1, ALU.mult))
                link(stt(bneg[:, :, 0:T], kk[:, :, 0:T], -1.0, bneg[:, :, 0:T], ALU.mult, ALU.mult))
                e.wait_ge(s["rows_kept"], at(l, "rows_kept", 1))
                for t in range(2):
                    e.wait_ge(s["rk_sum"], at(l, "rk_sum", t + 1))
                    link(tt(bonus[:, t, :], Q(2 + t), xs[:, 4 + t, 0:T], ALU.mult))

                e.wait_ge(s["rg_sq"], at(l, "rg_sq"))
                link(stt(rix, ru, 0.5, rix, ALU.mult, ALU.mult))
                for t in range(2):
                    e.tensor_tensor_scan(rh[:, t, 0:SEQ], ra[:, t, 0:SEQ], rix[:, t, 0:SEQ], 0.0, ALU.mult, ALU.add)
                    ins = e.tensor_tensor_scan(rh[:, t, SEQ:T], ra[:, t, SEQ + 3:XCW], rix[:, t, SEQ + 3:XCW],
                                               V(l, "h0", t), ALU.mult, ALU.add)
                link(ins)
                stt(hT[:, 0:2, :], gate, 0.5, rh, ALU.mult, ALU.mult).then_inc(s["rg_done"], 1)

                e.wait_ge(s["frames_zeroed"], at(l, "frames_zeroed"))
                chunks = lambda m: m.rearrange("p a (c n) -> p (a c) n", c=2)
                for j in range(2):
                    e.tensor_copy(ak[rope, j, 0:T], kr[rope, :])
                    e.tensor_copy(ak[rope, j, T:KEYS], W("kr", 0, PAST, rope))

                def columns(g):
                    return slice(GRP * g, GRP * g + GRP)

                def decay_sums(g):
                    for t in range(2):
                        ins = e.tensor_tensor_scan(Lc[:, t, :], C("reset", 0, GRP), ell[:, t, columns(g)], 0.0,
                                                   ALU.mult, ALU.add)
                    link(ins)
                    tt(dm, Lc, ell[:, :, columns(g)], ALU.subtract)
                    end = chunks(Lc)[:, :, CH - 1:CH].to_broadcast([128, 4, CH])
                    tt(chunks(le), chunks(Lc), end, ALU.subtract).then_inc(s["decay_cum"], 1)

                def factors(g):
                    e.wait_ge(s["decay_exp"], at(l, "decay_exp", g + 1))
                    cols = columns(g)
                    tt(be, bneg[:, :, cols], ee, ALU.mult)
                    tt(ke, xs[:, 2:4, cols], ee, ALU.mult)
                    tt(af, kk[:, :, cols], en1, ALU.mult)
                    tt(rf, xs[:, 0:2, cols], en, ALU.mult).then_inc(s["factors"], 1)

                def masked(g):
                    cols = columns(g)
                    tt(bf, bneg[:, :, cols], ep, ALU.mult)
                    tt(kf, xs[:, 2:4, cols], ep, ALU.mult)
                    e.wait_ge(s["factors"], at(l, "factors", g + 1))
                    for h in range(2):
                        e.tensor_copy(AR[rows_of[h], h:4:2, 0:128], af[rows_of[h]])
                        ins = e.tensor_copy(AR[rows_of[h], h:4:2, 128:256], rf[rows_of[h]])
                    ins.then_inc(s["masked"], 1)

                def recurrence():
                    for g in range(NG):
                        mask2 = bc(C("mask2", 0, 256), 4)
                        LT = LG[:, :, 0:128]
                        e.wait_ge(s["scores_t"], at(l, "scores_t", g + 1))
                        tt(LG, pair(PS[:, 1024:2048], 4), mask2, ALU.mult).then_inc(s["scores_t_out"], 1)
                        e.wait_ge(s["scores_t_out"], at(l, "scores_t_out", g + 1))
                        link(tt(XT, LT, bc(C("lev", 0, 128), 4), ALU.mult))
                        tt(XT, XT, bc(ident, 4), ALU.add)
                        yield
                        e.wait_ge(s["scores"], at(l, "scores", g + 1))
                        link(tt(X, pair(bank(2), 4), bc(C("lev1t", 0, 128), 4), ALU.mult))
                        tt(X, X, bc(ident, 4), ALU.add)
                        tt(MG, pair(PS[:, 0:1024], 4), mask2, ALU.mult).then_inc(s["scores_out"], 1)
                        yield
                        for b in range(5):
                            n = 5 * g + b
                            yield
                            e.wait_ge(s["lev_X"], at(l, "lev_X", n + 1))
                            if b < 4:
                                tt(X, X, pair(bank(1), 4), ALU.add)
                            tt(XT, XT, pair(bank(2), 4), ALU.add).then_inc(s["lev_X_out"], 1)
                            e.wait_ge(s["lev_X_out"], at(l, "lev_X_out", n + 1))
                            yield
                        yield
                        e.wait_ge(s["ab"], at(l, "ab", g + 1))
                        flat2 = lambda m: m.rearrange("p a c n -> p (a c) n")
                        link(tt(flat2(Abd), pair(bank(0), 4), bc(bones, 4), ALU.mult))
                        for i in range(4):
                            m = flat2(Abd)[:, i, :]
                            stt(m, ident, K(8 + i), m, ALU.mult, ALU.add)
                        tt(flat2(Bbd), pair(bank(1), 4), bc(bones, 4), ALU.mult)
                        tt(rp, pair(bank(2, 0, 256)), rf, ALU.add)
                        e.tensor_copy(yl, pair(bank(2, 256, 512))).then_inc(s["ab_out"], 1)
                        e.wait_ge(s["ab_out"], at(l, "ab_out", g + 1))
                        if g + 1 < NG:
                            decay_sums(g + 1)
                        yield
                        nc_ = 2 if g < NG - 1 else 1
                        for c in range(nc_):
                            n = 2 * g + c
                            e.wait_ge(s["state_mm"], at(l, "state_mm", n + 1))
                            tt(S[:, 1 - c, :, :], pair(bank(3, 0, 256)), Bbd[:, :, c, :], ALU.add)\
                                .then_inc(s["state_out"], 1)
                            if c == nc_ - 1:
                                n = min(GRP, T - GRP * g)
                                tt(yrw[:, :, GRP * g:GRP * g + n], pair(bank(0, 0, 256))[:, :, 0:n], yl[:, :, 0:n],
                                   ALU.add).then_inc(s["y_out"], 1)
                                if g + 1 < NG:
                                    masked(g + 1)
                            elif g + 1 < NG:
                                factors(g + 1)
                            yield

                    for t in range(2):
                        e.wait_ge(s["gn_sum"], at(l, "gn_sum", t + 1))
                        ins = stt(yrw[:, t, 0:T], Q(t), -1.0 / 64, yrw[:, t, 0:T], ALU.mult, ALU.add)
                    ins.then_inc(s["gn_mean"], 1)
                    yield
                    yield
                    e.wait_ge(s["gn_rstd"], at(l, "gn_rstd"))
                    link(tt(yrw[:, :, 0:T], yrw[:, :, 0:T], ell[:, :, 0:T], ALU.mult))
                    for t in range(2):
                        ins = ts(yrw[:, t, 0:T], yrw[:, t, 0:T], V(l, "gn_w", t), V(l, "gn_b", t), ALU.mult, ALU.add)
                    link(ins)
                    link(tt(yrw[:, :, 0:T], yrw[:, :, 0:T], bonus, ALU.add))
                    e.wait_ge(s["g_out"], at(l, "g_out"))
                    for t in range(2):
                        ins = tt(hT[:, 2 + t, :], Q(t), yrw[:, t, 0:T], ALU.mult)
                    ins.then_inc(s["rw_y"], 1)
                    split(tile_no(l, "out", 0))
                    split(tile_no(l, "out", 1))
                    yield

                def queries_out(n):
                    h, p = n // 5, n % 5
                    if h >= 2:
                        e.wait_ge(s["a_score"], at(l, "a_score", 5 * (h - 1)))
                    i = 3 * h + p + 1
                    e.wait_ge(s["q_mm"], at(l, "q_mm", i))
                    a, b = PIECES[p]
                    q, ps = aq[:, h % 2, a:b], bank(bank_of(("p", n)), 0, b - a)
                    tt(q[rope, :], ps[rope, :], C("cos", a, b, rope), ALU.mult)
                    tt(rs[rope, a:b], ps[swap, :], C("sin", a, b, swap), ALU.mult).then_inc(s["q_read"], 1)
                    e.wait_ge(s["q_read"], at(l, "q_read", i))
                    tt(q[rope, :], q[rope, :], rs[rope, a:b], ALU.add).then_inc(s["q_out"], 1)

                def maximum(u, name, n, nk, scale, scores):
                    e.wait_ge(s[name + "_score"], at(l, name + "_score", u + 1))
                    link(e.reduce_max(stat[0:n, 16 + u % 2:17 + u % 2], bank(scores, 0, nk)[0:n, :], AX))
                    ts(stat[0:n, 18 + u % 2:19 + u % 2], stat[0:n, 16 + u % 2:17 + u % 2], -scale, None,
                       ALU.mult).then_inc(s[name + "_max"], 1)

                def normalise(u, name, p, n, nk):
                    e.wait_ge(s[name + "_exp"], at(l, name + "_exp", u + 1))
                    r = stat[0:n, 22 + u % 2:23 + u % 2]
                    link(e.reciprocal(r, stat[0:n, 20 + u % 2:21 + u % 2]))
                    m = p[0:n, u % 2, 0:nk]
                    ts(m, m, r, None, ALU.mult).then_inc(s[name + "_norm"], 1)

                def size(b):
                    return (128, 128 * b + 128) if b < 4 else (DEC, KEYS - SEQ)

                def attention():
                    for j in range(7):
                        yield
                    for p in range(5):
                        if p < 3:
                            queries_out(p)
                        yield
                    for u, (h, b) in enumerate(UNITS):
                        maximum(u, "a", *size(b), MLA_SCALE, bank_of(("s", u)))
                        yield
                        if h + 1 < HEADS and b < 3:
                            queries_out(5 * (h + 1) + b)
                        normalise(u, "a", aP, *size(b))
                        yield
                    yield

                decay_sums(0)
                factors(0)
                masked(0)
                in_turn(recurrence(), attention())
                for k in range(8):
                    mixed_lo(l, 8, hT, k)

                for i in range(8):
                    ahead(l, "out", i)
                    if i == 4:
                        e.wait_ge(mem_rstd, 1)
                        e.wait_ge(tokens_ld, 16 * (l + 1))
                        for k in range(8):
                            ins = stt(mem32[:, k, :], mem32[:, k, :], V(l, "g_memkv", k), mrs, ALU.mult, ALU.mult)
                        ins.then_inc(s["mem_scaled"], 1)
                    if i == 6:
                        e.wait_ge(s["mem_hi"], at(l, "mem_hi"))
                        tt(memL[:, :, :], mem32, plain(memH[:, :, :]), ALU.subtract).then_inc(s["memn"], 1)
                    residual(l, "out", i)
                for st in ("mk", "mv"):
                    for i in range(8):
                        ahead(l, st, i)
                        if st == "mk":
                            scaled_lo(l, 16, "g_mem", i)
                e.wait_ge(s["rms_rstd"], 3 * l + 2)

                def queries_mem():
                    for i in range(8):
                        for k in range(8):
                            if k == 0:
                                ahead(l, "mq", i)
                            if k == 7:
                                ps = take_tile(l, "mq", i)
                                tt(mq[:, i, :], ps, rs, ALU.mult).then_inc(evac["dve"], 1)
                            yield

                def attention_mem():
                    for kind, n in MEM_STEPS:
                        m = 128 if MUNITS[n][1] < 4 else DEC
                        if kind == "score":
                            maximum(n, "m", m, MEM, MEM_SCALE, 4 + n % 2)
                        elif kind == "turn":
                            normalise(n, "m", mP, m, MEM)
                        yield

                in_turn(queries_mem(), attention_mem())
                for k in range(8):
                    mixed_lo(l, 24, oT, k)

                for i in range(8):
                    ahead(l, "mo", i)
                    residual(l, "mo", i)
                for k in range(8):
                    scaled_lo(l, 32, "g_ffn", k)
                e.wait_ge(stored["mem"], 32 * (l + 1))

                def hid_lo(i):
                    e.wait_ge(s["hid_hi"], at(l, "hid_hi", i + 1))
                    g, k = i // 8 % 2, i % 8
                    tt(hidL[:, g, k, :], hid[:, g, k, :], plain(hidH[:, g, k, :]), ALU.subtract)\
                        .then_inc(s["hid_lo"], 1)

                for g in range(5):
                    if g < 4:
                        for i in range(8 * g, 8 * g + 8):
                            ahead(l, "f1", i)
                            if i == 0:
                                e.wait_ge(s["rms_rstd"], 3 * l + 3)
                            if i >= 16 and i % 8 == 0:
                                wait_tile(e, l, "f2", i - 9)
                            ps, m = take_tile(l, "f1", i), hid[:, g % 2, i % 8, :]
                            tt(m, ps, rs, ALU.mult).then_inc(evac["dve"], 1)
                            wait_evac(e, l, "f1", i)
                            stt(m, m, 0.0, m, ALU.max, ALU.mult).then_inc(s["hid_sq"], 1)
                            if i:
                                hid_lo(i - 1)
                        if g == 3:
                            hid_lo(31)
                    if g:
                        for i in range(8 * g - 8, 8 * g):
                            ahead(l, "f2", i)
                            residual(l, "f2", i)
                            if g == 4 and i % 8 and l + 1 < DEPTH:
                                scaled_lo(l + 1, 0, "g_mix", i % 8 - 1)
                if l + 1 < DEPTH:
                    scaled_lo(l + 1, 0, "g_mix", 7)
            e.wait_ge(s["rms_rstd"], 3 * DEPTH + 1)
            for k in range(8):
                stt(hT[:, k, :], xT[:, k, :], C("g_final", k, k + 1), rs, ALU.mult, ALU.mult).then_inc(y_ready, 1)


_VECTORS = {"g_mix": "norm_mix", "g_mem": "norm_mem", "g_memkv": "norm_mem_kv", "g_ffn": "norm_ffn",
            "conv_w": "rg_conv_w", "conv_b": "rg_conv_b", "rg_ba": "rg_ba", "rg_bx": "rg_bx", "w0": "rw_w0",
            "a0": "rw_a0", "lam": "rg_lambda", "mu": "rw_mu", "k_k": "rw_k_k", "k_a": "rw_k_a", "r_k": "rw_r_k",
            "gn_w": "rw_gn_w", "gn_b": "rw_gn_b", "q_norm": "mla_q_norm", "kv_norm": "mla_kv_norm",
            "h0": "state_rg_h", "shift": "state_rw_shift"}


def _constants(norm_final):
    f = np.float32
    c = np.zeros((128, NCST), f)

    def put(name, a, rows=slice(0, 128)):
        c[rows, CST[name]:CST[name] + a.shape[1]] = a

    i = np.arange(128)
    row, col = i[:, None], i[None, :]
    same = row // CH == col // CH
    put("ident", np.eye(128, dtype=f))
    put("ones", np.ones((128, 128), f))
    put("bones", same.astype(f))
    put("mask2", np.concatenate([same & (row < col), same & (row <= col)], 1).astype(f))
    put("maskL", (same & (col < row)).astype(f))
    levels = []
    for b in range(6):
        n = 1 << b
        levels.append((row // (2 * n) == col // (2 * n)) & (row // n % 2 == 0) & (col // n % 2 == 1))
    put("lev", np.concatenate(levels, 1).astype(f))
    put("lev1t", levels[0].T.astype(f))
    half = ROPE // 2
    inv = f(10000.0) ** (-np.arange(half, dtype=f) / f(half))
    pos = np.concatenate([np.arange(SEQ), PAST + np.arange(DEC)]).astype(f)
    ang = inv[:, None] * pos[None, :]
    put("cos", np.concatenate([np.cos(ang)] * 2).astype(f), slice(64, 96))
    put("sin", np.concatenate([-np.sin(ang), np.sin(ang)]).astype(f), slice(96, 128))
    put("reset", np.broadcast_to((i % CH != 0).astype(f), (128, 128)))
    put("maskq", (i < CH).astype(f)[None, :], slice(0, 1))
    put("maskk", np.where(i >= CH, f(NEG), f(0))[None, :], slice(0, 1))
    put("g_final", np.asarray(norm_final).reshape(8, 128).T)
    return c


def kernel(**inputs):
    import concourse.bacc as bacc
    from concourse.bass_utils import run_bass_kernel_spmd

    a = {k: np.asarray(v) for k, v in inputs.items()}
    f = np.float32
    L = DEPTH

    def rows(m):
        return np.moveaxis(m.reshape((-1, 128) + m.shape[1:]), 0, 1)

    vec = np.zeros((128, L, NV), f)
    for name, src in _VECTORS.items():
        v = a[src].reshape(L, -1, 128)
        vec[:, :, VEC[name]:VEC[name] + v.shape[1]] = v.transpose(2, 0, 1)
    conv = a["state_rg_conv"].reshape(L, 3, 2, 128).transpose(3, 0, 2, 1).reshape(128, L, 6)
    vec[:, :, VEC["conv_s"]:VEC["conv_s"] + 6] = conv

    lw = np.zeros((L, 128, NLW), f)

    def put(name, at, m, r=slice(0, 128)):
        lw[:, r, LW[name] + at:LW[name] + at + m.shape[-1]] = m

    for name, src in (("wa", "rg_wa"), ("wx", "rg_wx")):
        for b in range(4):
            put(name, 64 * b, a[src][:, b], slice(64 * (b % 2), 64 * (b % 2) + 64))
    put("low", 0, a["rw_w2"], slice(0, 32))
    put("low", 0, a["rw_a2"], slice(32, 64))
    put("low", 0, a["rw_g2"], slice(64, 128))
    half = ROPE // 2
    uq = a["mla_w_uq"].reshape(L, 2, 128, HEADS, QKD).transpose(0, 2, 1, 3, 4)
    uq = np.concatenate([uq, uq[..., NOPE + half:], uq[..., NOPE:NOPE + half]], -1)
    put("uq", 0, uq.reshape(L, 128, -1))
    put("uk", 0, a["mla_w_uk"].reshape(L, 128, -1))
    put("uv", 0, a["mla_w_uv"].reshape(L, 128, -1))
    put("ckv", 0, a["cache_mla_ckv"][:, 0].transpose(0, 2, 1))
    put("kr", 0, a["cache_mla_krope"][:, 0].transpose(0, 2, 1), slice(64, 96))
    st = a["state_rw_wkv"][:, 0].transpose(0, 1, 3, 2)
    for h in range(4):
        put("S0", 128 * (h // 2) + 64 * (h % 2), st[:, h], slice(64 * (h % 2), 64 * (h % 2) + 64))

    wall = np.zeros((L, NT, 128, 8, 128), f)
    w_in = a["w_in"]
    rw0, mla0 = 512, 512 + 896
    order = [(rw0 + 128 * i, 128) for i in range(7)] + [(mla0, 128), (mla0 + 128, 128), (mla0 + 256, 128),
             (None, 2 * ROPE), (0, 128), (128, 128), (256, 128), (384, 128)]
    rotary = np.concatenate([w_in[:, :, mla0 + 384:mla0 + 416], w_in[:, :, mla0 + 384 + half:mla0 + 416], w_in[:, :, mla0 + 384:mla0 + 384 + half]], 2)
    mats = {"out": a["w_out"], "mk": a["mem_w_k"].reshape(L, D, D), "mv": a["mem_w_v"].reshape(L, D, D),
            "mq": a["mem_w_q"].reshape(L, D, D), "mo": a["mem_w_o"].reshape(L, D, D), "f1": a["ffn_w1"],
            "f2": a["ffn_w2"]}
    for t, (stg, i) in enumerate(STREAM):
        w, first, k = 128, 0, 0
        if stg == "in":
            at, w = order[i]
            m = rotary if at is None else w_in[:, :, at:at + w]
            first = NOPE if at is None else 0
        else:
            i, k = (i % 8, i // 8) if stg == "f2" else (i, 0)
            m = mats[stg][:, D * k:D * k + D, 128 * i:128 * i + 128]
        if stg == "mv":
            m = mats[stg][:, 512 * (i % 2):512 * (i % 2) + 512, 256 * (i // 2):256 * (i // 2) + 256]
            wall[:, t] = m.reshape(L, 4, 128, 256).transpose(0, 2, 1, 3).reshape(L, 128, 8, 128)
            continue
        wall[:, t, :, :, first:first + w] = m.reshape(L, 8, 128, w).transpose(0, 2, 1, 3)
    wall = wall.reshape(L, NT, 128, 1024)

    x = np.concatenate([a["x_prompt"][0], a["x_sample"][0]], 0)
    arrays = {
        "wall": wall, "lw_in": lw, "vec_in": vec, "cst_in": _constants(a["norm_final"]),
        "x_in": rows(np.ascontiguousarray(x.T)), "mem_in": rows(np.ascontiguousarray(a["mem_prompt"][0].T)),
        "mks_in": a["cache_mem_k"][:, 0].reshape(L, MEM, 8, 128).transpose(0, 3, 2, 1),
        "mvs_in": a["cache_mem_v"][:, 0].reshape(L, 2, 128, D).transpose(0, 2, 1, 3),
    }
    arrays = {k: np.ascontiguousarray(v) for k, v in arrays.items()}
    nc = bacc.Bacc("TRN2", target_bir_lowering=False, num_devices=1)
    F32 = mybir.dt.float32
    ins = [nc.dram_tensor(k, v.shape, F32, kind="ExternalInput").ap() for k, v in arrays.items()]
    outs = {k: nc.dram_tensor(k, shape, F32, kind="ExternalOutput").ap() for k, shape in OUTS}
    build(nc, *ins, outs)
    r = run_bass_kernel_spmd(nc, [arrays], core_ids=[0]).results[0]
    o = {k: np.asarray(r[k]).reshape(shape) for k, shape in OUTS}

    y = o["y_out"].transpose(2, 1, 0).reshape(T, D)
    last = o["last_out"]
    shift = last[:, :, 0:14].reshape(L, 128, RWT, 2).transpose(3, 0, 2, 1).reshape(2, L, 1, RWT * 128)
    conv = last[:, :, 14:26].reshape(L, 128, 2, 2, 3).transpose(3, 0, 4, 2, 1).reshape(2, L, 1, 3, 256)
    h = last[:, :, 26:30].reshape(L, 128, 2, 2).transpose(3, 0, 2, 1).reshape(2, L, 1, 256)
    wkv = np.zeros((2, L, 1, 4, 64, 64), f)
    for i in range(4):
        r_ = slice(64 * (i % 2), 64 * (i % 2) + 64)
        wkv[:, :, 0, i] = o["wkv_out"][:, r_, :, i // 2, r_].transpose(2, 0, 3, 1)
    ckv = o["ckv_out"].transpose(0, 2, 1)[:, None]
    kr = o["kr_out"].transpose(0, 2, 1)[:, None]
    mk = o["memk_out"].transpose(0, 3, 2, 1).reshape(L, 1, MEM, 4, 256)
    mv = o["memv_out"].transpose(0, 2, 1, 3).reshape(L, 1, MEM, 4, 256)
    got = (y[None, :SEQ], y[None, SEQ:], conv[0], h[0], shift[0], wkv[0], ckv[:, :, :SEQ], kr[:, :, :SEQ], mk, mv,
           conv[1], h[1], shift[1], wkv[1], ckv[:, :, SEQ:], kr[:, :, SEQ:])
    return tuple(np.ascontiguousarray(g) for g in got)
```
